# Optimizing a Trainium2 kernel written in Bass

```python
import math
import jax
import jax.numpy as jnp
from jax import lax
import numpy as np
import jax, jax.numpy as jnp

D_MODEL = 1024
BATCH = 1
SEQ = 512
DEPTH = 2

N_MIXERS = 2
HEAD_DIM = 64
N_HEADS = D_MODEL // HEAD_DIM
ATTN_WIDTH = N_HEADS * HEAD_DIM
ROPE_THETA = 10000.0
NORM_EPS = 1e-6

NSA_KV_HEADS = 2
NSA_GROUP = N_HEADS // NSA_KV_HEADS
NSA_KV_WIDTH = NSA_KV_HEADS * HEAD_DIM
NSA_BRANCHES = 3
CMP_LEN = 32
CMP_STRIDE = 16
CMP_HIDDEN = 256
SLC_LEN = 64
SLC_TOP = 16
WIN_LEN = 512
NSA_IN = ATTN_WIDTH + 6 * NSA_KV_WIDTH + ATTN_WIDTH + NSA_BRANCHES * N_HEADS
SLC_Q_BLOCK = 32
WIN_Q_BLOCK = 128

DIL_PATTERNS = ((128, 1), (512, 4), (2048, 16))
DIL_GROUP_HEADS = (N_HEADS - 2 * (N_HEADS // 3), N_HEADS // 3, N_HEADS // 3)
DIL_IN = 4 * ATTN_WIDTH
DIL_Q_BLOCK = 32


def rms_norm(x, g):
    xf = x.astype(jnp.float32)
    y = xf * lax.rsqrt(jnp.mean(xf * xf, axis=-1, keepdims=True) + NORM_EPS)
    return (y * g.astype(jnp.float32)).astype(x.dtype)

def rope(x):
    T = x.shape[1]
    half = x.shape[-1] // 2
    inv = ROPE_THETA ** (-jnp.arange(half, dtype=jnp.float32) / half)
    ang = jnp.arange(T, dtype=jnp.float32)[:, None] * inv[None, :]
    cos = jnp.cos(ang)[None, :, None, :]
    sin = jnp.sin(ang)[None, :, None, :]
    xf = x.astype(jnp.float32)
    x1, x2 = xf[..., :half], xf[..., half:]
    return jnp.concatenate([x1 * cos - x2 * sin, x2 * cos + x1 * sin], axis=-1).astype(x.dtype)

def masked_softmax(s, mask):
    s = jnp.where(mask, s.astype(jnp.float32), -jnp.inf)
    m = jnp.max(s, axis=-1, keepdims=True)
    m = jnp.where(jnp.isfinite(m), m, 0.0)
    e = jnp.exp(s - m)
    den = jnp.sum(e, axis=-1, keepdims=True)
    return e / jnp.where(den > 0, den, 1.0)

def adaln_norm(x, c, g, w_ada, b_ada):
    mod = jax.nn.silu(c) @ w_ada + b_ada
    shift, scale, gate = jnp.split(mod, 3, axis=-1)
    h = rms_norm(x, g) * (1.0 + scale[:, None, :]) + shift[:, None, :]
    return h, gate[:, None, :]

def nsa_mixer(h, w_in, pe_k, pe_v, ck_w1, ck_w2, cv_w1, cv_w2, w_out):
    B, T, _ = h.shape
    G, HG, DH = NSA_KV_HEADS, NSA_GROUP, HEAD_DIM
    scale = DH ** -0.5
    u = h @ w_in
    cuts = np.cumsum([ATTN_WIDTH] + [NSA_KV_WIDTH] * 6 + [ATTN_WIDTH]).tolist()
    q, k_c, v_c, k_s, v_s, k_w, v_w, z, g_logit = jnp.split(u, cuts, axis=-1)
    k_c, v_c, k_s, v_s, k_w, v_w = [a.reshape(B, T, G, DH) for a in (k_c, v_c, k_s, v_s, k_w, v_w)]
    gates = jax.nn.sigmoid(g_logit.astype(jnp.float32)).reshape(B, T, G, HG, NSA_BRANCHES).astype(h.dtype)
    t = jnp.arange(T)

    q_plain = q.reshape(B, T, G, HG, DH)
    n_cmp = (T - CMP_LEN) // CMP_STRIDE + 1
    cmp_idx = CMP_STRIDE * np.arange(n_cmp)[:, None] + np.arange(CMP_LEN)[None, :]

    def compress(a, pe, w1, w2):
        blk = a[:, cmp_idx] + pe[:, None, :]
        blk = jnp.moveaxis(blk, 3, 2).reshape(B, n_cmp, G, CMP_LEN * DH)
        return jax.nn.silu(blk @ w1) @ w2

    k_cmp = compress(k_c, pe_k, ck_w1, ck_w2)
    v_cmp = compress(v_c, pe_v, cv_w1, cv_w2)
    cmp_end = CMP_STRIDE * jnp.arange(n_cmp) + CMP_LEN - 1
    cmask = cmp_end[None, :] <= t[:, None]
    s_cmp = jnp.einsum('btghd,bngd->btghn', q_plain, k_cmp) * scale
    p_cmp = masked_softmax(s_cmp, cmask[None, :, None, None, :])
    o_cmp = jnp.einsum('btghn,bngd->btghd', p_cmp.astype(v_cmp.dtype), v_cmp)

    n_slc = T // SLC_LEN
    c_start = CMP_STRIDE * np.arange(n_cmp)
    s_start = SLC_LEN * np.arange(n_slc)
    overlap = ((c_start[:, None] < s_start[None, :] + SLC_LEN)
               & (c_start[:, None] + CMP_LEN > s_start[None, :])).astype(np.float32)
    p_slc = jnp.einsum('btghn,nj->btgj', p_cmp, overlap)
    jblk = jnp.arange(n_slc)[None, :]
    cur = (t // SLC_LEN)[:, None]
    visible = jblk <= cur
    forced = (jblk == 0) | (jblk == cur) | (jblk == cur - 1)
    rank = jnp.where(forced[None, :, None, :], jnp.inf,
                     jnp.where(visible[None, :, None, :], p_slc, -jnp.inf))
    n_top = min(SLC_TOP, n_slc)
    top_val, top_idx = lax.top_k(rank, n_top)
    top_ok = top_val > -jnp.inf

    q_r = rope(q.reshape(B, T, N_HEADS, DH)).reshape(B, T, G, HG, DH)
    k_s = rope(k_s)
    k_w = rope(k_w)

    k_blk = k_s.reshape(B, n_slc, SLC_LEN, G, DH).transpose(0, 3, 1, 2, 4)
    v_blk = v_s.reshape(B, n_slc, SLC_LEN, G, DH).transpose(0, 3, 1, 2, 4)
    C = SLC_Q_BLOCK
    n_qb = T // C
    q_sb = jnp.moveaxis(q_r.reshape(B, n_qb, C, G, HG, DH), 1, 0)
    idx_sb = jnp.moveaxis(top_idx.reshape(B, n_qb, C, G, n_top), 1, 0)
    ok_sb = jnp.moveaxis(top_ok.reshape(B, n_qb, C, G, n_top), 1, 0)
    gather_blocks = jax.vmap(jax.vmap(lambda blk, ix: blk[ix]))

    def slc_block(args):
        s0, qq, ii, ok = args
        ii_g = jnp.swapaxes(ii, 1, 2)
        kg = gather_blocks(k_blk, ii_g)
        vg = gather_blocks(v_blk, ii_g)
        s = jnp.einsum('bcghd,bgcnld->bcghnl', qq, kg) * scale
        tq = s0 + jnp.arange(C)
        kpos = ii[..., None] * SLC_LEN + jnp.arange(SLC_LEN)
        mask = (kpos <= tq[None, :, None, None, None]) & ok[..., None]
        p = masked_softmax(s.reshape(B, C, G, HG, n_top * SLC_LEN),
                           mask.reshape(B, C, G, 1, n_top * SLC_LEN))
        return jnp.einsum('bcghnl,bgcnld->bcghd', p.reshape(s.shape).astype(vg.dtype), vg)

    o_slc = lax.map(slc_block, (jnp.arange(n_qb) * C, q_sb, idx_sb, ok_sb))
    o_slc = jnp.moveaxis(o_slc, 0, 1).reshape(B, T, G, HG, DH)

    span = WIN_LEN + WIN_Q_BLOCK
    n_wb = T // WIN_Q_BLOCK
    k_pad = jnp.pad(k_w, ((0, 0), (WIN_LEN, 0), (0, 0), (0, 0)))
    v_pad = jnp.pad(v_w, ((0, 0), (WIN_LEN, 0), (0, 0), (0, 0)))
    q_wb = jnp.moveaxis(q_r.reshape(B, n_wb, WIN_Q_BLOCK, G, HG, DH), 1, 0)

    def win_block(args):
        s0, qq = args
        kk = lax.dynamic_slice_in_dim(k_pad, s0, span, axis=1)
        vv = lax.dynamic_slice_in_dim(v_pad, s0, span, axis=1)
        s = jnp.einsum('bcghd,bkgd->bcghk', qq, kk) * scale
        tq = s0 + jnp.arange(WIN_Q_BLOCK)
        kpos = s0 - WIN_LEN + jnp.arange(span)
        mask = ((kpos[None, :] <= tq[:, None]) & (kpos[None, :] > tq[:, None] - WIN_LEN)
                & (kpos[None, :] >= 0))
        p = masked_softmax(s, mask[None, :, None, None, :])
        return jnp.einsum('bcghk,bkgd->bcghd', p.astype(vv.dtype), vv)

    o_win = lax.map(win_block, (jnp.arange(n_wb) * WIN_Q_BLOCK, q_wb))
    o_win = jnp.moveaxis(o_win, 0, 1).reshape(B, T, G, HG, DH)

    o = gates[..., 0:1] * o_cmp + gates[..., 1:2] * o_slc + gates[..., 2:3] * o_win
    o = o.reshape(B, T, ATTN_WIDTH)
    return (o * jax.nn.silu(z)) @ w_out

def dilated_mixer(h, w_in, w_out):
    B, T, _ = h.shape
    DH = HEAD_DIM
    scale = DH ** -0.5
    n_grp = len(DIL_PATTERNS)
    q, k, v, z = jnp.split(h @ w_in, 4, axis=-1)
    q = rope(q.reshape(B, T, N_HEADS, DH))
    k = rope(k.reshape(B, T, N_HEADS, DH))
    v = v.reshape(B, T, N_HEADS, DH)
    offs = np.cumsum((0,) + DIL_GROUP_HEADS).tolist()
    k_grp = [k[:, :, offs[i]:offs[i + 1]] for i in range(n_grp)]
    v_grp = [v[:, :, offs[i]:offs[i + 1]] for i in range(n_grp)]
    C = DIL_Q_BLOCK
    n_qb = T // C
    q_blocks = jnp.moveaxis(q.reshape(B, n_qb, C, N_HEADS, DH), 1, 0)

    def block(args):
        s0, qb = args
        tq = s0 + jnp.arange(C)
        outs, lses = [], []
        for gi, (win, dil) in enumerate(DIL_PATTERNS):
            n_k = win // dil + 1
            kpos = tq[:, None] - dil * jnp.arange(n_k)[None, :]
            ok = kpos >= 0
            kidx = jnp.maximum(kpos, 0)
            kg = k_grp[gi][:, kidx]
            vg = v_grp[gi][:, kidx]
            qg = qb[:, :, offs[gi]:offs[gi + 1]]
            s = jnp.einsum('bchd,bckhd->bchk', qg, kg).astype(jnp.float32) * scale
            s = jnp.where(ok[None, :, None, :], s, -jnp.inf)
            m = jnp.max(s, axis=-1, keepdims=True)
            e = jnp.exp(s - m)
            den = jnp.sum(e, axis=-1, keepdims=True)
            outs.append(jnp.einsum('bchk,bckhd->bchd', (e / den).astype(vg.dtype), vg))
            lse = (m + jnp.log(den))[..., 0]
            lses.append(jax.nn.logsumexp(lse, axis=-1) - math.log(DIL_GROUP_HEADS[gi]))
        alpha = jax.nn.softmax(jnp.stack(lses, axis=-1), axis=-1) * n_grp
        return jnp.concatenate(
            [outs[i] * alpha[:, :, i, None, None].astype(outs[i].dtype) for i in range(n_grp)], axis=2)

    o = lax.map(block, (jnp.arange(n_qb) * C, q_blocks))
    o = jnp.moveaxis(o, 0, 1).reshape(B, T, ATTN_WIDTH)
    return (o * jax.nn.silu(z)) @ w_out

def first_inputs(seed: int = 0) -> dict:
    key = jax.random.key(seed)
    ks = jax.random.split(key, 16)
    n_a = len(range(0, DEPTH, N_MIXERS))
    n_b = len(range(1, DEPTH, N_MIXERS))
    D = D_MODEL

    def nrm(k, shape, s):
        return jax.random.normal(k, shape, jnp.float32) * s

    return {
        "x": nrm(ks[0], (BATCH, SEQ, D), 1.0),
        "c": nrm(ks[1], (BATCH, D), 1.0),
        "norm_g": 1.0 + nrm(ks[2], (DEPTH, D), 0.05),
        "ada_w": nrm(ks[3], (DEPTH, D, 3 * D), 0.5 * D ** -0.5),
        "ada_b": nrm(ks[4], (DEPTH, 3 * D), 0.02),
        "nsa_w_in": nrm(ks[5], (n_a, D, NSA_IN), D ** -0.5),
        "nsa_pe_k": nrm(ks[6], (n_a, CMP_LEN, HEAD_DIM), 0.1),
        "nsa_pe_v": nrm(ks[7], (n_a, CMP_LEN, HEAD_DIM), 0.1),
        "nsa_ck_w1": nrm(ks[8], (n_a, CMP_LEN * HEAD_DIM, CMP_HIDDEN), (CMP_LEN * HEAD_DIM) ** -0.5),
        "nsa_ck_w2": nrm(ks[9], (n_a, CMP_HIDDEN, HEAD_DIM), CMP_HIDDEN ** -0.5),
        "nsa_cv_w1": nrm(ks[10], (n_a, CMP_LEN * HEAD_DIM, CMP_HIDDEN), (CMP_LEN * HEAD_DIM) ** -0.5),
        "nsa_cv_w2": nrm(ks[11], (n_a, CMP_HIDDEN, HEAD_DIM), CMP_HIDDEN ** -0.5),
        "nsa_w_out": nrm(ks[12], (n_a, ATTN_WIDTH, D), ATTN_WIDTH ** -0.5),
        "dil_w_in": nrm(ks[13], (n_b, D, DIL_IN), D ** -0.5),
        "dil_w_out": nrm(ks[14], (n_b, ATTN_WIDTH, D), ATTN_WIDTH ** -0.5),
        "final_g": 1.0 + nrm(ks[15], (D,), 0.05),
    }

def first_block(x, c, norm_g, ada_w, ada_b, nsa_w_in, nsa_pe_k, nsa_pe_v, nsa_ck_w1, nsa_ck_w2,
              nsa_cv_w1, nsa_cv_w2, nsa_w_out, dil_w_in, dil_w_out, final_g):
    for i in range(DEPTH):
        h, gate = adaln_norm(x, c, norm_g[i], ada_w[i], ada_b[i])
        j = i // N_MIXERS
        if i % N_MIXERS == 0:
            y = nsa_mixer(h, nsa_w_in[j], nsa_pe_k[j], nsa_pe_v[j], nsa_ck_w1[j], nsa_ck_w2[j],
                          nsa_cv_w1[j], nsa_cv_w2[j], nsa_w_out[j])
        else:
            y = dilated_mixer(h, dil_w_in[j], dil_w_out[j])
        x = x + gate * y
    return rms_norm(x, final_g)


DEPTH_2 = 1

N_Q_HEADS = 8
N_KV_HEADS = 2
Q_PER_KV = N_Q_HEADS // N_KV_HEADS
ATTN_WIDTH_2 = N_Q_HEADS * HEAD_DIM
KV_WIDTH = N_KV_HEADS * HEAD_DIM
WINDOW = 128
ATTN_BLOCK = WINDOW
CONV_WIDTH = D_MODEL - ATTN_WIDTH_2
CONV_K = 3
IN_PROJ_WIDTH = ATTN_WIDTH_2 + 2 * KV_WIDTH + 3 * CONV_WIDTH
SPLITS = (ATTN_WIDTH_2, ATTN_WIDTH_2 + KV_WIDTH, ATTN_WIDTH_2 + 2 * KV_WIDTH,
          ATTN_WIDTH_2 + 2 * KV_WIDTH + CONV_WIDTH, ATTN_WIDTH_2 + 2 * KV_WIDTH + 2 * CONV_WIDTH)
PEER_HEADS = 8
PEER_KEYS = 128
PEER_EXPERTS = PEER_KEYS * PEER_KEYS
PEER_TOPK = 16
PEER_QDIM = 256
PEER_HALF = PEER_QDIM // 2
PEER_CHUNK = 128
N_MOD = 6
EPS = 1e-6
NEG = -1e30


def rmsnorm(x, g):
    x32 = x.astype(jnp.float32)
    y = x32 * lax.rsqrt(jnp.mean(x32 * x32, axis=-1, keepdims=True) + EPS)
    return (y * g.astype(jnp.float32)).astype(x.dtype)

def modulate(h, shift, scale):
    return h * (1.0 + scale[:, None, :]) + shift[:, None, :]

def rope_2(t, cos, sin):
    t1, t2 = jnp.split(t.astype(jnp.float32), 2, axis=-1)
    out = jnp.concatenate([t1 * cos - t2 * sin, t2 * cos + t1 * sin], axis=-1)
    return out.astype(t.dtype)

def sliding_window_attention(q, k, v, sinks):
    B, S = q.shape[0], q.shape[1]
    nb = S // ATTN_BLOCK
    qb = q.reshape(B, nb, ATTN_BLOCK, N_KV_HEADS, Q_PER_KV, HEAD_DIM)

    def band(t):
        tb = t.reshape(B, nb, ATTN_BLOCK, N_KV_HEADS, HEAD_DIM)
        prev = jnp.pad(tb, ((0, 0), (1, 0), (0, 0), (0, 0), (0, 0)))[:, :-1]
        return jnp.concatenate([prev, tb], axis=2)

    kb, vb = band(k), band(v)
    s = jnp.einsum('bnqhgd,bnkhd->bnhgqk', qb, kb).astype(jnp.float32) * (HEAD_DIM ** -0.5)
    qi = jnp.arange(ATTN_BLOCK)[:, None]
    kj = jnp.arange(2 * ATTN_BLOCK)[None, :]
    dist = qi + ATTN_BLOCK - kj
    blk = jnp.arange(nb)[:, None, None]
    valid = (dist >= 0) & (dist < WINDOW) & (blk * ATTN_BLOCK - ATTN_BLOCK + kj >= 0)
    s = jnp.where(valid[None, :, None, None], s, NEG)
    sink = sinks.astype(jnp.float32).reshape(1, 1, N_KV_HEADS, Q_PER_KV, 1, 1)
    m = jnp.maximum(jnp.max(s, axis=-1, keepdims=True), sink)
    e = jnp.exp(s - m)
    p = e / (jnp.sum(e, axis=-1, keepdims=True) + jnp.exp(sink - m))
    o = jnp.einsum('bnhgqk,bnkhd->bnqhgd', p.astype(v.dtype), vb)
    return o.reshape(B, S, ATTN_WIDTH_2)

def short_conv(h, w):
    S = h.shape[1]
    hp = jnp.pad(h, ((0, 0), (CONV_K - 1, 0), (0, 0)))
    y = w[0] * hp[:, 0:S]
    for k in range(1, CONV_K):
        y = y + w[k] * hp[:, k:k + S]
    return y

def peer(h, wq, subkeys, u_tab, v_tab):
    B, S, D = h.shape
    T = B * S
    xt = h.reshape(T, D)
    q = (xt @ wq).reshape(T, PEER_HEADS, 2, PEER_HALF)
    sc = jnp.einsum('thpd,hpkd->thpk', q, subkeys).astype(jnp.float32)
    vals, ids = lax.top_k(sc, PEER_TOPK)
    cand = (vals[:, :, 0, :, None] + vals[:, :, 1, None, :]).reshape(T, PEER_HEADS, PEER_TOPK * PEER_TOPK)
    cid = (ids[:, :, 0, :, None] * PEER_KEYS + ids[:, :, 1, None, :]).reshape(T, PEER_HEADS, PEER_TOPK * PEER_TOPK)
    top, pos = lax.top_k(cand, PEER_TOPK)
    idx = jnp.take_along_axis(cid, pos, axis=-1)
    g = jax.nn.softmax(top, axis=-1).astype(h.dtype)
    nc = T // PEER_CHUNK

    def expert_chunk(args):
        xc, ic, gc = args
        u = jnp.take(u_tab, ic, axis=0)
        a = jnp.einsum('chkd,cd->chk', u, xc)
        wgt = gc * jax.nn.gelu(a)
        vv = jnp.take(v_tab, ic, axis=0)
        return jnp.einsum('chk,chkd->cd', wgt, vv)

    out = lax.map(expert_chunk, (xt.reshape(nc, PEER_CHUNK, D),
                                 idx.reshape(nc, PEER_CHUNK, PEER_HEADS, PEER_TOPK),
                                 g.reshape(nc, PEER_CHUNK, PEER_HEADS, PEER_TOPK)))
    return out.reshape(B, S, D)

def second_inputs(seed: int = 0) -> dict:
    key = jax.random.key(seed)
    ks = jax.random.split(key, 20)
    f32 = jnp.float32
    D = D_MODEL

    def nrm(k, shape, scale):
        return jax.random.normal(k, shape, f32) * scale

    return {
        "x": nrm(ks[0], (BATCH, SEQ, D), 1.0),
        "c": nrm(ks[1], (BATCH, D), 1.0),
        "positions": jnp.broadcast_to(jnp.arange(SEQ, dtype=jnp.int32)[None, :], (BATCH, SEQ)),
        "ada_w": nrm(ks[2], (DEPTH_2, D, N_MOD * D), 0.5 * D ** -0.5),
        "ada_b": nrm(ks[3], (DEPTH_2, N_MOD * D), 0.02),
        "norm1_g": 1.0 + nrm(ks[4], (DEPTH_2, D), 0.02),
        "w_in": nrm(ks[5], (DEPTH_2, D, IN_PROJ_WIDTH), D ** -0.5),
        "q_norm_g": 1.0 + nrm(ks[6], (DEPTH_2, HEAD_DIM), 0.02),
        "k_norm_g": 1.0 + nrm(ks[7], (DEPTH_2, HEAD_DIM), 0.02),
        "sinks": nrm(ks[8], (DEPTH_2, N_Q_HEADS), 0.5),
        "conv_w": nrm(ks[9], (DEPTH_2, CONV_K, CONV_WIDTH), CONV_K ** -0.5),
        "attn_out_g": 1.0 + nrm(ks[10], (DEPTH_2, ATTN_WIDTH_2), 0.02),
        "conv_out_g": 1.0 + nrm(ks[11], (DEPTH_2, CONV_WIDTH), 0.02),
        "w_out": nrm(ks[12], (DEPTH_2, D, D), D ** -0.5),
        "norm2_g": 1.0 + nrm(ks[13], (DEPTH_2, D), 0.02),
        "peer_wq": nrm(ks[14], (DEPTH_2, D, PEER_HEADS * PEER_QDIM), D ** -0.5),
        "peer_subkeys": nrm(ks[15], (DEPTH_2, PEER_HEADS, 2, PEER_KEYS, PEER_HALF), PEER_HALF ** -0.5),
        "peer_u": nrm(ks[16], (DEPTH_2, PEER_EXPERTS, D), D ** -0.5),
        "peer_v": nrm(ks[17], (DEPTH_2, PEER_EXPERTS, D), (PEER_HEADS * PEER_TOPK) ** -0.5),
    }

def second_block(x, c, positions, ada_w, ada_b, norm1_g, w_in, q_norm_g, k_norm_g, sinks, conv_w,
              attn_out_g, conv_out_g, w_out, norm2_g, peer_wq, peer_subkeys, peer_u, peer_v):
    B, S, _ = x.shape
    inv_freq = ROPE_THETA ** (-jnp.arange(0, HEAD_DIM, 2, dtype=jnp.float32) / HEAD_DIM)
    ang = positions.astype(jnp.float32)[..., None] * inv_freq
    cos = jnp.cos(ang)[:, :, None, :]
    sin = jnp.sin(ang)[:, :, None, :]
    c_act = jax.nn.silu(c)

    for l in range(DEPTH_2):
        mod = c_act @ ada_w[l] + ada_b[l]
        shift1, scale1, gate1, shift2, scale2, gate2 = jnp.split(mod, N_MOD, axis=-1)

        h = modulate(rmsnorm(x, norm1_g[l]), shift1, scale1)
        proj = h @ w_in[l]
        q, k, v, cb, cc, cu = jnp.split(proj, SPLITS, axis=-1)

        q = rope_2(rmsnorm(q.reshape(B, S, N_Q_HEADS, HEAD_DIM), q_norm_g[l]), cos, sin)
        k = rope_2(rmsnorm(k.reshape(B, S, N_KV_HEADS, HEAD_DIM), k_norm_g[l]), cos, sin)
        v = v.reshape(B, S, N_KV_HEADS, HEAD_DIM)
        attn = sliding_window_attention(q, k, v, sinks[l])

        conv = cb * short_conv(cc * cu, conv_w[l])

        merged = jnp.concatenate([rmsnorm(attn, attn_out_g[l]), rmsnorm(conv, conv_out_g[l])], axis=-1)
        x = x + gate1[:, None, :] * (merged @ w_out[l])

        h2 = modulate(rmsnorm(x, norm2_g[l]), shift2, scale2)
        x = x + gate2[:, None, :] * peer(h2, peer_wq[l], peer_subkeys[l], peer_u[l], peer_v[l])
    return x


def setup_inputs(seed=0):
    out = dict(first_inputs(seed))
    for name, value in second_inputs(seed + 1).items():
        if name != "x":
            out[name + "_2"] = value
    return out


def reference(
    x, c, norm_g, ada_w, ada_b, nsa_w_in, nsa_pe_k, nsa_pe_v, nsa_ck_w1, nsa_ck_w2, nsa_cv_w1,
    nsa_cv_w2, nsa_w_out, dil_w_in, dil_w_out, final_g, c_2, positions_2, ada_w_2, ada_b_2,
    norm1_g_2, w_in_2, q_norm_g_2, k_norm_g_2, sinks_2, conv_w_2, attn_out_g_2, conv_out_g_2,
    w_out_2, norm2_g_2, peer_wq_2, peer_subkeys_2, peer_u_2, peer_v_2,
):
    x = first_block(
        x, c, norm_g, ada_w, ada_b, nsa_w_in, nsa_pe_k, nsa_pe_v, nsa_ck_w1, nsa_ck_w2,
        nsa_cv_w1, nsa_cv_w2, nsa_w_out, dil_w_in, dil_w_out, final_g,
    )
    return second_block(
        x, c_2, positions_2, ada_w_2, ada_b_2, norm1_g_2, w_in_2, q_norm_g_2, k_norm_g_2,
        sinks_2, conv_w_2, attn_out_g_2, conv_out_g_2, w_out_2, norm2_g_2, peer_wq_2,
        peer_subkeys_2, peer_u_2, peer_v_2,
    )


_drawn_inputs = setup_inputs


def setup_inputs(seed=0):
    import zlib

    import numpy as np

    out = dict(_drawn_inputs(seed))
    spreads = {}
    factors = {'norm_g': 5.637,
     'ada_b': 4.553,
     'nsa_pe_k': 8.0,
     'nsa_pe_v': 8.0,
     'nsa_ck_w1': 4.466,
     'nsa_ck_w2': 4.407,
     'norm1_g_2': 7.341,
     'q_norm_g_2': 8.0,
     'k_norm_g_2': 8.0,
     'sinks_2': 8.0,
     'attn_out_g_2': 8.0,
     'conv_out_g_2': 8.0,
     'norm2_g_2': 8.0,
     'peer_wq_2': 3.939,
     'peer_subkeys_2': 3.993,
     'peer_u_2': 4.387,
     'peer_v_2': 3.937}
    for name, (base, spread) in spreads.items():
        noise = np.random.default_rng([zlib.crc32(name.encode()), seed]).standard_normal(out[name].shape)
        drawn = base * np.exp(spread * noise) if base else spread * noise
        out[name] = jnp.asarray(drawn.astype(out[name].dtype))
    for name, factor in factors.items():
        out[name] = (out[name] * factor).astype(out[name].dtype)
    return out
```

```python
import math
from contextlib import ExitStack

import numpy as np

import concourse.bass as bass
from concourse import mybir

F32 = mybir.dt.float32
F32R = mybir.dt.float32r
U32 = mybir.dt.uint32
I32 = mybir.dt.int32
ALU = mybir.AluOpType
ACT = mybir.ActivationFunctionType
AX = mybir.AxisListType

P = 128
T = 512
D = 1024
TT = T // P
KD = D // P
DH = 64
HALF = DH // 2
NH = 16
NQ2, NKV2 = 8, 2
SCALE = DH ** -0.5
EPS = 1e-6
BIG = 1e30
N_CMP, CMP_PAD = 31, 32
CMP_H = 256
SPAN = 16
PH, PK, PTOP = 8, 128, 16
DIL_GROUPS = ((0, 6), (6, 11), (11, 16))

R = 4
RS = 3
PIECE = KD * P
GI = 4
NG = PK // GI
CHUNK = 64

CONST = dict(ident=P, ones=P, rot=P, bones=P, cos=T, sin=T, causal=T, causal16=P,
             band129=2 * P, band128=2 * P, mcmp=TT * CMP_PAD, iota=P, iota16=PTOP,
             valid=TT, invf=1)
SMALL = dict(c=KD, c2=KD, ng0=KD, ng1=KD, fg=KD, n1g=KD, n2g=KD, adab=96, qg=1, kg=1,
             aog=4, cog=4, convw=12, sinks=NQ2, pek=16, pev=16, w2k=2 * DH, w2v=2 * DH)


def offsets(widths):
    at, out = 0, {}
    for name, w in widths.items():
        out[name] = (at, at + w)
        at += w
    return out, at


CONST_AT, CONST_W = offsets(CONST)
SMALL_AT, SMALL_W = offsets(SMALL)

STREAM = [("ada0", 24), ("cmp_in", 2), ("ksw", 2), ("q", 8), ("cmp_w1", 8), ("vsw", 3), ("z", 8),
          ("ada12", 72), ("nsa_out", 8), ("dq", 8), ("dk", 8), ("dv", 8), ("dz", 8), ("dil_out", 8),
          ("q2", 4), ("k2", 1), ("v2", 1), ("cc", 4), ("cu", 4), ("cb", 4), ("out2", 8),
          ("wq", 16), ("subkeys", 2)]
PIECE_AT, N_PIECES = offsets(dict(STREAM))


RAW = ("ada0", "ada12", "cmp_w1", "subkeys")


def build(nc, w_stream, consts_in, small_in, x_in, pos_in, u_in, v_in, out, gates_dram, until=99):
    ctx = ExitStack()
    with ctx:
        def sb(name, shape, dt=F32):
            return ctx.enter_context(nc.sbuf_tensor(name, shape, dt))

        def sem(name):
            return ctx.enter_context(nc.semaphore(name))

        ps = ctx.enter_context(nc.psum_tensor("ps", [P, 8, 512], F32))
        cst = sb("cst", [P, CONST_W])
        sml = sb("sml", [P, SMALL_W])
        xT = sb("xT", [P, KD, T])
        rope2 = sb("rope2", [P, 2, T])
        mod = sb("mod", [P, 96])
        amp = sb("amp", [P, 4, KD])
        csil = sb("csil", [P, 2, KD])
        rstd = sb("rstd", [P, T])
        sdev = sb("sdev", [P, T])
        var = sb("var", [P, T])
        ARENA = 24320
        HR_AT, WR_AT = ARENA, ARENA + 2 * KD * T
        RING_AT = WR_AT + RS * 2 * PIECE
        SLAB = RING_AT + R * PIECE
        sb("slab", [P, SLAB])
        slab_at = nc.sbuf_base - 4 * SLAB

        def place(name, at, shape, dt=F32):
            assert at + math.prod(shape) <= SLAB, (name, at, shape)
            return nc.alloc_sbuf_tensor_at(name, [P] + list(shape), dt, offset=slab_at + 4 * at)

        arena = place("arena", 0, [ARENA])
        h_hi = place("h_hi", HR_AT, [KD, T], F32R)
        h_lo = place("h_lo", HR_AT + KD * T, [KD, T], F32R)
        w_split = place("w_split", WR_AT, [RS, 2, PIECE], F32R)
        ring = place("ring", RING_AT, [R, PIECE])

        def C(name):
            a, b = CONST_AT[name]
            return cst[:, a:b]

        def S(name):
            a, b = SMALL_AT[name]
            return sml[:, a:b]

        def area(at, *shape):
            n = math.prod(shape)
            assert at + n <= ARENA, (at, shape)
            v = arena[:, at:at + n]
            if len(shape) == 2:
                v = v.rearrange("p (a b) -> p a b", b=shape[1])
            elif len(shape) == 3:
                v = v.rearrange("p (a b c) -> p a b c", b=shape[1], c=shape[2])
            return v

        ident = C("ident")

        const_in = sem("const_in")
        x_loaded = sem("x_loaded")
        piece_in = [sem(f"piece_in{i}") for i in range(R)]
        piece_used = sem("piece_used")
        dve_step = sem("dve_step")
        act_step = sem("act_step")
        pool_step = sem("pool_step")
        counts = {"dve": 0, "act": 0, "pool": 0}
        step_sem = {"dve": dve_step, "act": act_step, "pool": pool_step}

        def note(who, ins, n=1):
            ins.then_inc(step_sem[who], 1)
            counts[who] += 1
            return counts[who]

        class Work:
            asked = 0
            used = 0
            hi = 0
            lo = 0

        split_of, n_split = {}, 0
        for name, _ in STREAM:
            for n in range(*PIECE_AT[name]):
                if name not in RAW:
                    split_of[n] = n_split
                    n_split += 1
        split_list = sorted(split_of)
        raw_used = {}
        hi_done, lo_done = sem("hi_done"), sem("lo_done")
        ADA12 = PIECE_AT["ada12"]
        ada_used = sem("ada_used")

        def ask_pieces(sp, upto):
            while Work.asked < min(upto, N_PIECES):
                n = Work.asked
                if n >= R:
                    m = n - R
                    if m in split_of:
                        sp.wait_ge(lo_done, split_of[m] + 1)
                    elif ADA12[0] <= m < ADA12[1]:
                        sp.wait_ge(ada_used, m - ADA12[0] + 1)
                    else:
                        sp.wait_ge(piece_used, m + 1)
                sp.dma_start(ring[:, n % R, :], w_stream[n]).then_inc(piece_in[n % R], 16)
                Work.asked += 1

        def split_hi(act, n):
            i = split_of[n]
            assert i == Work.hi
            Work.hi += 1
            act.wait_ge(piece_in[n % R], 16 * (n // R + 1))
            if i >= RS:
                act.wait_ge(piece_used, split_list[i - RS] + 1)
            act.activation(w_split[:, i % RS, 0, :], ring[:, n % R, :], ACT.Copy).then_inc(hi_done, 1)

        def split_lo(pool, n):
            i = split_of[n]
            assert i == Work.lo
            Work.lo += 1
            pool.wait_ge(hi_done, i + 1)
            pool.tensor_tensor(w_split[:, i % RS, 1, :], ring[:, n % R, :],
                               w_split[:, i % RS, 0, :].bitcast(F32), ALU.subtract).then_inc(lo_done, 1)

        def piece_ready(pe, n):
            assert n == Work.used, (n, Work.used)
            Work.used += 1
            if n in split_of:
                pe.wait_ge(lo_done, split_of[n] + 1)
                return w_split[:, split_of[n] % RS, :, :]
            pe.wait_ge(piece_in[n % R], 16 * (n // R + 1))
            return ring[:, n % R, :]

        HI_LO = ((0, 0), (0, 1), (1, 0))

        def feature_unit(pe, n, bank, src, src_ready=None):
            w = piece_ready(pe, n)
            for k in range(KD):
                if src_ready:
                    src_ready.wait(pe, k + 1)
                for a, b in HI_LO:
                    mm = pe.matmul(ps[:, bank, :], w[:, a, k * P:(k + 1) * P], src[b][:, k, :],
                                   start=(k + a + b == 0), stop=(k == KD - 1 and a == 1))
            mm.then_inc(piece_used, 1)

        def token_unit(pe, n, bank, src, tokens):
            w = piece_ready(pe, n)
            for i in range(TT):
                for k in range(KD):
                    for a, b in HI_LO:
                        mm = pe.matmul(ps[:, bank, i * P:(i + 1) * P], src[b][:, k, tokens(i)],
                                       w[:, a, k * P:(k + 1) * P],
                                       start=(k + a + b == 0), stop=(k == KD - 1 and a == 1))
            mm.then_inc(piece_used, 1)

        def ada_unit(pe, n, col, which, bank=7):
            w = piece_ready(pe, n)
            for k in range(KD):
                mm = pe.matmul(ps[:, bank, col:col + 1], w[:, k * P:(k + 1) * P],
                               csil[:, which, k:k + 1], start=(k == 0), stop=(k == KD - 1))
            mm.then_inc(piece_used, 1)

        h_parts = (h_hi, h_lo)

        def tile_tokens(i):
            return slice(i * P, (i + 1) * P)

        def class_tokens(r):
            return slice(r, T, TT)

        def phase():
            return nc.Block()

        def drain():
            with nc.Block() as block:
                @block.sync
                def _(sp):
                    for i in range(R):
                        n = sum(1 for m in range(Work.asked) if m % R == i)
                        sp.wait_ge(piece_in[i], 16 * n)

        class Since:

            def __init__(self, sem, base):
                self.sem, self.base = sem, base

            def wait(self, eng, n):
                eng.wait_ge(self.sem, self.base + n)

        shared = {}

        def since(name, n):
            s, base = shared.get(name) or (sem(name), 0)
            shared[name] = (s, base + n)
            return Since(s, base)

        def norm_parts(tag, src, dst, sq, units, bank, amps, shifts, parts=None):
            half = units // 2
            sq_d, sq_a = since("norm_sq_dve", half), since("norm_sq_act", half)
            summed, varied, rooted = since("norm_summed", 1), since("norm_varied", 1), since("norm_rooted", 1)
            scaled = since("norm_scaled", units)
            upper, done = since("norm_hi", units if parts else 0), since("norm_done", units if parts else 0)

            def dve_squares(dve):
                for k in range(0, units, 2):
                    dve.tensor_tensor(sq[:, k, :], src[:, k, :], src[:, k, :], ALU.mult).then_inc(sq_d.sem, 1)

            def act_squares(act):
                for k in range(1, units, 2):
                    act.activation(sq[:, k, :], src[:, k, :], ACT.Square).then_inc(sq_a.sem, 1)

            def pe_sum(pe):
                for k in range(units):
                    (sq_a if k % 2 else sq_d).wait(pe, k // 2 + 1)
                    mm = pe.matmul(ps[:, bank, :], C("ones"), sq[:, k, :],
                                   start=(k == 0), stop=(k == units - 1))
                mm.then_inc(summed.sem, 1)

            def act_root(act):
                varied.wait(act, 1)
                act.activation(sdev[:, :], var[:, :], ACT.Sqrt).then_inc(rooted.sem, 1)

            def dve_scale(dve):
                summed.wait(dve, 1)
                dve.tensor_scalar(var[:, :], ps[:, bank, :], 1.0 / (units * P), EPS,
                                  ALU.mult, ALU.add).then_inc(varied.sem, 1)
                rooted.wait(dve, 1)
                inverse_root(dve, var[:, :], sdev[:, :], rstd[:, :])
                for k in range(units):
                    dve.scalar_tensor_tensor(out=dst[:, k, :], in0=src[:, k, :], scalar=amps[:, k:k + 1],
                                             in1=rstd[:, :], op0=ALU.mult, op1=ALU.mult).then_inc(scaled.sem, 1)
                    if parts and k >= 2:
                        lower(dve, k - 2)
                if parts:
                    lower(dve, units - 2)
                    lower(dve, units - 1)

            def lower(dve, k):
                upper.wait(dve, k + 1)
                if shifts is None:
                    ins = dve.tensor_tensor(parts[1][:, k, :], dst[:, k, :], parts[0][:, k, :].bitcast(F32),
                                            ALU.subtract)
                else:
                    ins = dve.scalar_tensor_tensor(out=parts[1][:, k, :], in0=dst[:, k, :],
                                                   scalar=shifts[:, k:k + 1],
                                                   in1=parts[0][:, k, :].bitcast(F32),
                                                   op0=ALU.add, op1=ALU.subtract)
                ins.then_inc(done.sem, 1)

            def act_upper(act):
                for k in range(units):
                    scaled.wait(act, k + 1)
                    if shifts is None:
                        ins = act.activation(parts[0][:, k, :], dst[:, k, :], ACT.Copy)
                    else:
                        ins = act.activation(parts[0][:, k, :], dst[:, k, :], ACT.Identity, bias=shifts[:, k:k + 1])
                    ins.then_inc(upper.sem, 1)

            return dve_squares, act_squares, pe_sum, act_root, dve_scale, act_upper, scaled, done

        def inverse_root(dve, v, root, out_):
            n = note("dve", dve.reciprocal(out_, root))
            dve.wait_ge(dve_step, n)
            n = note("dve", dve.tensor_tensor(v, v, out_, ALU.mult))
            dve.wait_ge(dve_step, n)
            n = note("dve", dve.scalar_tensor_tensor(out=v, in0=v, scalar=-0.5, in1=out_, op0=ALU.mult, op1=ALU.mult))
            dve.wait_ge(dve_step, n)
            n = note("dve", dve.scalar_tensor_tensor(out=out_, in0=v, scalar=1.5, in1=out_, op0=ALU.add, op1=ALU.mult))
            dve.wait_ge(dve_step, n)

        nsq, ntmp = area(0, KD, T), area(KD * T, KD, T)

        n0 = norm_parts("n0", xT, ntmp, nsq, KD, 6, amp[:, 0, :], mod[:, 0:8], h_parts)
        silu_done = sem("silu_done")
        mod0_done = sem("mod0_done")
        wrapped = sem("wrapped")
        pos_loaded = sem("pos_loaded")
        pos_i = area(8192, T).bitcast(I32)
        ang = area(8704, T)
        turns = area(9216, 2, T)
        wrap = area(10240, 2, T)
        TWO_PI = (6.28125, 0.0019350051879882812, 3.019916050561733e-07)
        with phase() as block:
            @block.sync
            def _(sp):
                sp.dma_start(sml[:, :], small_in).then_inc(const_in, 16)
                ask_pieces(sp, 2)
                sp.dma_start(cst[:, :], consts_in).then_inc(const_in, 16)
                for k in range(0, KD, 4):
                    sp.dma_start(xT[:, k:k + 4, :], x_in[:, k:k + 4, :]).then_inc(x_loaded, 16)
                sp.dma_start(pos_i, pos_in.partition_broadcast(P)).then_inc(pos_loaded, 16)
                ask_pieces(sp, PIECE_AT["ada0"][1] + R)

            @block.scalar
            def _(act):
                act.wait_ge(const_in, 32)
                for i, name in enumerate(("c", "c2")):
                    act.activation(csil[:, i, :], S(name), ACT.Silu).then_inc(silu_done, 1)
                act.wait_ge(x_loaded, 32)
                n0[1](act)
                n0[3](act)
                act.wait_ge(wrapped, 2)
                act.activation(rope2[:, 0, :], wrap[:, 0, :], ACT.Sin)
                act.activation(rope2[:, 1, :], wrap[:, 1, :], ACT.Sin)
                act.wait_ge(mod0_done, 2)
                n0[5](act)

            @block.tensor
            def _(pe):
                pe.wait_ge(silu_done, 2)
                at = PIECE_AT["ada0"][0]
                for j in range(16):
                    ada_unit(pe, at + j, j, 0)
                n0[2](pe)
                for j in range(16, 24):
                    ada_unit(pe, at + j, j, 0, 5)

            @block.vector
            def _(dve):
                dve.wait_ge(x_loaded, 32)
                n0[0](dve)
                dve.wait_ge(pos_loaded, 16)
                dve.wait_ge(const_in, 32)
                v = note("dve", dve.tensor_copy(wrap[:, 0, :], pos_i))
                dve.wait_ge(dve_step, v)
                v = note("dve", dve.tensor_scalar(ang, wrap[:, 0, :], C("invf"), None, ALU.mult))
                dve.wait_ge(dve_step, v)
                for i, quarter in enumerate((0.25, 0.0)):
                    v = note("dve", dve.tensor_scalar(turns[:, i, :], ang, 1.0 / (2 * math.pi), quarter,
                                                      ALU.mult, ALU.add))
                    dve.wait_ge(dve_step, v)
                    v = note("dve", dve.tensor_scalar(turns[:, i, :], turns[:, i, :], 12582912.0, None, ALU.add))
                    dve.wait_ge(dve_step, v)
                    v = note("dve", dve.tensor_scalar(turns[:, i, :], turns[:, i, :], -12582912.0, None, ALU.add))
                    dve.wait_ge(dve_step, v)
                    for j, part in enumerate(TWO_PI):
                        v = note("dve", dve.scalar_tensor_tensor(
                            out=wrap[:, i, :], in0=turns[:, i, :], scalar=-part,
                            in1=ang if j == 0 else wrap[:, i, :], op0=ALU.mult, op1=ALU.add))
                        dve.wait_ge(dve_step, v)
                    v = note("dve", dve.tensor_scalar(wrap[:, i, :], wrap[:, i, :],
                                                      math.pi / 2 if i == 0 else 0.0, 3.1415925,
                                                      ALU.add, ALU.min))
                    dve.wait_ge(dve_step, v)
                    dve.tensor_scalar(wrap[:, i, :], wrap[:, i, :], -3.1415925, None,
                                      ALU.max).then_inc(wrapped, 1)
                dve.wait_ge(piece_used, 16)
                dve.tensor_tensor(mod[:, 0:16], ps[:, 7, 0:16], S("adab")[:, 0:16], ALU.add).then_inc(mod0_done, 1)
                dve.wait_ge(mod0_done, 1)
                dve.scalar_tensor_tensor(out=amp[:, 0, :], in0=mod[:, 8:16], scalar=1.0, in1=S("ng0"),
                                         op0=ALU.add, op1=ALU.mult).then_inc(mod0_done, 1)
                dve.wait_ge(mod0_done, 2)
                n0[4](dve)
                dve.wait_ge(piece_used, 24)
                dve.tensor_tensor(mod[:, 16:24], ps[:, 5, 16:24], S("adab")[:, 16:24], ALU.add)

        if until < 2:
            drain()
            return

        def rope_parts(tag, n, raw, t1, t2, dst, cos, sin, bank0, raw_ready):
            rotated, cosed = since("rope_rotated", n), since("rope_cosed", n)
            sined, roped = since("rope_sined", n), since("rope_roped", n)

            def pe_part(pe, r):
                raw_ready(pe, r)
                if r >= 2:
                    sined.wait(pe, r - 1)
                pe.matmul(ps[:, bank0 + r % 2, :], C("rot"), raw(r), start=True, stop=True).then_inc(rotated.sem, 1)

            def pool_part(pool, r):
                raw_ready(pool, r)
                if r >= 2:
                    roped.wait(pool, r - 1)
                pool.tensor_tensor(t1[:, r % 2, :], raw(r), cos, ALU.mult).then_inc(cosed.sem, 1)

            def dve_part(dve, r):
                rotated.wait(dve, r + 1)
                if r >= 2:
                    roped.wait(dve, r - 1)
                dve.tensor_tensor(t2[:, r % 2, :], ps[:, bank0 + r % 2, :], sin, ALU.mult).then_inc(sined.sem, 1)
                cosed.wait(dve, r + 1)
                sined.wait(dve, r + 1)
                dve.tensor_tensor(dst(r), t1[:, r % 2, :], t2[:, r % 2, :], ALU.add).then_inc(roped.sem, 1)

            return pe_part, pool_part, dve_part, roped

        def evacuated(order, sems):
            def wait(eng, i):
                eng.wait_ge(sems[order[i]], sum(o == order[i] for o in order[:i + 1]))
            return wait

        rp = area(0, 10, T)
        qr = area(5120, 10, T)
        zs = area(10240, 8, T)
        ot = area(14336, TT, D)
        vs = area(18432, TT, P)
        vw = area(18944, TT, P)
        gate = area(19456, TT, 48)
        kcm = area(19648, 2, CMP_PAD)
        vbd = area(19712, 4, DH)
        WORK = 20192
        xc = area(WORK, 2, 2, T // 2)
        h1 = area(WORK + 1024, 2, 2, 2 * N_CMP)
        rt1 = area(WORK + 1272, 2, T)
        rt2 = area(WORK + 2296, 2, T)

        order2 = ["dve"] * 2 + ["act"] * 21
        ev2 = {"dve": sem("ev2_dve"), "act": sem("ev2_act")}
        left2 = evacuated(order2, ev2)
        h1_sum, h1_done, cmp_sum, cmp_zero = sem("h1_sum"), sem("h1_done"), sem("cmp_sum"), sem("cmp_zero")
        vc_done = sem("vc_done")
        rope_nsa = rope_parts("r0", 10, lambda r: rp[:, r, :], rt1, rt2, lambda r: qr[:, r, :],
                              C("cos"), C("sin"), 4, lambda eng, r: left2(eng, r + 2))
        base2 = PIECE_AT["cmp_in"][0]
        with phase() as block:
            @block.sync
            def _(sp):
                ask_pieces(sp, PIECE_AT["z"][1] + R)

            @block.tensor
            def _(pe):
                def free(u):
                    if u >= 4:
                        left2(pe, u - 4)

                for u in range(12):
                    free(u)
                    feature_unit(pe, base2 + u, u % 4, h_parts)
                    if u >= 4:
                        rope_nsa[0](pe, u - 4)
                for kv, pe_name in enumerate(("pek", "pev")):
                    if kv == 0:
                        left2(pe, 1)
                    for q4 in range(4):
                        w = piece_ready(pe, PIECE_AT["cmp_w1"][0] + kv * 4 + q4)
                        for m in range(4):
                            tap = 4 * q4 + m
                            for ch in range(2):
                                o = ps[:, 6 + ch, kv * 64:kv * 64 + 2 * N_CMP].rearrange("p (g n) -> p g n", g=2)
                                wt = w[:, m * CMP_H + ch * P:m * CMP_H + (ch + 1) * P]
                                pe.matmul(o, wt, xc[:, kv, :, tap:tap + 8 * (N_CMP - 1) + 1:8],
                                          start=(tap == 0), stop=False)
                                mm = pe.matmul(o, wt, S(pe_name)[:, tap:tap + 1].unsqueeze(2).to_broadcast([P, 2, N_CMP]),
                                               start=False, stop=(tap == 15))
                        mm.then_inc(piece_used, 1)
                rope_nsa[0](pe, 8)
                rope_nsa[0](pe, 9)
                for u in range(12, 15):
                    free(u)
                    token_unit(pe, PIECE_AT["vsw"][0] + u - 12, u % 4, h_parts, tile_tokens)
                pe.wait_ge(h1_done, 2)
                for g in range(2):
                    for ch in range(2):
                        pe.matmul(ps[g * DH:(g + 1) * DH, 6, 128:128 + N_CMP], S("w2k")[:, ch * DH:(ch + 1) * DH],
                                  h1[:, 0, ch, g * N_CMP:(g + 1) * N_CMP], start=(ch == 0), stop=(ch == 1))
                    for ch in range(2):
                        mm = pe.matmul(ps[0:N_CMP, 7, 128 + g * DH:128 + (g + 1) * DH],
                                       h1[:, 1, ch, g * N_CMP:(g + 1) * N_CMP],
                                       S("w2v")[:, ch * DH:(ch + 1) * DH], start=(ch == 0), stop=(ch == 1))
                mm.then_inc(cmp_sum, 1)
                for u in range(15, 23):
                    free(u)
                    feature_unit(pe, PIECE_AT["z"][0] + u - 15, u % 4, h_parts)

            @block.scalar
            def _(act):
                def unit(u):
                    n = base2 + u + (8 if u >= 12 else 0)
                    act.wait_ge(piece_used, n + 1)
                    b = ps[:, u % 4, :]
                    if u < 12:
                        ins = act.activation(rp[:, u - 2, :], b, ACT.Copy)
                    elif u < 14:
                        ins = act.activation((vs, vw)[u - 12].rearrange("p a b -> p (a b)"), b, ACT.Copy)
                    elif u == 14:
                        ins = act.activation(gate, b.rearrange("p (a b) -> p a b", b=P)[:, :, 0:48], ACT.Sigmoid)
                    else:
                        ins = act.activation(zs[:, u - 15, :], b, ACT.Silu)
                    ins.then_inc(ev2["act"], 1)

                def piece_of(u):
                    return base2 + u + (8 if u >= 12 else 0)

                split_hi(act, piece_of(0))
                split_hi(act, piece_of(1))
                for u in range(12):
                    split_hi(act, piece_of(u + 2))
                    if u >= 2:
                        unit(u)
                act.wait_ge(piece_used, PIECE_AT["cmp_w1"][1])
                for kv in range(2):
                    act.activation(h1[:, kv, :, :], ps[:, 6:8, kv * 64:kv * 64 + 2 * N_CMP], ACT.Silu).then_inc(h1_done, 1)
                for u in range(12, 23):
                    if u + 2 < 23:
                        split_hi(act, piece_of(u + 2))
                    unit(u)

            @block.gpsimd
            def _(pool):
                parted = [base2 + u for u in range(12)] + [base2 + 8 + u for u in range(12, 23)]
                pool.memset(kcm, 0.0).then_inc(cmp_zero, 1)
                pool.memset(vbd, 0.0).then_inc(cmp_zero, 1)
                for u, n in enumerate(parted):
                    split_lo(pool, n)
                    if 5 <= u < 15:
                        rope_nsa[1](pool, u - 5)

            @block.vector
            def _(dve):
                for kv in range(2):
                    dve.wait_ge(piece_used, base2 + kv + 1)
                    for g in range(2):
                        pair = ps[g * DH:(g + 1) * DH, kv, :].rearrange("p (s par) -> p s par", par=2)
                        for par in range(2):
                            ins = dve.tensor_copy(xc[par * DH:(par + 1) * DH, kv, g, :], pair[:, :, par])
                            if g * 2 + par < 3:
                                note("dve", ins)
                            else:
                                dve.wait_ge(dve_step, counts["dve"])
                                ins.then_inc(ev2["dve"], 1)
                for r in range(10):
                    rope_nsa[2](dve, r)
                dve.wait_ge(cmp_sum, 1)
                dve.wait_ge(cmp_zero, 2)
                for g in range(2):
                    rows = slice(g * DH, (g + 1) * DH)
                    dve.tensor_copy(kcm[rows, g, 0:N_CMP], ps[rows, 6, 128:128 + N_CMP])
                for a in range(4):
                    dve.tensor_copy(vbd[a * 32:a * 32 + N_CMP, a, :],
                                    ps[0:N_CMP, 7, 128 + (a % 2) * DH:128 + (a % 2 + 1) * DH])
        if until < 3:
            drain()
            return

        sc = area(WORK, NH * CMP_PAD)
        pc = area(WORK + 512, NH * CMP_PAD)
        ptc = area(WORK + 1024, 4 * P)
        cmx = area(WORK + 1536, NH)
        cden = area(WORK + 1552, NH)
        cr = area(WORK + 1568, NH)
        c_qk, c_sub, c_exp, c_t, c_copied, c_pv, c_out = (sem("c_" + n) for n in "qk sub exp t copied pv out".split())
        by_head = lambda v: v.rearrange("p (h n) -> p h n", h=NH)
        with phase() as block:
            @block.tensor
            def _(pe):
                for i in range(TT):
                    for u in range(8):
                        mm = pe.matmul(ps[:, i, u * 64:(u + 1) * 64], rp[:, 2 + u, tile_tokens(i)],
                                       kcm.rearrange("p g n -> p (g n)"), start=True, stop=True)
                    mm.then_inc(c_qk, 1)
                for i in range(TT):
                    pe.wait_ge(c_exp, i + 1)
                    for a in range(4):
                        mm = pe.transpose(ps[:, 4, a * P:(a + 1) * P], pc[:, a * P:(a + 1) * P], ident)
                    mm.then_inc(c_t, 1)
                    pe.wait_ge(c_copied, i + 1)
                    if i >= 1:
                        pe.wait_ge(c_out, i)
                    for a in range(4):
                        mm = pe.matmul(ps[:, 5 + a // 2, (a % 2) * 256:(a % 2 + 1) * 256], ptc[:, a * P:(a + 1) * P],
                                       vbd.rearrange("p a d -> p (a d)"), start=True, stop=True)
                    mm.then_inc(c_pv, 1)

            @block.scalar
            def _(act):
                for i in range(TT):
                    act.wait_ge(c_sub, i + 1)
                    if i >= 1:
                        act.wait_ge(c_t, i)
                        act.wait_ge(c_out, i)
                    act.activation(pc, sc, ACT.Exp, scale=SCALE).then_inc(c_exp, 1)
                    act.wait_ge(c_t, i + 1)
                    if i >= 1:
                        act.wait_ge(c_pv, i)
                    act.activation(ptc, ps[:, 4, :], ACT.Copy).then_inc(c_copied, 1)

            @block.vector
            def _(dve):
                for i in range(TT):
                    dve.wait_ge(c_qk, i + 1)
                    if i >= 1:
                        dve.wait_ge(c_exp, i)
                    mask = C("mcmp")[:, i * CMP_PAD:(i + 1) * CMP_PAD].unsqueeze(1).to_broadcast([P, NH, CMP_PAD])
                    v = note("dve", dve.tensor_tensor(by_head(sc), by_head(ps[:, i, :]), mask, ALU.add))
                    dve.wait_ge(dve_step, v)
                    v = note("dve", dve.tensor_reduce(cmx, by_head(sc), AX.X, ALU.max))
                    dve.wait_ge(dve_step, v)
                    dve.tensor_tensor(by_head(sc), by_head(sc), cmx.unsqueeze(2).to_broadcast([P, NH, CMP_PAD]),
                                      ALU.subtract).then_inc(c_sub, 1)
                    dve.wait_ge(c_exp, i + 1)
                    v = note("dve", dve.tensor_reduce(cden, by_head(pc), AX.X, ALU.add))
                    dve.wait_ge(dve_step, v)
                    v = note("dve", dve.reciprocal(cr, cden))
                    dve.wait_ge(dve_step, v)
                    v = note("dve", dve.scalar_tensor_tensor(
                        out=cr.rearrange("p (u g) -> p u g", g=2), in0=cr.rearrange("p (u g) -> p u g", g=2),
                        scalar=C("valid")[:, i:i + 1],
                        in1=gate[:, i, 0:48:3].rearrange("p (g u) -> p u g", g=2), op0=ALU.mult, op1=ALU.mult))
                    dve.wait_ge(dve_step, v)
                    dve.wait_ge(c_pv, i + 1)
                    dst = ot[:, i, :].rearrange("p (g u d) -> p u g d", g=2, d=DH)
                    crv = cr.rearrange("p (u g) -> p u g", g=2)
                    for half in range(2):
                        us = slice(4 * half, 4 * half + 4)
                        ins = dve.tensor_tensor(dst[:, us, :, :],
                                                ps[:, 5 + half, :].rearrange("p (u g d) -> p u g d", g=2, d=DH),
                                                crv[:, us, :].unsqueeze(3).to_broadcast([P, 4, 2, DH]), ALU.mult)
                        if half == 0:
                            dve.wait_ge(dve_step, note("dve", ins))
                        else:
                            ins.then_inc(c_out, 1)
        if until < 4:
            drain()
            return

        def attention(tag, block, units, work, finish, finish_pool=None, pe_filler=None, dve_filler=None, ask=0,
                      pads=()):
            LT, LP = 3, 5
            SB, PB, TB = 3, 4, 3
            N = len(units)
            neg = area(work, SB, T)
            prt = area(work + SB * T, TB, T)
            prob = place("prob_" + tag, WR_AT, [PB, T])
            pad_zero, pad_dve, pad_act = sem(tag + "_pad_zero"), sem(tag + "_pad_dve"), sem(tag + "_pad_act")
            nmax = area(work + 3584, N)
            den = area(work + 3584 + N, N)
            s_done, neg_done, exp_done = since("att_scores", N), since("att_neg", N), since("att_exp", N)
            t_done, pv_done = since("att_transposed", N), since("att_pv", N)
            copied = [since("att_copied_act", N // 2), since("att_copied_dve", N // 2)]
            o_read = since("att_o_read", N // 8)

            def wait_copied(eng, n):
                copied[n % 2].wait(eng, n // 2 + 1)

            def copy(n, eng):
                nb = len(units[n][3])
                t_done.wait(eng, n + 1)
                if n >= TB:
                    pv_done.wait(eng, n - TB + 1)
                src, dst = ps[:, 3 + n % 2, 0:nb * P], prt[:, n % TB, 0:nb * P]
                if n % 2 == 0:
                    eng.activation(dst, src, ACT.Copy).then_inc(copied[0].sem, 1)
                else:
                    eng.tensor_copy(dst, src).then_inc(copied[1].sem, 1)

            @block.sync
            def _(sp):
                ask_pieces(sp, ask)

            @block.tensor
            def _(pe):
                pe.wait_ge(pad_zero, 2 * len(pads))
                pe.wait_ge(pad_dve, len(pads))
                pe.wait_ge(pad_act, len(pads))
                for n in range(N + LP):
                    if n < N:
                        q, k, mask, vb, _ = units[n]
                        if n >= SB:
                            neg_done.wait(pe, n - SB + 1)
                        pe.matmul(ps[:, n % SB, 0:len(vb) * P], q, k, start=True, stop=True).then_inc(s_done.sem, 1)
                    if LT <= n < N + LT:
                        m = n - LT
                        exp_done.wait(pe, m + 1)
                        if m >= 2:
                            wait_copied(pe, m - 2)
                        nb = len(units[m][3])
                        for b in range(nb):
                            mm = pe.transpose(ps[:, 3 + m % 2, b * P:(b + 1) * P],
                                              prob[:, m % PB, b * P:(b + 1) * P], ident)
                        mm.then_inc(t_done.sem, 1)
                    if pe_filler and n < N:
                        pe_filler(pe, n)
                    if n >= LP:
                        m = n - LP
                        wait_copied(pe, m)
                        if m % 8 == 0 and m >= 16:
                            o_read.wait(pe, m // 8 - 1)
                        vb = units[m][3]
                        for b, v in enumerate(vb):
                            mm = pe.matmul(ps[:, 5 + (m // 8) % 2, (m % 8) * DH:(m % 8 + 1) * DH],
                                           prt[:, m % TB, b * P:(b + 1) * P], v,
                                           start=(b == 0), stop=(b == len(vb) - 1))
                        mm.then_inc(pv_done.sem, 1)

            @block.scalar
            def _(act):
                for dst, src in pads:
                    act.activation(dst[DH:P, 1], src[DH:P], ACT.Copy).then_inc(pad_act, 1)
                for n in range(N + LT):
                    if n < N:
                        w = len(units[n][3]) * P
                        neg_done.wait(act, n + 1)
                        if n >= PB:
                            t_done.wait(act, n - PB + 1)
                        act.activation(prob[:, n % PB, 0:w], neg[:, n % SB, 0:w], ACT.Exp, scale=-1.0,
                                       bias=nmax[:, n:n + 1], accum_out=den[:, n:n + 1]).then_inc(exp_done.sem, 1)
                    if n >= LT and (n - LT) % 2 == 0:
                        copy(n - LT, act)

            @block.vector
            def _(dve):
                for dst, src in pads:
                    dve.tensor_copy(dst[0:DH, 0], src[0:DH]).then_inc(pad_dve, 1)
                for n in range(N + LP + 1):
                    if n < N:
                        q, k, mask, vb, init = units[n]
                        w = len(vb) * P
                        s_done.wait(dve, n + 1)
                        if n >= SB:
                            exp_done.wait(dve, n - SB + 1)
                        dve.tensor_tensor_reduce(out=neg[:, n % SB, 0:w], in0=ps[:, n % SB, 0:w], in1=mask,
                                                 scale=-SCALE, scalar=init, op0=ALU.add, op1=ALU.min,
                                                 accum_out=nmax[:, n:n + 1]).then_inc(neg_done.sem, 1)
                    if LT <= n < N + LT and (n - LT) % 2 == 1:
                        copy(n - LT, dve)
                    if dve_filler and n < N:
                        dve_filler(dve, n)
                    if n > LP and (n - LP - 1) % 8 == 7:
                        g = (n - LP - 1) // 8
                        exp_done.wait(dve, 8 * (g + 1))
                        pv_done.wait(dve, 8 * (g + 1))
                        finish(dve, g, ps[:, 5 + g % 2, :].rearrange("p (h d) -> p h d", d=DH),
                               den[:, 8 * g:8 * g + 8], nmax[:, 8 * g:8 * g + 8], o_read)

            @block.gpsimd
            def _(pool):
                for dst, _ in pads:
                    pool.memset(dst[DH:P, 0], 0.0).then_inc(pad_zero, 1)
                    pool.memset(dst[0:DH, 1], 0.0).then_inc(pad_zero, 1)
                if finish_pool:
                    finish_pool(pool, o_read)
            return nmax, den

        ks_pad = place("ks_pad", WR_AT + 4 * T, [2, 2, T])
        nsa_units = []
        for branch, (ku, vt) in enumerate(((0, vs), (1, vw))):
            for i in range(TT):
                for h in range(NH):
                    g = h // 8
                    nsa_units.append((qr[:, 2 + h % 8, tile_tokens(i)], ks_pad[:, g, ku, 0:(i + 1) * P],
                                      C("causal")[:, T - (i + 1) * P:T],
                                      [vt[:, b, g * DH:(g + 1) * DH] for b in range(i + 1)], BIG))
        gr = area(WORK + 3840, 2, 8)
        added = sem("nsa_added")
        gtmp = place("gtmp", HR_AT, [2, 512])

        def nsa_finish(dve, g, o, den, nmax, o_read):
            branch, i, half = g // 8, (g // 2) % 4, g % 2
            r = gr[:, g % 2, :]
            v = note("dve", dve.reciprocal(r, den))
            dve.wait_ge(dve_step, v)
            v = note("dve", dve.tensor_tensor(r, r, gate[:, i, 24 * half + 1 + branch:24 * half + 24:3], ALU.mult))
            dve.wait_ge(dve_step, v)
            if g >= 2:
                dve.wait_ge(added, g - 1)
            dve.tensor_tensor(gtmp[:, g % 2, :].rearrange("p (h d) -> p h d", d=DH), o,
                              r.unsqueeze(2).to_broadcast([P, 8, DH]), ALU.mult).then_inc(o_read.sem, 1)

        def nsa_finish_pool(pool, o_read):
            for g in range(16):
                i, half = (g // 2) % 4, g % 2
                o_read.wait(pool, g + 1)
                if g >= 8:
                    pool.wait_ge(added, g - 7)
                dst = ot[:, i, half * 512:(half + 1) * 512]
                pool.tensor_tensor(dst, dst, gtmp[:, g % 2, :], ALU.add).then_inc(added, 1)

        ada_sum = place("ada_sum", HR_AT + 4 * T, [2, PIECE])
        ada_full, ada_taken = sem("ada_full"), sem("ada_taken")
        ada_pace, ada_after, due = (0, 0, 0.5, 0.75, 1.0), [], 0.0
        for unit in nsa_units:
            due += ada_pace[len(unit[3])]
            ada_after.append(min(int(due), ADA12[1] - ADA12[0]))
        assert ada_after[-1] == ADA12[1] - ADA12[0]

        def ada_dve(dve, n):
            for j in range(ada_after[n - 1] if n else 0, ada_after[n]):
                piece, chunk, k = ADA12[0] + j, j // KD, j % KD
                total, c = ada_sum[:, chunk % 2, :], csil[:, (0 if chunk < 3 else 1), k:k + 1]
                dve.wait_ge(piece_in[piece % R], 16 * (piece // R + 1))
                if k == 0:
                    if chunk >= 2:
                        dve.wait_ge(ada_taken, chunk - 1)
                    dve.tensor_scalar(total, ring[:, piece % R, :], c, None, ALU.mult).then_inc(ada_used, 1)
                else:
                    dve.wait_ge(ada_used, j)
                    dve.scalar_tensor_tensor(out=total, in0=ring[:, piece % R, :], scalar=c, in1=total,
                                             op0=ALU.mult, op1=ALU.add).then_inc(ada_used, 1)

        def ada_pe(pe, n):
            for chunk in range(9):
                last = (chunk + 1) * KD - 1
                if n == min(next(i for i, a in enumerate(ada_after) if a > last) + 2, len(nsa_units) - 1):
                    pe.wait_ge(ada_used, last + 1)
                    for b in range(KD):
                        col = 24 + chunk * KD + b
                        mm = pe.matmul(ps[:, 7, col:col + 1], ada_sum[:, chunk % 2, b * P:(b + 1) * P],
                                       C("ones")[:, 0:1], start=True, stop=True)
                    mm.then_inc(ada_taken, 1)

        with phase() as block:
            attention("nsa", block, nsa_units, WORK, nsa_finish, nsa_finish_pool, ada_pe, ada_dve,
                      ADA12[1] + R, [(ks_pad, qr[:, 0:2, :])])
        Work.used += ADA12[1] - ADA12[0]
        if until < 5:
            drain()
            return

        def out_projection(tag, block, at, ready, gate_cols, dve_before, pe_before, act_before,
                           pool_before=None, n_ready=KD):
            added_x = sem(tag + "_x")

            @block.sync
            def _(sp):
                ask_pieces(sp, at + KD + R)

            @block.tensor
            def _(pe):
                if at == ADA12[1]:
                    pe.sem_inc(piece_used, ADA12[1] - ADA12[0])
                pe_before(pe)
                ready.wait(pe, n_ready)
                for u in range(KD):
                    if u >= 3:
                        pe.wait_ge(added_x, u - 2)
                    feature_unit(pe, at + u, 4 + u % 3, h_parts)

            @block.vector
            def _(dve):
                dve_before(dve)
                for u in range(KD):
                    dve.wait_ge(piece_used, at + u + 1)
                    dve.scalar_tensor_tensor(out=xT[:, u, :], in0=ps[:, 4 + u % 3, :],
                                             scalar=gate_cols[:, u:u + 1], in1=xT[:, u, :],
                                             op0=ALU.mult, op1=ALU.add).then_inc(added_x, 1)

            @block.scalar
            def _(act):
                split_hi(act, at)
                split_hi(act, at + 1)
                act_before(act)
                for u in range(2, KD):
                    split_hi(act, at + u)

            @block.gpsimd
            def _(pool):
                split_lo(pool, at)
                split_lo(pool, at + 1)
                if pool_before:
                    pool_before(pool)
                for u in range(2, KD):
                    split_lo(pool, at + u)
            return added_x

        def transposes(pe, src, units, read, done):
            for u in range(units):
                if u >= 4:
                    pe.wait_ge(read, u - 3)
                for i in range(TT):
                    mm = pe.transpose(ps[:, u % 4, i * P:(i + 1) * P], src[:, i, u * P:(u + 1) * P], ident)
                mm.then_inc(done, 1)

        e_t, e_z, e_mod = sem("e_transposed"), sem("e_gated"), sem("e_mod")
        e_hi, e_lo = sem("e_hi"), sem("e_lo")
        with phase() as block:
            def dve5(dve):
                for u in range(KD + 2):
                    if u < KD:
                        dve.wait_ge(e_t, u + 1)
                        dve.tensor_tensor(zs[:, u, :], ps[:, u % 4, :], zs[:, u, :], ALU.mult).then_inc(e_z, 1)
                    if u >= 2:
                        k = u - 2
                        dve.wait_ge(e_hi, k + 1)
                        dve.tensor_tensor(h_lo[:, k, :], zs[:, k, :], h_hi[:, k, :].bitcast(F32),
                                          ALU.subtract).then_inc(e_lo, 1)
                dve.tensor_tensor(mod[:, 24:96], ps[:, 7, 24:96], S("adab")[:, 24:96], ALU.add).then_inc(e_mod, 1)
                dve.wait_ge(e_mod, 1)
                for i, (col, g) in enumerate(((32, "ng1"), (56, "n1g"), (80, "n2g"))):
                    dve.scalar_tensor_tensor(out=amp[:, 1 + i, :], in0=mod[:, col:col + 8], scalar=1.0, in1=S(g),
                                             op0=ALU.add, op1=ALU.mult)
            def act5(act):
                for u in range(KD):
                    act.wait_ge(e_z, u + 1)
                    act.activation(h_hi[:, u, :], zs[:, u, :], ACT.Copy).then_inc(e_hi, 1)

            out_projection("e", block, PIECE_AT["nsa_out"][0], Since(e_lo, 0), mod[:, 16:24], dve5,
                           lambda pe: transposes(pe, ot, KD, e_z, e_t), act5)
        if until < 6:
            drain()
            return

        n1 = norm_parts("n1", xT, ntmp, nsq, KD, 6, amp[:, 1, :], mod[:, 24:32], h_parts)
        qd, kd = area(0, 8, T), area(4096, 8, T)
        zd = area(8192, 8, T)
        vd = area(12288, TT, D)
        od = area(16384, TT, D)
        raw6 = area(16384, 4, T)
        rt61, rt62 = area(18432, 2, T), area(19456, 2, T)
        order6 = ["act"] * 32
        ev6 = {"act": sem("ev6_act")}
        left6 = evacuated(order6, ev6)
        rope_dil = rope_parts("r6", 16, lambda r: raw6[:, r % 4, :], rt61, rt62,
                              lambda r: (qd if r < 8 else kd)[:, r % 8, :], C("cos"), C("sin"), 4, left6)
        base6 = PIECE_AT["dq"][0]
        with phase() as block:
            @block.sync
            def _(sp):
                ask_pieces(sp, PIECE_AT["dz"][1] + R)

            @block.tensor
            def _(pe):
                n1[2](pe)
                n1[7].wait(pe, KD)
                for u in range(32):
                    if u >= 4:
                        left6(pe, u - 4)
                    if 16 <= u < 24:
                        token_unit(pe, base6 + u, u % 4, h_parts, tile_tokens if u < 19 else class_tokens)
                    else:
                        feature_unit(pe, base6 + u, u % 4, h_parts)
                    if 2 <= u < 18:
                        rope_dil[0](pe, u - 2)

            @block.scalar
            def _(act):
                split_hi(act, base6)
                split_hi(act, base6 + 1)
                n1[1](act)
                n1[3](act)
                n1[5](act)
                for u in range(32):
                    if u + 2 < 32:
                        split_hi(act, base6 + u + 2)
                    act.wait_ge(piece_used, base6 + u + 1)
                    b = ps[:, u % 4, :]
                    if u < 16:
                        if u >= 4:
                            rope_dil[3].wait(act, u - 3)
                        ins = act.activation(raw6[:, u % 4, :], b, ACT.Copy)
                    elif u < 24:
                        ins = act.activation(vd[:, :, (u - 16) * P:(u - 15) * P],
                                             b.rearrange("p (a b) -> p a b", b=P), ACT.Copy)
                    else:
                        ins = act.activation(zd[:, u - 24, :], b, ACT.Silu)
                    ins.then_inc(ev6["act"], 1)

            @block.gpsimd
            def _(pool):
                for u in range(32):
                    split_lo(pool, base6 + u)
                    if 3 <= u < 19:
                        rope_dil[1](pool, u - 3)

            @block.vector
            def _(dve):
                n1[0](dve)
                n1[4](dve)
                for r in range(16):
                    rope_dil[2](dve, r)
        if until < 7:
            drain()
            return

        kd_pad = place("kd_pad", HR_AT, [2, KD, T])
        dil_units = []
        for i in range(TT):
            for h in range(NH):
                u, keys = h // 2, kd_pad[:, h % 2]
                cols = slice(h * DH, (h + 1) * DH)
                if h < 6:
                    lo = max(i - 1, 0)
                    dil_units.append((qd[:, u, tile_tokens(i)], keys[:, u, lo * P:(i + 1) * P],
                                      C("band129")[:, (0 if i else P):2 * P],
                                      [vd[:, b, cols] for b in range(lo, i + 1)], BIG))
                else:
                    mask = C("causal")[:, T - P:T] if h < 11 else C("causal16")
                    dil_units.append((qd[:, u, class_tokens(i)], keys[:, u, class_tokens(i)], mask,
                                      [vd[:, i, cols]], BIG))
        dr = sb("dr", [P, 2, 8])

        def plain_finish(dst):
            def finish(dve, g, o, den, nmax, o_read):
                r = dr[:, g % 2, :]
                v = note("dve", dve.reciprocal(r, den))
                dve.wait_ge(dve_step, v)
                dve.tensor_tensor(dst(g), o, r.unsqueeze(2).to_broadcast([P, 8, DH]), ALU.mult).then_inc(o_read.sem, 1)
            return finish

        with phase() as block:
            dnmax, dden = attention("dil", block, dil_units, 20480, plain_finish(
                lambda g: od[:, g // 2, (g % 2) * 512:(g % 2 + 1) * 512].rearrange("p (h d) -> p h d", d=DH)),
                pads=[(kd_pad[:, :, u:u + 2, :], kd[:, u:u + 2, :]) for u in range(0, KD, 2)])
        if until < 8:
            drain()
            return

        lse = area(20480, TT, NH)
        lsub = area(20544, TT, NH)
        lg = area(20608, 3, TT)
        lmx = area(20620, 3, TT)
        lrow = area(20640, 3, T)
        lmax = area(22176, T)
        lsum = area(22688, T)
        f_ln, f_lse, f_sub, f_exp, f_sum, f_log, f_row, f_rows, f_e, f_eexp, f_alpha, f_t, f_az, f_z = (
            sem("f_" + n) for n in "ln lse sub exp sum log row rows e eexp alpha t az gated".split())
        f_mx, f_hi, f_lo = sem("f_mx"), sem("f_hi"), sem("f_lo")
        oz = area(0, KD, T)
        dview = dden.rearrange("p (a b) -> p a b", b=NH)
        with phase() as block:
            def act8(act):
                act.activation(lse, dview, ACT.Ln).then_inc(f_ln, 1)
                act.wait_ge(f_sub, 3)
                act.activation(lsub, lsub, ACT.Exp).then_inc(f_exp, 1)
                act.wait_ge(f_sum, 3)
                act.activation(lg, lg, ACT.Ln).then_inc(f_log, 1)
                act.wait_ge(f_rows, 1)
                for g in range(3):
                    act.activation(lrow[:, g, :], ps[:, 4 + g, :], ACT.Copy).then_inc(f_row, 1)
                act.wait_ge(f_e, 3)
                act.activation(lrow, lrow, ACT.Exp).then_inc(f_eexp, 1)
                for u in range(KD):
                    act.wait_ge(f_z, u + 1)
                    act.activation(h_hi[:, u, :], zd[:, u, :], ACT.Copy).then_inc(f_hi, 1)

            def dve8(dve):
                dve.wait_ge(f_ln, 1)
                dve.tensor_tensor(lse, lse, dnmax.rearrange("p (a b) -> p a b", b=NH), ALU.subtract).then_inc(f_lse, 1)
                dve.wait_ge(f_lse, 1)
                for g, (a, b) in enumerate(DIL_GROUPS):
                    dve.tensor_reduce(lmx[:, g, :], lse[:, :, a:b], AX.X, ALU.max).then_inc(f_mx, 1)
                dve.wait_ge(f_mx, 3)
                for g, (a, b) in enumerate(DIL_GROUPS):
                    dve.tensor_tensor(lsub[:, :, a:b], lse[:, :, a:b],
                                      lmx[:, g, :].unsqueeze(2).to_broadcast([P, TT, b - a]),
                                      ALU.subtract).then_inc(f_sub, 1)
                dve.wait_ge(f_exp, 1)
                for g, (a, b) in enumerate(DIL_GROUPS):
                    dve.tensor_reduce(lg[:, g, :], lsub[:, :, a:b], AX.X, ALU.add).then_inc(f_sum, 1)
                dve.wait_ge(f_log, 1)
                for g, (a, b) in enumerate(DIL_GROUPS):
                    dve.scalar_tensor_tensor(out=lg[:, g, :], in0=lg[:, g, :], scalar=-math.log(b - a),
                                             in1=lmx[:, g, :], op0=ALU.add, op1=ALU.add).then_inc(f_log, 1)
                dve.wait_ge(f_row, 3)
                v = note("dve", dve.tensor_tensor(lmax, lrow[:, 0, :], lrow[:, 1, :], ALU.max))
                dve.wait_ge(dve_step, v)
                v = note("dve", dve.tensor_tensor(lmax, lmax, lrow[:, 2, :], ALU.max))
                dve.wait_ge(dve_step, v)
                for g in range(3):
                    dve.tensor_tensor(lrow[:, g, :], lrow[:, g, :], lmax, ALU.subtract).then_inc(f_e, 1)
                dve.wait_ge(f_eexp, 1)
                v = note("dve", dve.tensor_tensor(lsum, lrow[:, 0, :], lrow[:, 1, :], ALU.add))
                dve.wait_ge(dve_step, v)
                v = note("dve", dve.tensor_tensor(lsum, lsum, lrow[:, 2, :], ALU.add))
                dve.wait_ge(dve_step, v)
                v = note("dve", dve.reciprocal(lsum, lsum))
                dve.wait_ge(dve_step, v)
                for g in range(3):
                    dve.scalar_tensor_tensor(out=lrow[:, g, :], in0=lrow[:, g, :], scalar=3.0, in1=lsum,
                                             op0=ALU.mult, op1=ALU.mult).then_inc(f_alpha, 1)
                dve.wait_ge(f_alpha, 3)
                for u in range(KD):
                    dve.wait_ge(f_t, u + 1)
                    parts = [(slice(0, P), 0 if u < 3 else 1 if u < 5 else 2)]
                    if u == 5:
                        parts = [(slice(0, DH), 1), (slice(DH, P), 2)]
                    for rows, g in parts:
                        src = ps[rows, u % 4, :]
                        dst, al = oz[rows, u, :], lrow[rows, g, :]
                        if g:
                            src = src.rearrange("p (r a) -> p a r", r=TT)
                            dst = dst.rearrange("p (a r) -> p a r", r=TT)
                            al = al.rearrange("p (a r) -> p a r", r=TT)
                        ins = dve.tensor_tensor(dst, src, al, ALU.mult)
                        if rows.stop < P:
                            v = note("dve", ins)
                            dve.wait_ge(dve_step, v)
                        else:
                            ins.then_inc(f_az, 1)
                for u in range(KD):
                    dve.wait_ge(f_hi, u + 1)
                    dve.tensor_tensor(h_lo[:, u, :], zd[:, u, :], h_hi[:, u, :].bitcast(F32),
                                      ALU.subtract).then_inc(f_lo, 1)

            def pool8(pool):
                for u in range(KD):
                    pool.wait_ge(f_az, u + 1)
                    pool.tensor_tensor(zd[:, u, :], oz[:, u, :], zd[:, u, :], ALU.mult).then_inc(f_z, 1)

            def pe8(pe):
                pe.wait_ge(f_log, 4)
                for g in range(3):
                    for i in range(TT):
                        cols = tile_tokens(i) if g == 0 else class_tokens(i)
                        mm = pe.matmul(ps[:, 4 + g, cols], lg[:, g, i:i + 1].to_broadcast([P, P]), ident,
                                       start=True, stop=True)
                mm.then_inc(f_rows, 1)
                transposes(pe, od, KD, f_az, f_t)
                pe.wait_ge(f_row, 3)
            out_projection("f", block, PIECE_AT["dil_out"][0], Since(f_lo, 0), mod[:, 40:48], dve8, pe8, act8, pool8)
        if until < 9:
            drain()
            return

        nf = norm_parts("nf", xT, xT, nsq, KD, 6, S("fg"), None)
        n2 = norm_parts("n2", xT, ntmp, nsq, KD, 7, amp[:, 2, :], mod[:, 48:56], h_parts)
        raw9, sq9, qn9 = area(0, 5, T), area(2560, 5, T), area(5120, 5, T)
        qr9 = area(7680, 5, T)
        v9 = area(10240, TT, P)
        ccs = area(10752, 4, T)
        hp = area(12800, 4, T + 2)
        conv = area(14856, 4, T)
        rt91, rt92 = area(16904, 2, T), area(17928, 2, T)
        sd9 = area(18952, 2, T)
        va9 = area(19976, 2, T)
        order9 = ["act"] * 10 + ["dve"] * 8
        ev9 = {"act": sem("ev9_act"), "dve": sem("ev9_dve")}
        left9 = evacuated(order9, ev9)
        q_sq, q_sum, q_var, q_root, q_norm = sem("q_sq"), sem("q_sum"), sem("q_var"), sem("q_root"), sem("q_norm")
        hp_zero, conv_in = sem("hp_zero"), sem("conv_in")
        rope_two = rope_parts("r9", 5, lambda r: qn9[:, r, :], rt91, rt92, lambda r: qr9[:, r, :],
                              rope2[:, 0, :], rope2[:, 1, :], 4, lambda eng, r: eng.wait_ge(q_norm, r + 1))
        base9 = PIECE_AT["q2"][0]
        with phase() as block:
            @block.sync
            def _(sp):
                ask_pieces(sp, PIECE_AT["cb"][1] + R)

            @block.tensor
            def _(pe):
                nf[2](pe)
                n2[2](pe)
                n2[7].wait(pe, KD)
                for u in range(18):
                    if u >= 4:
                        left9(pe, u - 4)
                    if u == 5:
                        token_unit(pe, base9 + u, u % 4, h_parts, tile_tokens)
                    else:
                        feature_unit(pe, base9 + u, u % 4, h_parts)
                    if 1 <= u < 6:
                        r = u - 1
                        pe.wait_ge(q_sq, r + 1)
                        if r >= 2:
                            pe.wait_ge(q_var, r - 1)
                        pe.matmul(ps[:, 6 + r % 2, :], C("bones"), sq9[:, r, :], start=True,
                                  stop=True).then_inc(q_sum, 1)
                    if 4 <= u < 9:
                        rope_two[0](pe, u - 4)

            @block.scalar
            def _(act):
                split_hi(act, base9)
                split_hi(act, base9 + 1)
                nf[1](act)
                nf[3](act)
                nf[6].wait(act, KD)
                n2[1](act)
                n2[3](act)
                n2[5](act)
                for u in range(16):
                    split_hi(act, base9 + u + 2)
                    if u >= 10:
                        continue
                    act.wait_ge(piece_used, base9 + u + 1)
                    b = ps[:, u % 4, :]
                    if u < 5:
                        act.activation(raw9[:, u, :], b, ACT.Copy).then_inc(ev9["act"], 1)
                        left9(act, u)
                        act.activation(sq9[:, u, :], raw9[:, u, :], ACT.Square).then_inc(q_sq, 1)
                        act.wait_ge(q_var, u + 1)
                        act.activation(sd9[:, u % 2, :], va9[:, u % 2, :], ACT.Sqrt).then_inc(q_root, 1)
                    elif u == 5:
                        act.activation(v9.rearrange("p a b -> p (a b)"), b, ACT.Copy).then_inc(ev9["act"], 1)
                    else:
                        act.activation(ccs[:, u - 6, :], b, ACT.Copy).then_inc(ev9["act"], 1)

            @block.gpsimd
            def _(pool):
                pool.memset(hp[:, :, 0:2], 0.0).then_inc(hp_zero, 1)
                for u in range(18):
                    split_lo(pool, base9 + u)
                    if 8 <= u < 13:
                        rope_two[1](pool, u - 8)

            @block.vector
            def _(dve):
                nf[0](dve)
                nf[4](dve)
                nf[6].wait(dve, KD)
                n2[0](dve)
                n2[4](dve)
                for r in range(5):
                    dve.wait_ge(q_sum, r + 1)
                    dve.tensor_scalar(va9[:, r % 2, :], ps[:, 6 + r % 2, :], 1.0 / DH, EPS,
                                      ALU.mult, ALU.add).then_inc(q_var, 1)
                    dve.wait_ge(q_root, r + 1)
                    inverse_root(dve, va9[:, r % 2, :], sd9[:, r % 2, :], rstd[:, :])
                    dve.scalar_tensor_tensor(out=qn9[:, r, :], in0=raw9[:, r, :],
                                             scalar=S("qg" if r < 4 else "kg"), in1=rstd[:, :],
                                             op0=ALU.mult, op1=ALU.mult).then_inc(q_norm, 1)
                    dve.wait_ge(q_norm, r + 1)
                for r in range(5):
                    rope_two[2](dve, r)
                dve.wait_ge(hp_zero, 1)
                for u in range(4):
                    dve.wait_ge(piece_used, base9 + 10 + u + 1)
                    left9(dve, 6 + u)
                    dve.tensor_tensor(hp[:, u, 2:T + 2], ps[:, (10 + u) % 4, :], ccs[:, u, :],
                                      ALU.mult).then_inc(ev9["dve"], 1)
                for u in range(4):
                    left9(dve, 10 + u)
                    w = S("convw")
                    v = note("dve", dve.tensor_scalar(conv[:, u, :], hp[:, u, 0:T], w[:, u:u + 1], None, ALU.mult))
                    for k in (1, 2):
                        dve.wait_ge(dve_step, v)
                        v = note("dve", dve.scalar_tensor_tensor(
                            out=conv[:, u, :], in0=hp[:, u, k:T + k], scalar=w[:, 4 * k + u:4 * k + u + 1],
                            in1=conv[:, u, :], op0=ALU.mult, op1=ALU.add))
                    dve.wait_ge(dve_step, v)
                    dve.wait_ge(piece_used, base9 + 14 + u + 1)
                    dve.tensor_tensor(conv[:, u, :], ps[:, (14 + u) % 4, :], conv[:, u, :],
                                      ALU.mult).then_inc(ev9["dve"], 1)
        if until < 10:
            drain()
            return

        neg_sink = sb("neg_sink", [P, NQ2])
        o10 = area(0, TT, 512)
        k_pad = place("k_pad", HR_AT, [2, 1, T])
        win_units = []
        for i in range(TT):
            for h in range(NQ2):
                g = h // 4
                lo = max(i - 1, 0)
                win_units.append((qr9[:, h % 4, tile_tokens(i)], k_pad[:, g, 0, lo * P:(i + 1) * P],
                                  C("band128")[:, (0 if i else P):2 * P],
                                  [v9[:, b, g * DH:(g + 1) * DH] for b in range(lo, i + 1)],
                                  neg_sink[:, h:h + 1]))

        def win_finish(dve, g, o, den, nmax, o_read):
            dve.tensor_copy(o10[:, g, :].rearrange("p (h d) -> p h d", d=DH), o).then_inc(o_read.sem, 1)

        with phase() as block:
            @block.vector
            def _(dve):
                dve.tensor_scalar(neg_sink[:, :], S("sinks"), -1.0, None, ALU.mult)
        with phase() as block:
            wnmax, wden = attention("win", block, win_units, 18440, win_finish, pads=[(k_pad, qr9[:, 4:5, :])])

        at11, m11 = area(2048, 4, T), area(4096, 8, T)
        sq11 = area(8192, 4, T)
        se = area(12288, TT, NQ2)
        rd = area(12320, TT, NQ2)
        g_e, g_x, g_d, g_o, g_t, g_a = (sem("g_" + n) for n in "e sinks d o t a".split())
        na = norm_parts("na", at11, m11[:, 0:4, :], sq11, 4, 4, S("aog"), None, (h_hi[:, 0:4, :], h_lo[:, 0:4, :]))
        nb_ = norm_parts("nb", conv, m11[:, 4:8, :], sq11, 4, 5, S("cog"), None, (h_hi[:, 4:8, :], h_lo[:, 4:8, :]))
        m_ready = sem("m_ready")
        with phase() as block:
            def act11(act):
                act.wait_ge(g_e, 1)
                act.activation(se, se, ACT.Exp).then_inc(g_x, 1)
                act.wait_ge(g_a, 4)
                na[1](act)
                na[3](act)
                na[5](act)
                nb_[1](act)
                nb_[3](act)
                nb_[5](act)

            def dve11(dve):
                wn = wnmax.rearrange("p (a b) -> p a b", b=NQ2)
                wd = wden.rearrange("p (a b) -> p a b", b=NQ2)
                dve.tensor_tensor(se, wn, S("sinks").unsqueeze(1).to_broadcast([P, TT, NQ2]), ALU.add).then_inc(g_e, 1)
                dve.wait_ge(g_x, 1)
                v = note("dve", dve.tensor_tensor(rd, se, wd, ALU.add))
                dve.wait_ge(dve_step, v)
                v = note("dve", dve.reciprocal(rd, rd))
                dve.wait_ge(dve_step, v)
                for i in range(TT):
                    o = o10[:, i, :].rearrange("p (h d) -> p h d", d=DH)
                    dve.tensor_tensor(o, o, rd[:, i, :].unsqueeze(2).to_broadcast([P, NQ2, DH]),
                                      ALU.mult).then_inc(g_o, 1)
                for u in range(4):
                    dve.wait_ge(g_t, u + 1)
                    dve.tensor_copy(at11[:, u, :], ps[:, u % 4, :]).then_inc(g_a, 1)
                dve.wait_ge(g_a, 4)
                na[0](dve)
                na[4](dve)
                na[6].wait(dve, 4)
                nb_[0](dve)
                nb_[4](dve)

            def pe11(pe):
                pe.wait_ge(g_o, 4)
                transposes(pe, o10, 4, g_a, g_t)
                na[2](pe)
                nb_[2](pe)
                na[7].wait(pe, 4)
            out_projection("g", block, PIECE_AT["out2"][0], nb_[7], mod[:, 64:72], dve11, pe11, act11, n_ready=4)
        if until < 12:
            drain()
            return

        n3 = norm_parts("n3", xT, ntmp, nsq, KD, 6, amp[:, 3, :], mod[:, 72:80], h_parts)
        qp = area(0, 16, T)
        scs = area(8192, TT * 16, PK)
        order12 = ["act", "dve"] * 16
        ev12 = {"act": sem("ev12_act"), "dve": sem("ev12_dve")}
        left12 = evacuated(order12, ev12)
        k_sum = sem("k_sum")
        base12, sub12 = PIECE_AT["wq"][0], PIECE_AT["subkeys"][0]
        scv = scs.rearrange("p (s q) k -> p s (q k)", q=4)
        with phase() as block:
            @block.sync
            def _(sp):
                ask_pieces(sp, N_PIECES)

            @block.tensor
            def _(pe):
                n3[2](pe)
                n3[7].wait(pe, KD)
                for u in range(16):
                    if u >= 4:
                        left12(pe, u - 4)
                    feature_unit(pe, base12 + u, u % 4, h_parts)
                for u in range(16, 32):
                    left12(pe, u - 4)
                    s, i, q = (u - 16) // 8, (u - 16) // 2 % 4, u % 2
                    if u == 16:
                        left12(pe, 15)
                        left12(pe, 14)
                    if (u - 16) % 8 == 0:
                        w = piece_ready(pe, sub12 + s)
                    for j in range(4):
                        mm = pe.matmul(ps[:, u % 4, j * P:(j + 1) * P], qp[:, s * 8 + q * 4 + j, tile_tokens(i)],
                                       w[:, (q * 4 + j) * P:(q * 4 + j + 1) * P], start=True, stop=True)
                    mm.then_inc(k_sum, 1)

            def out12(eng, who, u):
                if u < 16:
                    eng.wait_ge(piece_used, base12 + u + 1)
                    dst = qp[:, u, :]
                else:
                    eng.wait_ge(k_sum, u - 15)
                    s, i, q = (u - 16) // 8, (u - 16) // 2 % 4, u % 2
                    dst = scv[:, i * 4 + s * 2 + q, :]
                if who == "act":
                    eng.activation(dst, ps[:, u % 4, :], ACT.Copy).then_inc(ev12["act"], 1)
                else:
                    eng.tensor_copy(dst, ps[:, u % 4, :]).then_inc(ev12["dve"], 1)

            @block.scalar
            def _(act):
                split_hi(act, base12)
                split_hi(act, base12 + 1)
                n3[1](act)
                n3[3](act)
                n3[5](act)
                for u in range(32):
                    if u + 2 < 16:
                        split_hi(act, base12 + u + 2)
                    if u % 2 == 0:
                        out12(act, "act", u)

            @block.gpsimd
            def _(pool):
                for u in range(16):
                    split_lo(pool, base12 + u)

            @block.vector
            def _(dve):
                n3[0](dve)
                n3[4](dve)
                for u in range(1, 32, 2):
                    out12(dve, "dve", u)
        if until < 13:
            drain()
            return

        rep = area(0, 16, PK)
        cand = area(2048, PH, PTOP * PTOP)
        rep2 = area(4096, PH, PTOP * PTOP)
        eq = rep2.rearrange("p h (k a) -> p h k a", a=PTOP)
        prod = area(16384, PH, PTOP * PTOP).rearrange("p h (k a) -> p h k a", a=PTOP)
        vals = area(18432, 16, PTOP)
        ids_u = area(18688, 16, PTOP).bitcast(U32)
        ids_f = area(18944, 16, PTOP)
        top = area(19200, PH, PTOP)
        pos_u = area(19328, PH, PTOP).bitcast(U32)
        posab = area(19456, 2, P)
        posab_u = area(19712, 2, P).bitcast(U32)
        sel = area(19968, 3, P)
        gsum = area(20352, PH)
        selT = area(20480, 3, T)
        t_cand, t_vals, t_top, t_gate, t_sel, t_tr, t_read = (
            sem("t_" + n) for n in "cand vals top gate sel tr read".split())
        ids3 = ids_f.rearrange("p (h two) k -> p h two k", two=2)
        val3 = vals.rearrange("p (h two) k -> p h two k", two=2)
        with phase() as block:
            @block.gpsimd
            def _(pool):
                for i in range(TT):
                    pool.wait_ge(t_vals, i + 1)
                    if i >= 1:
                        pool.wait_ge(t_sel, i)
                    pool.tensor_tensor(cand.rearrange("p h (a b) -> p h a b", b=PTOP),
                                       val3[:, :, 0, :].unsqueeze(3).to_broadcast([P, PH, PTOP, PTOP]),
                                       val3[:, :, 1, :].unsqueeze(2).to_broadcast([P, PH, PTOP, PTOP]),
                                       ALU.add).then_inc(t_cand, 1)

            @block.scalar
            def _(act):
                for i in range(TT):
                    act.wait_ge(t_top, i + 1)
                    act.activation(top, top, ACT.Exp).then_inc(t_gate, 1)
                    act.wait_ge(t_tr, i + 1)
                    act.activation(selT[:, :, tile_tokens(i)],
                                   ps[:, i % 2, 0:3 * P].rearrange("p (a b) -> p a b", b=P),
                                   ACT.Copy).then_inc(t_read, 1)

            @block.tensor
            def _(pe):
                for i in range(TT):
                    pe.wait_ge(t_sel, i + 1)
                    if i >= 2:
                        pe.wait_ge(t_read, i - 1)
                    for j in range(3):
                        mm = pe.transpose(ps[:, i % 2, j * P:(j + 1) * P], sel[:, j, :], ident)
                    mm.then_inc(t_tr, 1)

            @block.vector
            def _(dve):
                def step(ins):
                    dve.wait_ge(dve_step, note("dve", ins))

                def top16(src, scratch, values, index, n):
                    for j in range(n):
                        v = note("dve", dve.max(values[:, j, 0:8], src[:, j, :]))
                    dve.wait_ge(dve_step, v)
                    for j in range(n):
                        note("dve", dve.max_index(index[:, j, 0:8], values[:, j, 0:8], src[:, j, :]))
                        v = note("dve", dve.match_replace(scratch[:, j, :], values[:, j, 0:8], src[:, j, :], -3e38))
                    dve.wait_ge(dve_step, v)
                    for j in range(n):
                        v = note("dve", dve.max(values[:, j, 8:16], scratch[:, j, :]))
                    dve.wait_ge(dve_step, v)
                    for j in range(n):
                        v = note("dve", dve.max_index(index[:, j, 8:16], values[:, j, 8:16], scratch[:, j, :]))
                    dve.wait_ge(dve_step, v)

                for i in range(TT):
                    if i >= 1:
                        dve.wait_ge(t_cand, i)
                    top16(scs[:, i * 16:(i + 1) * 16, :], rep, vals, ids_u, 16)
                    dve.tensor_copy(ids_f, ids_u).then_inc(t_vals, 1)
                    dve.wait_ge(t_vals, i + 1)
                    dve.wait_ge(t_cand, i + 1)
                    top16(cand, rep2, top, pos_u, PH)
                    step(dve.tensor_copy(gsum, top[:, :, 0]))
                    dve.tensor_tensor(top, top, gsum.unsqueeze(2).to_broadcast([P, PH, PTOP]),
                                      ALU.subtract).then_inc(t_top, 1)
                    flat = pos_u.rearrange("p h k -> p (h k)")
                    note("dve", dve.tensor_scalar(posab_u[:, 0, :], flat, 4, None, ALU.logical_shift_right))
                    step(dve.tensor_scalar(posab_u[:, 1, :], flat, 15, None, ALU.bitwise_and))
                    step(dve.tensor_copy(posab, posab_u))
                    if i >= 1:
                        dve.wait_ge(t_tr, i)
                    for j in range(2):
                        step(dve.tensor_tensor(
                            eq.rearrange("p h k a -> p (h k) a"),
                            posab[:, j, :].unsqueeze(2).to_broadcast([P, P, PTOP]),
                            C("iota16").unsqueeze(1).to_broadcast([P, P, PTOP]), ALU.is_equal))
                        step(dve.tensor_tensor(
                            prod, eq, ids3[:, :, j, :].unsqueeze(2).to_broadcast([P, PH, PTOP, PTOP]), ALU.mult))
                        step(dve.tensor_reduce(sel[:, j, :], prod.rearrange("p h k a -> p (h k) a"), AX.X, ALU.add))
                    dve.wait_ge(t_gate, i + 1)
                    step(dve.tensor_reduce(gsum, top, AX.X, ALU.add))
                    step(dve.reciprocal(gsum, gsum))
                    dve.tensor_tensor(sel[:, 2, :].rearrange("p (h k) -> p h k", k=PTOP), top,
                                      gsum.unsqueeze(2).to_broadcast([P, PH, PTOP]), ALU.mult).then_inc(t_sel, 1)
                    dve.wait_ge(t_sel, i + 1)
        if until < 14:
            drain()
            return

        QT, NQ = 4, 4
        stage = area(0, 2, NG * CHUNK * GI)
        hot_a = area(16384, NQ * QT, P)
        hot_b = area(18432, NQ * QT, P)
        a_ready, b_dve, b_pool = sem("a_ready"), sem("b_dve"), sem("b_pool")
        g_done, g_read, keys_here = sem("g_done"), sem("g_read"), sem("keys_here")
        keys_seen = sem("keys_seen")
        keys_q = area(22016, 2, QT)
        stored = [sem("stored0"), sem("stored1")]
        NCH = T // CHUNK
        STEP = NQ * QT
        POOL_QUADS = (0, 2)
        QC = CHUNK // STEP
        with phase() as block:
            @block.vector
            def _(dve):
                with dve.Fori(0, T // STEP) as q:
                    for quad in range(NQ):
                        dve.wait_ge(g_done, q * NQ + (quad + 1))
                        for s in range(QT):
                            slot, t = quad * QT + s, q * STEP + (quad * QT + s)
                            if quad not in POOL_QUADS:
                                dve.tensor_scalar(hot_b[:, slot, :], C("iota"), selT[:, 1, bass.ds(t, 1)], None,
                                                  ALU.is_equal).then_inc(b_dve, 1)
                            dve.tensor_scalar(hot_a[:, slot, :], C("iota"), selT[:, 0, bass.ds(t, 1)],
                                              selT[:, 2, bass.ds(t, 1)], ALU.is_equal, ALU.mult).then_inc(a_ready, 1)

            @block.gpsimd
            def _(pool):
                with pool.Fori(0, T // STEP) as q:
                    for quad in POOL_QUADS:
                        pool.wait_ge(g_done, q * NQ + (quad + 1))
                        pool.tensor_copy(keys_q[:, quad // 2, :],
                                         selT[:, 1, bass.ds(q * STEP + quad * QT, QT)]).then_inc(keys_here, 1)
                        pool.wait_ge(keys_here, q * 2 + (quad // 2 + 1))
                        pool.sem_inc(keys_seen, 1)
                        for s in range(QT):
                            pool.tensor_scalar(hot_b[:, quad * QT + s, :], C("iota"), keys_q[:, quad // 2, s:s + 1],
                                               None, ALU.is_equal).then_inc(b_pool, 1)

            @block.tensor
            def _(pe):
                pe.sem_inc(g_done, NQ)
                with pe.Fori(0, T // STEP) as q:
                    for quad in range(NQ):
                        if quad in POOL_QUADS:
                            pe.wait_ge(b_pool, q * (2 * QT) + (quad // 2 + 1) * QT)
                        else:
                            pe.wait_ge(b_dve, q * (2 * QT) + (quad // 2 + 1) * QT)
                        pe.wait_ge(a_ready, q * STEP + (quad + 1) * QT)
                        pe.wait_ge(g_read, q * NQ + (quad + 1))
                        for s in range(QT):
                            mm = pe.matmul(ps[:, quad, s * P:(s + 1) * P], hot_b[:, quad * QT + s, :],
                                           hot_a[:, quad * QT + s, :], start=True, stop=True)
                        mm.then_inc(g_done, 1)

            @block.scalar
            def _(act):
                act.sem_inc(g_read, NQ)
                for ch in range(NCH):
                    if ch >= 2:
                        act.wait_ge(stored[ch % 2], 16 * (ch // 2))
                    sv = stage[:, ch % 2, :].rearrange("p (g t i) -> p t g i", t=CHUNK, i=GI)
                    with act.Fori(0, QC) as q:
                        for quad in range(NQ):
                            act.wait_ge(g_done, q * NQ + (ch * QC * NQ + quad + 1 + NQ))
                            act.activation(sv[:, bass.ds(q * STEP + quad * QT, QT), :, :],
                                           ps[:, quad, :].rearrange("p (t g i) -> p t g i", t=QT, i=GI),
                                           ACT.Copy).then_inc(g_read, 1)

            @block.sync
            def _(sp):
                for ch in range(NCH):
                    sp.wait_ge(g_read, NQ + (ch + 1) * QC * NQ)
                    sp.dma_start(gates_dram[:, :, ch * CHUNK * GI:(ch + 1) * CHUNK * GI].rearrange("g p n -> p g n"),
                                 stage[:, ch % 2, :].rearrange("p (g n) -> p g n", g=NG)).then_inc(stored[ch % 2], 16)
                for i in range(2):
                    sp.wait_ge(stored[i], 16 * (NCH // 2))
        if until < 15:
            drain()
            return

        UB = 2
        WS = GI + 1
        at = 0
        acc = place("acc", at, [KD, T]); at += KD * T
        u_raw = place("u_raw", at, [UB, PIECE]); at += UB * PIECE
        v_raw = place("v_raw", at, [GI, PIECE]); at += GI * PIECE
        gbuf = place("gbuf", at, [2, GI * T]); at += 2 * GI * T
        gel = place("gel", WR_AT + GI * 2 * PIECE, [2, T])
        u_split = place("u_split", at, [UB, 2, PIECE], F32R); at += UB * 2 * PIECE
        wgt = place("wgt", at, [WS, 2, T], F32R); at += WS * 2 * T
        assert at <= HR_AT
        v_split = place("v_split", WR_AT, [GI, 2, PIECE], F32R)
        ug = u_in.rearrange("(g i) p n -> g i p n", i=GI)
        vg = v_in.rearrange("(g i p) d -> g p i d", i=GI, p=P)
        gview = gbuf.rearrange("p b (t i) -> p b i t", i=GI)
        u_landed = [sem(f"u_landed{i}") for i in range(UB)]
        v_landed = sem("v_landed")
        g_landed = [sem(f"g_landed{i}") for i in range(2)]
        u_hi, u_lo, v_hi, v_lo = sem("u_hi"), sem("u_lo"), sem("v_hi"), sem("v_lo")
        a_sum, gelus = sem("a_sum"), sem("gelus")
        y_sum, y_added, acc_zero, x_final = sem("y_sum"), sem("y_added"), sem("acc_zero"), sem("x_final")
        gated, w_done = sem("gated"), sem("w_done")
        out_stored = sem("out_stored")
        A0, UL0, VL0, GE0, W0, Y0, B0 = UB, UB, GI, 2, 2 * GI, KD, 4

        with phase() as block:
            @block.sync
            def _(sp):
                with sp.Fori(0, NG // 2) as pair:
                    for b in range(2):
                        g = pair * 2 + b
                        sp.wait_ge(w_done, g * GI + GI)
                        sp.dma_start(gbuf[:, b, :], gates_dram[g]).then_inc(g_landed[b], 16)
                        for i in range(GI):
                            sp.wait_ge(u_lo, g * GI + (i + 1))
                            sp.dma_start(u_raw[:, i % UB, :], ug[g, i]).then_inc(u_landed[i % UB], 16)
                            if i == 1:
                                sp.wait_ge(v_lo, g * GI + GI)
                                sp.dma_start(v_raw[:, :, :], vg[g]).then_inc(v_landed, 16)
                for i in range(2):
                    sp.wait_ge(x_final, (i + 1) * (KD // 2))
                    sp.dma_start(out[:, i * (KD // 2):(i + 1) * (KD // 2), :],
                                 xT[:, i * (KD // 2):(i + 1) * (KD // 2), :]).then_inc(out_stored, 16)
                sp.wait_ge(out_stored, 32)

            @block.tensor
            def _(pe):
                def first(i, g):
                    pe.wait_ge(u_lo, g * GI + (i + 1 + UL0))
                    pe.wait_ge(gelus, g * GI + (i + 1))
                    for k in range(KD):
                        for a, b in HI_LO:
                            mm = pe.matmul(ps[:, i % 2, :], u_split[:, i % UB, a, k * P:(k + 1) * P],
                                           h_parts[b][:, k, :], start=(k + a + b == 0),
                                           stop=(k == KD - 1 and a == 1))
                    mm.then_inc(a_sum, 1)

                def slot(i, g_parity):
                    return i if i else (0, GI)[g_parity]

                def second(g, parity):
                    pe.wait_ge(v_lo, g * GI + (GI + VL0))
                    pe.wait_ge(w_done, g * GI + (GI + W0))
                    for j in range(KD):
                        pe.wait_ge(y_added, g * KD + (j + 1))
                        for i in range(GI):
                            for a, b in HI_LO:
                                mm = pe.matmul(ps[:, 2 + j % 4, :], v_split[:, i, a, j * P:(j + 1) * P],
                                               wgt[:, slot(i, parity), b, :], start=(i + a + b == 0),
                                               stop=(i == GI - 1 and a == 1))
                        mm.then_inc(y_sum, 1)

                pe.sem_inc(a_sum, A0)
                pe.sem_inc(y_sum, Y0)
                first(0, 0)
                for i in range(1, GI):
                    first(i, 0)
                with pe.Fori(0, NG // 2 - 1) as pair:
                    for b in range(2):
                        g = pair * 2 + b
                        first(0, g + 1)
                        second(g, b)
                        for i in range(1, GI):
                            first(i, g + 1)
                first(0, NG - 1)
                second(NG - 2, 0)
                for i in range(1, GI):
                    first(i, NG - 1)
                second(NG - 1, 1)

            @block.scalar
            def _(act):
                def u_upper(i, g):
                    buf = i % UB
                    act.wait_ge(u_landed[buf], g * (16 * GI // UB) + 16 * (i // UB + 1))
                    act.wait_ge(a_sum, g * GI + (i + 1))
                    act.activation(u_split[:, buf, 0, :], u_raw[:, buf, :], ACT.Copy).then_inc(u_hi, 1)

                def v_upper(i, g):
                    if i == 0:
                        act.wait_ge(v_landed, g * 16 + 16)
                        act.wait_ge(y_sum, g * KD + KD)
                    act.activation(v_split[:, i, 0, :], v_raw[:, i, :], ACT.Copy).then_inc(v_hi, 1)

                def gelu(i, g):
                    act.wait_ge(a_sum, g * GI + (i + 1 + A0))
                    act.wait_ge(w_done, g * GI + (i + 1 + W0 - 2))
                    act.activation(gel[:, i % 2, :], ps[:, i % 2, :], ACT.Gelu_apprx_tanh).then_inc(gelus, 1)

                act.sem_inc(gelus, GE0)
                u_upper(0, 0)
                u_upper(1, 0)
                with act.Fori(0, NG - 1) as g:
                    gelu(0, g)
                    u_upper(2, g)
                    v_upper(0, g)
                    v_upper(1, g)
                    gelu(1, g)
                    u_upper(3, g)
                    v_upper(2, g)
                    v_upper(3, g)
                    gelu(2, g)
                    u_upper(0, g + 1)
                    gelu(3, g)
                    u_upper(1, g + 1)
                g = NG - 1
                gelu(0, g)
                u_upper(2, g)
                v_upper(0, g)
                v_upper(1, g)
                gelu(1, g)
                u_upper(3, g)
                v_upper(2, g)
                v_upper(3, g)
                gelu(2, g)
                gelu(3, g)

            @block.gpsimd
            def _(pool):
                def u_lower(i, g):
                    buf = i % UB
                    pool.wait_ge(u_hi, g * GI + (i + 1))
                    pool.tensor_tensor(u_split[:, buf, 1, :], u_raw[:, buf, :], u_split[:, buf, 0, :].bitcast(F32),
                                       ALU.subtract).then_inc(u_lo, 1)

                def v_lower(i, g):
                    pool.wait_ge(v_hi, g * GI + (i + 1))
                    pool.tensor_tensor(v_split[:, i, 1, :], v_raw[:, i, :], v_split[:, i, 0, :].bitcast(F32),
                                       ALU.subtract).then_inc(v_lo, 1)

                pool.memset(acc[:, :, :], 0.0).then_inc(acc_zero, 1)
                pool.sem_inc(u_lo, UL0)
                pool.sem_inc(v_lo, VL0)
                u_lower(0, 0)
                u_lower(1, 0)
                with pool.Fori(0, NG - 1) as g:
                    u_lower(2, g)
                    v_lower(0, g)
                    v_lower(1, g)
                    u_lower(3, g)
                    v_lower(2, g)
                    v_lower(3, g)
                    u_lower(0, g + 1)
                    u_lower(1, g + 1)
                g = NG - 1
                u_lower(2, g)
                v_lower(0, g)
                v_lower(1, g)
                u_lower(3, g)
                v_lower(2, g)
                v_lower(3, g)

            @block.vector
            def _(dve):
                def weights(i, g, parity):
                    if i == 0:
                        dve.wait_ge(g_landed[parity], g * 8 + (16 - 8 * parity))
                    s = i if i else (0, GI)[parity]
                    dve.wait_ge(gelus, g * GI + (i + 1 + GE0))
                    dve.tensor_tensor(gel[:, i % 2, :], gel[:, i % 2, :], gview[:, parity, i, :],
                                      ALU.mult).then_inc(gated, 1)
                    dve.wait_ge(gated, g * (2 * GI) + (2 * i + 1))
                    if i == 1:
                        dve.wait_ge(y_sum, g * KD + KD)
                    dve.tensor_copy(wgt[:, s, 0, :], gel[:, i % 2, :]).then_inc(gated, 1)
                    dve.wait_ge(gated, g * (2 * GI) + (2 * i + 2))
                    dve.tensor_tensor(wgt[:, s, 1, :], gel[:, i % 2, :], wgt[:, s, 0, :].bitcast(F32),
                                      ALU.subtract).then_inc(w_done, 1)

                def adds(g):
                    for j in range(KD):
                        dve.wait_ge(y_sum, g * KD + (j + 1 + Y0))
                        dve.wait_ge(y_added, g * KD + (j + 2))
                        dve.tensor_tensor(acc[:, j, :], ps[:, 2 + j % 4, :], acc[:, j, :],
                                          ALU.add).then_inc(y_added, 1)

                dve.sem_inc(w_done, W0)
                dve.sem_inc(y_added, B0)
                dve.wait_ge(acc_zero, 1)
                for i in range(GI):
                    weights(i, 0, 0)
                with dve.Fori(0, NG // 2 - 1) as pair:
                    for b in range(2):
                        g = pair * 2 + b
                        weights(0, g + 1, 1 - b)
                        adds(g)
                        for i in range(1, GI):
                            weights(i, g + 1, 1 - b)
                weights(0, NG - 1, 1)
                adds(NG - 2)
                for i in range(1, GI):
                    weights(i, NG - 1, 1)
                adds(NG - 1)
                for j in range(KD):
                    dve.wait_ge(y_added, B0 + (NG - 1) * KD + j + 1)
                    dve.scalar_tensor_tensor(out=xT[:, j, :], in0=acc[:, j, :], scalar=mod[:, 88 + j:89 + j],
                                             in1=xT[:, j, :], op0=ALU.mult, op1=ALU.add).then_inc(x_final, 1)


def pieces_of(w):
    n = w.shape[1] // P
    return w.reshape(KD, P, n, P).transpose(2, 1, 0, 3).reshape(n, P, PIECE)


def columns(v):
    return v.reshape(-1, P).T


def constants():
    c = np.zeros((P, CONST_W), np.float32)

    def put(name, a):
        lo, hi = CONST_AT[name]
        c[:, lo:hi] = a.reshape(P, hi - lo)

    p = np.arange(P)
    put("ident", np.eye(P))
    put("ones", np.ones((P, P)))
    put("bones", (p[:, None] // DH == p[None, :] // DH).astype(np.float32))
    rot = np.zeros((P, P))
    for m in range(P):
        if m % DH < HALF:
            rot[m + HALF, m] = -1.0
        else:
            rot[m - HALF, m] = 1.0
    put("rot", rot)
    inv = np.float32(10000.0) ** (-np.arange(HALF, dtype=np.float32) / np.float32(HALF))
    inv = inv.astype(np.float32)[p % HALF]
    angle = (np.arange(T, dtype=np.float32)[None, :] * inv[:, None]).astype(np.float64)
    put("cos", np.cos(angle))
    put("sin", np.sin(angle))
    put("invf", inv)
    u = np.arange(T)
    put("causal", np.where(u[None, :] - (T - P) <= p[:, None], 0.0, -BIG))
    d = p[:, None] - p[None, :]
    put("causal16", np.where((d >= 0) & (d % 4 == 0), 0.0, -BIG))
    dist = p[:, None] + P - np.arange(2 * P)[None, :]
    put("band129", np.where((dist >= 0) & (dist <= 128), 0.0, -BIG))
    put("band128", np.where((dist >= 0) & (dist < 128), 0.0, -BIG))
    t = np.arange(TT)[None, :, None] * P + p[:, None, None]
    n = np.arange(CMP_PAD)[None, None, :]
    put("mcmp", np.where((n * SPAN + 2 * SPAN - 1 <= t) & (n < N_CMP), 0.0, -BIG))
    put("valid", (t[:, :, 0] >= 2 * SPAN - 1).astype(np.float32))
    put("iota", np.tile(p, (P, 1)))
    put("iota16", np.tile(np.arange(PTOP), (P, 1)))
    return c


def small_arrays(x):
    s = np.zeros((P, SMALL_W), np.float32)

    def put(name, a):
        lo, hi = SMALL_AT[name]
        s[:, lo:hi] = a.reshape(P, hi - lo)

    put("c", columns(x["c"][0]))
    put("c2", columns(x["c_2"][0]))
    put("ng0", columns(x["norm_g"][0]))
    put("ng1", columns(x["norm_g"][1]))
    put("fg", columns(x["final_g"]))
    put("n1g", columns(x["norm1_g_2"][0]))
    put("n2g", columns(x["norm2_g_2"][0]))
    put("adab", columns(np.concatenate([x["ada_b"][0], x["ada_b"][1], x["ada_b_2"][0]])))
    put("qg", np.tile(x["q_norm_g_2"][0], 2))
    put("kg", np.tile(x["k_norm_g_2"][0], 2))
    put("aog", columns(x["attn_out_g_2"][0]))
    put("cog", columns(x["conv_out_g_2"][0]))
    put("convw", x["conv_w_2"][0].reshape(3, 4, P).transpose(2, 0, 1))
    put("sinks", np.tile(x["sinks_2"][0], (P, 1)))
    put("pek", x["nsa_pe_k"][0].reshape(16, P).T)
    put("pev", x["nsa_pe_v"][0].reshape(16, P).T)
    put("w2k", x["nsa_ck_w2"][0].reshape(2, P, DH).transpose(1, 0, 2))
    put("w2v", x["nsa_cv_w2"][0].reshape(2, P, DH).transpose(1, 0, 2))
    return s


def weight_stream(x):
    w = np.zeros((N_PIECES, P, PIECE), np.float32)

    def put(name, a):
        lo, hi = PIECE_AT[name]
        w[lo:hi] = a

    def pairs(m, heads):
        return m.reshape(D, 2, heads // 2, DH).transpose(0, 2, 1, 3).reshape(D, heads * DH)

    n = x["nsa_w_in"][0]
    kc, vc, ks, vs_, kw, vw_ = (n[:, D + i * P:D + (i + 1) * P] for i in range(6))
    put("ada0", pieces_of(x["ada_w"][0]))
    put("cmp_in", pieces_of(np.concatenate([kc, vc], 1)))
    put("ksw", pieces_of(np.concatenate([ks, kw], 1)))
    put("q", pieces_of(pairs(n[:, :D], NH)))
    put("cmp_w1", np.concatenate([x[k][0].reshape(4, 4, P, CMP_H).transpose(0, 2, 1, 3).reshape(4, P, PIECE)
                                  for k in ("nsa_ck_w1", "nsa_cv_w1")]))
    gates = np.zeros((D, P), np.float32)
    gates[:, :3 * NH] = n[:, 2 * D + 6 * P:]
    put("vsw", pieces_of(np.concatenate([vs_, vw_, gates], 1)))
    put("z", pieces_of(n[:, D + 6 * P:2 * D + 6 * P]))
    put("ada12", np.concatenate([x["ada_w"][1], x["ada_w_2"][0]], 1).reshape(KD, P, 9, PIECE)
        .transpose(2, 0, 1, 3).reshape(72, P, PIECE))
    put("nsa_out", pieces_of(x["nsa_w_out"][0]))
    d = x["dil_w_in"][0]
    for i, name in enumerate(("dq", "dk", "dv", "dz")):
        put(name, pieces_of(d[:, i * D:(i + 1) * D]))
    put("dil_out", pieces_of(x["dil_w_out"][0]))
    m = x["w_in_2"][0]
    put("q2", pieces_of(pairs(m[:, :512], NQ2)))
    put("k2", pieces_of(m[:, 512:640]))
    put("v2", pieces_of(m[:, 640:768]))
    for i, name in enumerate(("cb", "cc", "cu")):
        put(name, pieces_of(m[:, 768 + 512 * i:1280 + 512 * i]))
    put("out2", pieces_of(x["w_out_2"][0]))
    put("wq", pieces_of(x["peer_wq_2"][0]))
    put("subkeys", x["peer_subkeys_2"][0].reshape(2, 8, P, P).transpose(0, 3, 1, 2).reshape(2, P, PIECE))
    return w


def kernel(**inputs):
    import concourse.bacc as _bacc
    from concourse.bass_utils import run_bass_kernel_spmd as _run

    x = {k: np.asarray(v) for k, v in inputs.items()}
    nc = _bacc.Bacc("TRN2", target_bir_lowering=False, num_devices=1)
    arrays = {
        "w_stream": weight_stream(x),
        "consts": constants(),
        "small": small_arrays(x),
        "x_in": np.ascontiguousarray(x["x"][0].reshape(T, KD, P).transpose(2, 1, 0)),
        "positions": np.ascontiguousarray(x["positions_2"][0]),
        "u_table": np.ascontiguousarray(x["peer_u_2"][0].reshape(PK, PK, KD, P).transpose(0, 3, 2, 1)
                                        .reshape(PK, P, PIECE)),
        "v_table": np.ascontiguousarray(x["peer_v_2"][0]),
    }
    aps = [nc.dram_tensor(name, a.shape, mybir.dt.from_np(a.dtype), kind="ExternalInput").ap()
           for name, a in arrays.items()]
    out = nc.dram_tensor("out_t", (P, KD, T), F32, kind="ExternalOutput").ap()
    gates = nc.dram_tensor("gates_scratch", (NG, P, GI * T), F32).ap()
    build(nc, *aps, out, gates)
    r = _run(nc, [arrays], core_ids=[0])
    return np.ascontiguousarray(r.results[0]["out_t"].transpose(2, 1, 0)).reshape(1, T, D)
```

```python
import math
from contextlib import ExitStack

import numpy as np

import concourse.bass as bass
from concourse import mybir

F32 = mybir.dt.float32
F32R = mybir.dt.float32r
U32 = mybir.dt.uint32
I32 = mybir.dt.int32
ALU = mybir.AluOpType
ACT = mybir.ActivationFunctionType
AX = mybir.AxisListType

P = 128
T = 512
D = 1024
TT = T // P
KD = D // P
DH = 64
HALF = DH // 2
NH = 16
NQ2, NKV2 = 8, 2
SCALE = DH ** -0.5
EPS = 1e-6
BIG = 1e30
N_CMP, CMP_PAD = 31, 32
CMP_H = 256
SPAN = 16
PH, PK, PTOP = 8, 128, 16
DIL_GROUPS = ((0, 6), (6, 11), (11, 16))

R = 4
RS = 3
PIECE = KD * P
GI = 4
NG = PK // GI
CHUNK = 64
EARLY_TOP = 10
EARLY_GATES = T // CHUNK * 2
EARLY = TT * EARLY_TOP + EARLY_GATES

CONST = dict(ident=P, ones=P, rot=P, bones=P, cos=T, sin=T, causal=T, causal16=P,
             band129=2 * P, band128=2 * P, mcmp=TT * CMP_PAD, iota=P, iota16=PTOP,
             valid=TT, invf=1)
SMALL = dict(c=KD, c2=KD, ng0=KD, ng1=KD, fg=KD, n1g=KD, n2g=KD, adab=96, qg=1, kg=1,
             aog=4, cog=4, convw=12, sinks=NQ2, pek=16, pev=16, w2k=2 * DH, w2v=2 * DH)


def offsets(widths):
    at, out = 0, {}
    for name, w in widths.items():
        out[name] = (at, at + w)
        at += w
    return out, at


CONST_AT, CONST_W = offsets(CONST)
SMALL_AT, SMALL_W = offsets(SMALL)

STREAM = [("ada0", 24), ("cmp_in", 2), ("ksw", 2), ("q", 8), ("cmp_w1", 8), ("vsw", 3), ("z", 8),
          ("ada12", 72), ("nsa_out", 8), ("dq", 8), ("dk", 8), ("dv", 8), ("dz", 8), ("dil_out", 8),
          ("q2", 4), ("k2", 1), ("v2", 1), ("cc", 4), ("cu", 4), ("cb", 4), ("out2", 8),
          ("wq", 16), ("subkeys", 2)]
PIECE_AT, N_PIECES = offsets(dict(STREAM))


RAW = ("ada0", "ada12", "cmp_w1", "subkeys")


def build(nc, w_stream, consts_in, small_in, x_in, pos_in, u_in, v_in, out, gates_dram, gelu_dram):
    ctx = ExitStack()
    with ctx:
        def sb(name, shape, dt=F32):
            return ctx.enter_context(nc.sbuf_tensor(name, shape, dt))

        def sem(name):
            return ctx.enter_context(nc.semaphore(name))

        ps = ctx.enter_context(nc.psum_tensor("ps", [P, 8, 512], F32))
        cst = sb("cst", [P, CONST_W])
        sml = sb("sml", [P, SMALL_W])
        xT = sb("xT", [P, KD, T])
        rope2 = sb("rope2", [P, 2, T])
        mod = sb("mod", [P, 96])
        amp = sb("amp", [P, 4, KD])
        csil = sb("csil", [P, 2, KD])
        rstd = sb("rstd", [P, T])
        sdev = sb("sdev", [P, T])
        var = sb("var", [P, T])
        ARENA = 24320
        HR_AT, WR_AT = ARENA, ARENA + 2 * KD * T
        RING_AT = WR_AT + RS * 2 * PIECE
        SLAB = RING_AT + R * PIECE
        sb("slab", [P, SLAB])
        slab_at = nc.sbuf_base - 4 * SLAB

        def place(name, at, shape, dt=F32):
            assert at + math.prod(shape) <= SLAB, (name, at, shape)
            return nc.alloc_sbuf_tensor_at(name, [P] + list(shape), dt, offset=slab_at + 4 * at)

        arena = place("arena", 0, [ARENA])
        h_hi = place("h_hi", HR_AT, [KD, T], F32R)
        h_lo = place("h_lo", HR_AT + KD * T, [KD, T], F32R)
        w_split = place("w_split", WR_AT, [RS, 2, PIECE], F32R)
        ring = place("ring", RING_AT, [R, PIECE])

        def C(name):
            a, b = CONST_AT[name]
            return cst[:, a:b]

        def S(name):
            a, b = SMALL_AT[name]
            return sml[:, a:b]

        def area(at, *shape):
            n = math.prod(shape)
            assert at + n <= ARENA, (at, shape)
            v = arena[:, at:at + n]
            if len(shape) == 2:
                v = v.rearrange("p (a b) -> p a b", b=shape[1])
            elif len(shape) == 3:
                v = v.rearrange("p (a b c) -> p a b c", b=shape[1], c=shape[2])
            return v

        ident = C("ident")

        const_in = sem("const_in")
        x_loaded = sem("x_loaded")
        piece_in = [sem(f"piece_in{i}") for i in range(R)]
        piece_used = sem("piece_used")
        dve_step = sem("dve_step")
        act_step = sem("act_step")
        pool_step = sem("pool_step")
        counts = {"dve": 0, "act": 0, "pool": 0}
        step_sem = {"dve": dve_step, "act": act_step, "pool": pool_step}

        def note(who, ins, n=1):
            ins.then_inc(step_sem[who], 1)
            counts[who] += 1
            return counts[who]

        class Work:
            asked = 0
            used = 0
            hi = 0
            lo = 0

        split_of, n_split = {}, 0
        for name, _ in STREAM:
            for n in range(*PIECE_AT[name]):
                if name not in RAW:
                    split_of[n] = n_split
                    n_split += 1
        split_list = sorted(split_of)
        raw_used = {}
        hi_done, lo_done = sem("hi_done"), sem("lo_done")
        ADA0, ADA12 = PIECE_AT["ada0"], PIECE_AT["ada12"]
        ada_place = {n: i for i, n in enumerate([*range(*ADA0), *range(*ADA12)])}
        ada_used = sem("ada_used")
        ada_taken = sem("ada_taken")

        def ask_pieces(sp, upto):
            while Work.asked < min(upto, N_PIECES):
                n = Work.asked
                if n >= R:
                    m = n - R
                    if m in split_of:
                        sp.wait_ge(lo_done, split_of[m] + 1)
                    elif m in ada_place:
                        sp.wait_ge(ada_used, ada_place[m] + 1)
                    else:
                        sp.wait_ge(piece_used, m + 1)
                sp.dma_start(ring[:, n % R, :], w_stream[n]).then_inc(piece_in[n % R], 16)
                Work.asked += 1

        def split_hi(act, n):
            i = split_of[n]
            assert i == Work.hi
            Work.hi += 1
            act.wait_ge(piece_in[n % R], 16 * (n // R + 1))
            if i >= RS:
                act.wait_ge(piece_used, split_list[i - RS] + 1)
            act.activation(w_split[:, i % RS, 0, :], ring[:, n % R, :], ACT.Copy).then_inc(hi_done, 1)

        def split_lo(pool, n):
            i = split_of[n]
            assert i == Work.lo
            Work.lo += 1
            pool.wait_ge(hi_done, i + 1)
            pool.tensor_tensor(w_split[:, i % RS, 1, :], ring[:, n % R, :],
                               w_split[:, i % RS, 0, :].bitcast(F32), ALU.subtract).then_inc(lo_done, 1)

        def piece_ready(pe, n):
            assert n == Work.used, (n, Work.used)
            Work.used += 1
            if n in split_of:
                pe.wait_ge(lo_done, split_of[n] + 1)
                return w_split[:, split_of[n] % RS, :, :]
            pe.wait_ge(piece_in[n % R], 16 * (n // R + 1))
            return ring[:, n % R, :]

        HI_LO = ((0, 0), (0, 1), (1, 0))

        def feature_unit(pe, n, bank, src, src_ready=None):
            w = piece_ready(pe, n)
            for k in range(KD):
                if src_ready:
                    src_ready.wait(pe, k + 1)
                for a, b in HI_LO:
                    mm = pe.matmul(ps[:, bank, :], w[:, a, k * P:(k + 1) * P], src[b][:, k, :],
                                   start=(k + a + b == 0), stop=(k == KD - 1 and a == 1))
            mm.then_inc(piece_used, 1)

        def token_unit(pe, n, bank, src, tokens):
            w = piece_ready(pe, n)
            for i in range(TT):
                for k in range(KD):
                    for a, b in HI_LO:
                        mm = pe.matmul(ps[:, bank, i * P:(i + 1) * P], src[b][:, k, tokens(i)],
                                       w[:, a, k * P:(k + 1) * P],
                                       start=(k + a + b == 0), stop=(k == KD - 1 and a == 1))
            mm.then_inc(piece_used, 1)

        def ada_piece(dve, j, sums, which):
            piece, chunk, k = (ADA0[0] + j if j < 24 else ADA12[0] + j - 24), j // KD, j % KD
            total, c = sums[:, chunk % 2, :], csil[:, which, k:k + 1]
            dve.wait_ge(piece_in[piece % R], 16 * (piece // R + 1))
            if k == 0:
                if chunk >= 2:
                    dve.wait_ge(ada_taken, chunk - 1)
                dve.tensor_scalar(total, ring[:, piece % R, :], c, None, ALU.mult).then_inc(ada_used, 1)
            else:
                dve.wait_ge(ada_used, j)
                dve.scalar_tensor_tensor(out=total, in0=ring[:, piece % R, :], scalar=c, in1=total,
                                         op0=ALU.mult, op1=ALU.add).then_inc(ada_used, 1)

        def ada_chunk(pe, chunk, sums, bank):
            pe.wait_ge(ada_used, (chunk + 1) * KD)
            for b in range(KD):
                col = chunk * KD + b
                mm = pe.matmul(ps[:, bank, col:col + 1], sums[:, chunk % 2, b * P:(b + 1) * P],
                               C("ones")[:, 0:1], start=True, stop=True)
            mm.then_inc(ada_taken, 1)

        h_parts = (h_hi, h_lo)

        def tile_tokens(i):
            return slice(i * P, (i + 1) * P)

        def class_tokens(r):
            return slice(r, T, TT)

        def phase():
            return nc.Block()

        class Since:

            def __init__(self, sem, base):
                self.sem, self.base = sem, base

            def wait(self, eng, n):
                eng.wait_ge(self.sem, self.base + n)

        shared = {}

        def since(name, n):
            s, base = shared.get(name) or (sem(name), 0)
            shared[name] = (s, base + n)
            return Since(s, base)

        def norm_parts(tag, src, dst, sq, units, bank, amps, shifts, parts=None):
            half = units // 2
            sq_d, sq_a = since("norm_sq_dve", half), since("norm_sq_act", half)
            summed, varied, rooted = since("norm_summed", 1), since("norm_varied", 1), since("norm_rooted", 1)
            scaled = since("norm_scaled", units)
            upper, done = since("norm_hi", units if parts else 0), since("norm_done", units if parts else 0)

            def dve_squares(dve):
                for k in range(0, units, 2):
                    dve.tensor_tensor(sq[:, k, :], src[:, k, :], src[:, k, :], ALU.mult).then_inc(sq_d.sem, 1)

            def act_squares(act):
                for k in range(1, units, 2):
                    act.activation(sq[:, k, :], src[:, k, :], ACT.Square).then_inc(sq_a.sem, 1)

            def pe_sum(pe):
                for k in range(units):
                    (sq_a if k % 2 else sq_d).wait(pe, k // 2 + 1)
                    mm = pe.matmul(ps[:, bank, :], C("ones"), sq[:, k, :],
                                   start=(k == 0), stop=(k == units - 1))
                mm.then_inc(summed.sem, 1)

            def act_root(act):
                varied.wait(act, 1)
                act.activation(sdev[:, :], var[:, :], ACT.Sqrt).then_inc(rooted.sem, 1)

            def dve_scale(dve):
                summed.wait(dve, 1)
                dve.tensor_scalar(var[:, :], ps[:, bank, :], 1.0 / (units * P), EPS,
                                  ALU.mult, ALU.add).then_inc(varied.sem, 1)
                rooted.wait(dve, 1)
                inverse_root(dve, var[:, :], sdev[:, :], rstd[:, :])
                for k in range(units):
                    dve.scalar_tensor_tensor(out=dst[:, k, :], in0=src[:, k, :], scalar=amps[:, k:k + 1],
                                             in1=rstd[:, :], op0=ALU.mult, op1=ALU.mult).then_inc(scaled.sem, 1)
                    if parts and k >= 2:
                        lower(dve, k - 2)
                if parts:
                    lower(dve, units - 2)
                    lower(dve, units - 1)

            def lower(dve, k):
                upper.wait(dve, k + 1)
                if shifts is None:
                    ins = dve.tensor_tensor(parts[1][:, k, :], dst[:, k, :], parts[0][:, k, :].bitcast(F32),
                                            ALU.subtract)
                else:
                    ins = dve.scalar_tensor_tensor(out=parts[1][:, k, :], in0=dst[:, k, :],
                                                   scalar=shifts[:, k:k + 1],
                                                   in1=parts[0][:, k, :].bitcast(F32),
                                                   op0=ALU.add, op1=ALU.subtract)
                ins.then_inc(done.sem, 1)

            def act_upper(act):
                for k in range(units):
                    scaled.wait(act, k + 1)
                    if shifts is None:
                        ins = act.activation(parts[0][:, k, :], dst[:, k, :], ACT.Copy)
                    else:
                        ins = act.activation(parts[0][:, k, :], dst[:, k, :], ACT.Identity, bias=shifts[:, k:k + 1])
                    ins.then_inc(upper.sem, 1)

            return dve_squares, act_squares, pe_sum, act_root, dve_scale, act_upper, scaled, done

        def inverse_root(dve, v, root, out_):
            n = note("dve", dve.reciprocal(out_, root))
            dve.wait_ge(dve_step, n)
            n = note("dve", dve.tensor_tensor(v, v, out_, ALU.mult))
            dve.wait_ge(dve_step, n)
            n = note("dve", dve.scalar_tensor_tensor(out=v, in0=v, scalar=-0.5, in1=out_, op0=ALU.mult, op1=ALU.mult))
            dve.wait_ge(dve_step, n)
            n = note("dve", dve.scalar_tensor_tensor(out=out_, in0=v, scalar=1.5, in1=out_, op0=ALU.add, op1=ALU.mult))
            dve.wait_ge(dve_step, n)

        nsq, ntmp = area(0, KD, T), area(KD * T, KD, T)

        n0 = norm_parts("n0", xT, ntmp, nsq, KD, 6, amp[:, 0, :], mod[:, 0:8], h_parts)
        silu_done = sem("silu_done")
        mod0_done = sem("mod0_done")
        wrapped = sem("wrapped")
        pos_loaded = sem("pos_loaded")
        pos_i = area(8192, T).bitcast(I32)
        ang = area(8704, T)
        turns = area(9216, 2, T)
        wrap = area(10240, 2, T)
        TWO_PI = (6.28125, 0.0019350051879882812, 3.019916050561733e-07)
        ada_sum0 = place("ada_sum0", WR_AT, [2, PIECE])
        with phase() as block:
            @block.sync
            def _(sp):
                sp.dma_start(sml[:, :], small_in).then_inc(const_in, 16)
                sp.dma_start(pos_i, pos_in.partition_broadcast(P)).then_inc(pos_loaded, 16)
                sp.dma_start(cst[:, :], consts_in).then_inc(const_in, 16)
                for k in range(0, KD, 4):
                    sp.dma_start(xT[:, k:k + 4, :], x_in[:, k:k + 4, :]).then_inc(x_loaded, 16)
                ask_pieces(sp, PIECE_AT["ada0"][1] + R)

            @block.scalar
            def _(act):
                act.wait_ge(const_in, 32)
                for i, name in enumerate(("c", "c2")):
                    act.activation(csil[:, i, :], S(name), ACT.Silu).then_inc(silu_done, 1)
                act.wait_ge(x_loaded, 32)
                n0[1](act)
                n0[3](act)
                act.wait_ge(wrapped, 2)
                act.activation(rope2[:, 0, :], wrap[:, 0, :], ACT.Sin)
                act.activation(rope2[:, 1, :], wrap[:, 1, :], ACT.Sin)
                act.wait_ge(mod0_done, 2)
                n0[5](act)

            @block.tensor
            def _(pe):
                pe.wait_ge(const_in, 32)
                n0[2](pe)
                for chunk in range(3):
                    ada_chunk(pe, chunk, ada_sum0, 7 if chunk < 2 else 5)
                pe.sem_inc(piece_used, ADA0[1] - ADA0[0])

            @block.vector
            def _(dve):
                dve.wait_ge(pos_loaded, 16)
                dve.wait_ge(const_in, 32)
                v = note("dve", dve.tensor_copy(wrap[:, 0, :], pos_i))
                dve.wait_ge(dve_step, v)
                v = note("dve", dve.tensor_scalar(ang, wrap[:, 0, :], C("invf"), None, ALU.mult))
                dve.wait_ge(dve_step, v)
                for i, quarter in enumerate((0.25, 0.0)):
                    v = note("dve", dve.tensor_scalar(turns[:, i, :], ang, 1.0 / (2 * math.pi), quarter,
                                                      ALU.mult, ALU.add))
                    dve.wait_ge(dve_step, v)
                    v = note("dve", dve.tensor_scalar(turns[:, i, :], turns[:, i, :], 12582912.0, None, ALU.add))
                    dve.wait_ge(dve_step, v)
                    v = note("dve", dve.tensor_scalar(turns[:, i, :], turns[:, i, :], -12582912.0, None, ALU.add))
                    dve.wait_ge(dve_step, v)
                    for j, part in enumerate(TWO_PI):
                        v = note("dve", dve.scalar_tensor_tensor(
                            out=wrap[:, i, :], in0=turns[:, i, :], scalar=-part,
                            in1=ang if j == 0 else wrap[:, i, :], op0=ALU.mult, op1=ALU.add))
                        dve.wait_ge(dve_step, v)
                    v = note("dve", dve.tensor_scalar(wrap[:, i, :], wrap[:, i, :],
                                                      math.pi / 2 if i == 0 else 0.0, 3.1415925,
                                                      ALU.add, ALU.min))
                    dve.wait_ge(dve_step, v)
                    dve.tensor_scalar(wrap[:, i, :], wrap[:, i, :], -3.1415925, None,
                                      ALU.max).then_inc(wrapped, 1)
                dve.wait_ge(x_loaded, 32)
                n0[0](dve)
                dve.wait_ge(silu_done, 2)
                for j in range(16):
                    ada_piece(dve, j, ada_sum0, 0)
                dve.wait_ge(ada_taken, 2)
                dve.tensor_tensor(mod[:, 0:16], ps[:, 7, 0:16], S("adab")[:, 0:16], ALU.add).then_inc(mod0_done, 1)
                dve.wait_ge(mod0_done, 1)
                dve.scalar_tensor_tensor(out=amp[:, 0, :], in0=mod[:, 8:16], scalar=1.0, in1=S("ng0"),
                                         op0=ALU.add, op1=ALU.mult).then_inc(mod0_done, 1)
                dve.wait_ge(mod0_done, 2)
                n0[4](dve)
                for j in range(16, 24):
                    ada_piece(dve, j, ada_sum0, 0)
                dve.wait_ge(ada_taken, 3)
                dve.tensor_tensor(mod[:, 16:24], ps[:, 5, 16:24], S("adab")[:, 16:24], ALU.add)


        Work.used += ADA0[1] - ADA0[0]

        def rope_parts(tag, n, raw, t1, t2, dst, cos, sin, bank0, raw_ready):
            rotated, cosed = since("rope_rotated", n), since("rope_cosed", n)
            sined, roped = since("rope_sined", n), since("rope_roped", n)

            def pe_part(pe, r):
                raw_ready(pe, r)
                if r >= 2:
                    sined.wait(pe, r - 1)
                pe.matmul(ps[:, bank0 + r % 2, :], C("rot"), raw(r), start=True, stop=True).then_inc(rotated.sem, 1)

            def pool_part(pool, r):
                raw_ready(pool, r)
                if r >= 2:
                    roped.wait(pool, r - 1)
                pool.tensor_tensor(t1[:, r % 2, :], raw(r), cos, ALU.mult).then_inc(cosed.sem, 1)

            def dve_part(dve, r):
                rotated.wait(dve, r + 1)
                if r >= 2:
                    roped.wait(dve, r - 1)
                dve.tensor_tensor(t2[:, r % 2, :], ps[:, bank0 + r % 2, :], sin, ALU.mult).then_inc(sined.sem, 1)
                cosed.wait(dve, r + 1)
                sined.wait(dve, r + 1)
                dve.tensor_tensor(dst(r), t1[:, r % 2, :], t2[:, r % 2, :], ALU.add).then_inc(roped.sem, 1)

            return pe_part, pool_part, dve_part, roped

        def evacuated(order, sems):
            def wait(eng, i):
                eng.wait_ge(sems[order[i]], sum(o == order[i] for o in order[:i + 1]))
            return wait

        rp = area(0, 10, T)
        qr = area(5120, 10, T)
        zs = area(10240, 8, T)
        ot = area(14336, TT, D)
        vs = area(18432, TT, P)
        vw = area(18944, TT, P)
        gate = area(19456, TT, 48)
        kcm = area(19648, 2, CMP_PAD)
        vbd = area(19712, 4, DH)
        WORK = 20192
        xc = area(WORK, 2, 2, T // 2)
        h1 = area(WORK + 1024, 2, 2, 2 * N_CMP)
        rt1 = area(WORK + 1272, 2, T)
        rt2 = area(WORK + 2296, 2, T)

        order2 = ["dve"] * 2 + ["act"] * 21
        ev2 = {"dve": sem("ev2_dve"), "act": sem("ev2_act")}
        left2 = evacuated(order2, ev2)
        h1_sum, h1_done, cmp_sum, cmp_zero = sem("h1_sum"), sem("h1_done"), sem("cmp_sum"), sem("cmp_zero")
        vc_done = sem("vc_done")
        rope_nsa = rope_parts("r0", 10, lambda r: rp[:, r, :], rt1, rt2, lambda r: qr[:, r, :],
                              C("cos"), C("sin"), 4, lambda eng, r: left2(eng, r + 2))
        base2 = PIECE_AT["cmp_in"][0]
        with phase() as block:
            @block.sync
            def _(sp):
                ask_pieces(sp, PIECE_AT["z"][1] + R)

            @block.tensor
            def _(pe):
                def free(u):
                    if u >= 4:
                        left2(pe, u - 4)

                for u in range(12):
                    free(u)
                    feature_unit(pe, base2 + u, u % 4, h_parts)
                    if u >= 4:
                        rope_nsa[0](pe, u - 4)
                for kv, pe_name in enumerate(("pek", "pev")):
                    if kv == 0:
                        left2(pe, 1)
                    for q4 in range(4):
                        w = piece_ready(pe, PIECE_AT["cmp_w1"][0] + kv * 4 + q4)
                        for m in range(4):
                            tap = 4 * q4 + m
                            for ch in range(2):
                                o = ps[:, 6 + ch, kv * 64:kv * 64 + 2 * N_CMP].rearrange("p (g n) -> p g n", g=2)
                                wt = w[:, m * CMP_H + ch * P:m * CMP_H + (ch + 1) * P]
                                pe.matmul(o, wt, xc[:, kv, :, tap:tap + 8 * (N_CMP - 1) + 1:8],
                                          start=(tap == 0), stop=False)
                                mm = pe.matmul(o, wt, S(pe_name)[:, tap:tap + 1].unsqueeze(2).to_broadcast([P, 2, N_CMP]),
                                               start=False, stop=(tap == 15))
                        mm.then_inc(piece_used, 1)
                rope_nsa[0](pe, 8)
                rope_nsa[0](pe, 9)
                for u in range(12, 15):
                    free(u)
                    token_unit(pe, PIECE_AT["vsw"][0] + u - 12, u % 4, h_parts, tile_tokens)
                pe.wait_ge(h1_done, 2)
                for g in range(2):
                    for ch in range(2):
                        pe.matmul(ps[g * DH:(g + 1) * DH, 6, 128:128 + N_CMP], S("w2k")[:, ch * DH:(ch + 1) * DH],
                                  h1[:, 0, ch, g * N_CMP:(g + 1) * N_CMP], start=(ch == 0), stop=(ch == 1))
                    for ch in range(2):
                        mm = pe.matmul(ps[0:N_CMP, 7, 128 + g * DH:128 + (g + 1) * DH],
                                       h1[:, 1, ch, g * N_CMP:(g + 1) * N_CMP],
                                       S("w2v")[:, ch * DH:(ch + 1) * DH], start=(ch == 0), stop=(ch == 1))
                mm.then_inc(cmp_sum, 1)
                for u in range(15, 23):
                    free(u)
                    feature_unit(pe, PIECE_AT["z"][0] + u - 15, u % 4, h_parts)

            @block.scalar
            def _(act):
                def unit(u):
                    n = base2 + u + (8 if u >= 12 else 0)
                    act.wait_ge(piece_used, n + 1)
                    b = ps[:, u % 4, :]
                    if u < 12:
                        ins = act.activation(rp[:, u - 2, :], b, ACT.Copy)
                    elif u < 14:
                        ins = act.activation((vs, vw)[u - 12].rearrange("p a b -> p (a b)"), b, ACT.Copy)
                    elif u == 14:
                        ins = act.activation(gate, b.rearrange("p (a b) -> p a b", b=P)[:, :, 0:48], ACT.Sigmoid)
                    else:
                        ins = act.activation(zs[:, u - 15, :], b, ACT.Silu)
                    ins.then_inc(ev2["act"], 1)

                def piece_of(u):
                    return base2 + u + (8 if u >= 12 else 0)

                split_hi(act, piece_of(0))
                split_hi(act, piece_of(1))
                for u in range(12):
                    split_hi(act, piece_of(u + 2))
                    if u >= 2:
                        unit(u)
                act.wait_ge(piece_used, PIECE_AT["cmp_w1"][1])
                for kv in range(2):
                    act.activation(h1[:, kv, :, :], ps[:, 6:8, kv * 64:kv * 64 + 2 * N_CMP], ACT.Silu).then_inc(h1_done, 1)
                for u in range(12, 23):
                    if u + 2 < 23:
                        split_hi(act, piece_of(u + 2))
                    unit(u)

            @block.gpsimd
            def _(pool):
                parted = [base2 + u for u in range(12)] + [base2 + 8 + u for u in range(12, 23)]
                pool.memset(kcm, 0.0).then_inc(cmp_zero, 1)
                pool.memset(vbd, 0.0).then_inc(cmp_zero, 1)
                for u, n in enumerate(parted):
                    split_lo(pool, n)
                    if 5 <= u < 15:
                        rope_nsa[1](pool, u - 5)

            @block.vector
            def _(dve):
                for kv in range(2):
                    dve.wait_ge(piece_used, base2 + kv + 1)
                    for g in range(2):
                        pair = ps[g * DH:(g + 1) * DH, kv, :].rearrange("p (s par) -> p s par", par=2)
                        for par in range(2):
                            ins = dve.tensor_copy(xc[par * DH:(par + 1) * DH, kv, g, :], pair[:, :, par])
                            if g * 2 + par < 3:
                                note("dve", ins)
                            else:
                                dve.wait_ge(dve_step, counts["dve"])
                                ins.then_inc(ev2["dve"], 1)
                for r in range(10):
                    rope_nsa[2](dve, r)
                dve.wait_ge(cmp_sum, 1)
                dve.wait_ge(cmp_zero, 2)
                for g in range(2):
                    rows = slice(g * DH, (g + 1) * DH)
                    dve.tensor_copy(kcm[rows, g, 0:N_CMP], ps[rows, 6, 128:128 + N_CMP])
                for a in range(4):
                    dve.tensor_copy(vbd[a * 32:a * 32 + N_CMP, a, :],
                                    ps[0:N_CMP, 7, 128 + (a % 2) * DH:128 + (a % 2 + 1) * DH])

        sc = area(WORK, NH * CMP_PAD)
        pc = area(WORK + 512, NH * CMP_PAD)
        ptc = area(WORK + 1024, 4 * P)
        cmx = area(WORK + 1536, NH)
        cden = area(WORK + 1552, NH)
        cr = area(WORK + 1568, NH)
        c_qk, c_sub, c_exp, c_t, c_copied, c_pv, c_out = (sem("c_" + n) for n in "qk sub exp t copied pv out".split())
        by_head = lambda v: v.rearrange("p (h n) -> p h n", h=NH)
        with phase() as block:
            @block.tensor
            def _(pe):
                for i in range(TT):
                    for u in range(8):
                        mm = pe.matmul(ps[:, i, u * 64:(u + 1) * 64], rp[:, 2 + u, tile_tokens(i)],
                                       kcm.rearrange("p g n -> p (g n)"), start=True, stop=True)
                    mm.then_inc(c_qk, 1)
                for i in range(TT):
                    pe.wait_ge(c_exp, i + 1)
                    for a in range(4):
                        mm = pe.transpose(ps[:, 4, a * P:(a + 1) * P], pc[:, a * P:(a + 1) * P], ident)
                    mm.then_inc(c_t, 1)
                    pe.wait_ge(c_copied, i + 1)
                    if i >= 1:
                        pe.wait_ge(c_out, i)
                    for a in range(4):
                        mm = pe.matmul(ps[:, 5 + a // 2, (a % 2) * 256:(a % 2 + 1) * 256], ptc[:, a * P:(a + 1) * P],
                                       vbd.rearrange("p a d -> p (a d)"), start=True, stop=True)
                    mm.then_inc(c_pv, 1)

            @block.scalar
            def _(act):
                for i in range(TT):
                    act.wait_ge(c_sub, i + 1)
                    if i >= 1:
                        act.wait_ge(c_t, i)
                        act.wait_ge(c_out, i)
                    act.activation(pc, sc, ACT.Exp, scale=SCALE).then_inc(c_exp, 1)
                    act.wait_ge(c_t, i + 1)
                    if i >= 1:
                        act.wait_ge(c_pv, i)
                    act.activation(ptc, ps[:, 4, :], ACT.Copy).then_inc(c_copied, 1)

            @block.vector
            def _(dve):
                for i in range(TT):
                    dve.wait_ge(c_qk, i + 1)
                    if i >= 1:
                        dve.wait_ge(c_exp, i)
                    mask = C("mcmp")[:, i * CMP_PAD:(i + 1) * CMP_PAD].unsqueeze(1).to_broadcast([P, NH, CMP_PAD])
                    v = note("dve", dve.tensor_tensor(by_head(sc), by_head(ps[:, i, :]), mask, ALU.add))
                    dve.wait_ge(dve_step, v)
                    v = note("dve", dve.tensor_reduce(cmx, by_head(sc), AX.X, ALU.max))
                    dve.wait_ge(dve_step, v)
                    dve.tensor_tensor(by_head(sc), by_head(sc), cmx.unsqueeze(2).to_broadcast([P, NH, CMP_PAD]),
                                      ALU.subtract).then_inc(c_sub, 1)
                    dve.wait_ge(c_exp, i + 1)
                    v = note("dve", dve.tensor_reduce(cden, by_head(pc), AX.X, ALU.add))
                    dve.wait_ge(dve_step, v)
                    v = note("dve", dve.reciprocal(cr, cden))
                    dve.wait_ge(dve_step, v)
                    v = note("dve", dve.scalar_tensor_tensor(
                        out=cr.rearrange("p (u g) -> p u g", g=2), in0=cr.rearrange("p (u g) -> p u g", g=2),
                        scalar=C("valid")[:, i:i + 1],
                        in1=gate[:, i, 0:48:3].rearrange("p (g u) -> p u g", g=2), op0=ALU.mult, op1=ALU.mult))
                    dve.wait_ge(dve_step, v)
                    dve.wait_ge(c_pv, i + 1)
                    dst = ot[:, i, :].rearrange("p (g u d) -> p u g d", g=2, d=DH)
                    crv = cr.rearrange("p (u g) -> p u g", g=2)
                    for half in range(2):
                        us = slice(4 * half, 4 * half + 4)
                        ins = dve.tensor_tensor(dst[:, us, :, :],
                                                ps[:, 5 + half, :].rearrange("p (u g d) -> p u g d", g=2, d=DH),
                                                crv[:, us, :].unsqueeze(3).to_broadcast([P, 4, 2, DH]), ALU.mult)
                        if half == 0:
                            dve.wait_ge(dve_step, note("dve", ins))
                        else:
                            ins.then_inc(c_out, 1)

        def attention(tag, block, units, work, finish, finish_pool=None, pe_filler=None, dve_filler=None, ask=0,
                      pads=()):
            LT, LP = 3, 5
            CY = 4
            SB, PB, TB = 3, 4, 3
            N = len(units)
            neg = area(work, SB, T)
            prt = area(work + SB * T, TB, T)
            prob = place("prob_" + tag, WR_AT, [PB, T])
            pad_zero, pad_dve, pad_act = since("pad_zero", 2 * len(pads)), since("pad_dve", len(pads)), since("pad_act", len(pads))
            nmax = area(work + 3584, N)
            den = area(work + 3584 + N, N)
            s_done, neg_done, exp_done = since("att_scores", N), since("att_neg", N), since("att_exp", N)
            t_done, pv_done = since("att_transposed", N), since("att_pv", N)
            copied = [since("att_copied_act", N - N // CY), since("att_copied_dve", N // CY)]
            o_read = since("att_o_read", N // 8)

            def wait_copied(eng, n):
                turn = int(n % CY == CY - 1)
                copied[turn].wait(eng, (n + 1) // CY if turn else n + 1 - (n + 1) // CY)

            def copy(n, eng):
                nb = len(units[n][3])
                t_done.wait(eng, n + 1)
                if n >= TB:
                    pv_done.wait(eng, n - TB + 1)
                src, dst = ps[:, 3 + n % 2, 0:nb * P], prt[:, n % TB, 0:nb * P]
                if n % CY < CY - 1:
                    eng.activation(dst, src, ACT.Copy).then_inc(copied[0].sem, 1)
                else:
                    eng.tensor_copy(dst, src).then_inc(copied[1].sem, 1)

            @block.sync
            def _(sp):
                ask_pieces(sp, ask)

            @block.tensor
            def _(pe):
                pad_zero.wait(pe, 2 * len(pads))
                pad_dve.wait(pe, len(pads))
                pad_act.wait(pe, len(pads))
                for n in range(N + LP):
                    if n < N:
                        q, k, mask, vb, _ = units[n]
                        if n >= SB:
                            neg_done.wait(pe, n - SB + 1)
                        pe.matmul(ps[:, n % SB, 0:len(vb) * P], q, k, start=True, stop=True).then_inc(s_done.sem, 1)
                    if LT <= n < N + LT:
                        m = n - LT
                        exp_done.wait(pe, m + 1)
                        if m >= 2:
                            wait_copied(pe, m - 2)
                        nb = len(units[m][3])
                        for b in range(nb):
                            mm = pe.transpose(ps[:, 3 + m % 2, b * P:(b + 1) * P],
                                              prob[:, m % PB, b * P:(b + 1) * P], ident)
                        mm.then_inc(t_done.sem, 1)
                    if pe_filler and n < N:
                        pe_filler(pe, n)
                    if n >= LP:
                        m = n - LP
                        wait_copied(pe, m)
                        if m % 8 == 0 and m >= 16:
                            o_read.wait(pe, m // 8 - 1)
                        vb = units[m][3]
                        for b, v in enumerate(vb):
                            mm = pe.matmul(ps[:, 5 + (m // 8) % 2, (m % 8) * DH:(m % 8 + 1) * DH],
                                           prt[:, m % TB, b * P:(b + 1) * P], v,
                                           start=(b == 0), stop=(b == len(vb) - 1))
                        mm.then_inc(pv_done.sem, 1)

            @block.scalar
            def _(act):
                for dst, src in pads:
                    act.activation(dst[DH:P, 1], src[DH:P], ACT.Copy).then_inc(pad_act.sem, 1)
                for n in range(N + LT):
                    if n < N:
                        w = len(units[n][3]) * P
                        neg_done.wait(act, n + 1)
                        if n >= PB:
                            t_done.wait(act, n - PB + 1)
                        act.activation(prob[:, n % PB, 0:w], neg[:, n % SB, 0:w], ACT.Exp, scale=-1.0,
                                       bias=nmax[:, n:n + 1], accum_out=den[:, n:n + 1]).then_inc(exp_done.sem, 1)
                    if n >= LT and (n - LT) % CY < CY - 1:
                        copy(n - LT, act)

            @block.vector
            def _(dve):
                for dst, src in pads:
                    dve.tensor_copy(dst[0:DH, 0], src[0:DH]).then_inc(pad_dve.sem, 1)
                for n in range(N + LP + 1):
                    if n < N:
                        q, k, mask, vb, init = units[n]
                        w = len(vb) * P
                        s_done.wait(dve, n + 1)
                        if n >= SB:
                            exp_done.wait(dve, n - SB + 1)
                        dve.tensor_tensor_reduce(out=neg[:, n % SB, 0:w], in0=ps[:, n % SB, 0:w], in1=mask,
                                                 scale=-SCALE, scalar=init, op0=ALU.add, op1=ALU.min,
                                                 accum_out=nmax[:, n:n + 1]).then_inc(neg_done.sem, 1)
                    if LT <= n < N + LT and (n - LT) % CY == CY - 1:
                        copy(n - LT, dve)
                    if dve_filler and n < N:
                        dve_filler(dve, n)
                    if n > LP and (n - LP - 1) % 8 == 7:
                        g = (n - LP - 1) // 8
                        exp_done.wait(dve, 8 * (g + 1))
                        pv_done.wait(dve, 8 * (g + 1))
                        finish(dve, g, ps[:, 5 + g % 2, :].rearrange("p (h d) -> p h d", d=DH),
                               den[:, 8 * g:8 * g + 8], nmax[:, 8 * g:8 * g + 8], o_read)

            @block.gpsimd
            def _(pool):
                for dst, _ in pads:
                    pool.memset(dst[DH:P, 0], 0.0).then_inc(pad_zero.sem, 1)
                    pool.memset(dst[0:DH, 1], 0.0).then_inc(pad_zero.sem, 1)
                if finish_pool:
                    finish_pool(pool, o_read)
            return nmax, den

        ks_pad = place("ks_pad", WR_AT + 4 * T, [2, 2, T])
        nsa_units = []
        for branch, (ku, vt) in enumerate(((0, vs), (1, vw))):
            for i in range(TT):
                for h in range(NH):
                    g = h // 8
                    nsa_units.append((qr[:, 2 + h % 8, tile_tokens(i)], ks_pad[:, g, ku, 0:(i + 1) * P],
                                      C("causal")[:, T - (i + 1) * P:T],
                                      [vt[:, b, g * DH:(g + 1) * DH] for b in range(i + 1)], BIG))
        gr = area(WORK + 3840, 2, 8)
        added = sem("nsa_added")
        gtmp = place("gtmp", HR_AT, [2, 512])

        def nsa_finish(dve, g, o, den, nmax, o_read):
            branch, i, half = g // 8, (g // 2) % 4, g % 2
            r = gr[:, g % 2, :]
            v = note("dve", dve.reciprocal(r, den))
            dve.wait_ge(dve_step, v)
            v = note("dve", dve.tensor_tensor(r, r, gate[:, i, 24 * half + 1 + branch:24 * half + 24:3], ALU.mult))
            dve.wait_ge(dve_step, v)
            if g >= 2:
                dve.wait_ge(added, g - 1)
            dve.tensor_tensor(gtmp[:, g % 2, :].rearrange("p (h d) -> p h d", d=DH), o,
                              r.unsqueeze(2).to_broadcast([P, 8, DH]), ALU.mult).then_inc(o_read.sem, 1)

        def nsa_finish_pool(pool, o_read):
            for g in range(16):
                i, half = (g // 2) % 4, g % 2
                o_read.wait(pool, g + 1)
                if g >= 8:
                    pool.wait_ge(added, g - 7)
                dst = ot[:, i, half * 512:(half + 1) * 512]
                pool.tensor_tensor(dst, dst, gtmp[:, g % 2, :], ALU.add).then_inc(added, 1)

        ada_sum = place("ada_sum", HR_AT + 4 * T, [2, PIECE])
        ada_pace, ada_after, due = (0, 0, 0.5, 0.75, 1.0), [], 0.0
        for unit in nsa_units:
            due += ada_pace[len(unit[3])]
            ada_after.append(min(int(due), ADA12[1] - ADA12[0]))
        assert ada_after[-1] == ADA12[1] - ADA12[0]

        def ada_dve(dve, n):
            for j in range(ada_after[n - 1] if n else 0, ada_after[n]):
                ada_piece(dve, 24 + j, ada_sum, 0 if j < 24 else 1)

        def ada_pe(pe, n):
            for chunk in range(9):
                last = (chunk + 1) * KD - 1
                if n == min(next(i for i, a in enumerate(ada_after) if a > last) + 2, len(nsa_units) - 1):
                    ada_chunk(pe, 3 + chunk, ada_sum, 7)

        with phase() as block:
            attention("nsa", block, nsa_units, WORK, nsa_finish, nsa_finish_pool, ada_pe, ada_dve,
                      ADA12[1] + R, [(ks_pad, qr[:, 0:2, :])])
        Work.used += ADA12[1] - ADA12[0]

        def out_projection(tag, block, at, ready, gate_cols, dve_before, pe_before, act_before,
                           pool_before=None):
            added_x = sem(tag + "_x")

            @block.sync
            def _(sp):
                ask_pieces(sp, at + KD + R)

            @block.tensor
            def _(pe):
                if at == ADA12[1]:
                    pe.sem_inc(piece_used, ADA12[1] - ADA12[0])
                pe_before(pe)
                for u in range(KD):
                    if u >= 3:
                        pe.wait_ge(added_x, u - 2)
                    feature_unit(pe, at + u, 4 + u % 3, h_parts, ready if u == 0 else None)

            @block.vector
            def _(dve):
                dve_before(dve)
                for u in range(KD):
                    dve.wait_ge(piece_used, at + u + 1)
                    dve.scalar_tensor_tensor(out=xT[:, u, :], in0=ps[:, 4 + u % 3, :],
                                             scalar=gate_cols[:, u:u + 1], in1=xT[:, u, :],
                                             op0=ALU.mult, op1=ALU.add).then_inc(added_x, 1)

            @block.scalar
            def _(act):
                split_hi(act, at)
                split_hi(act, at + 1)
                act_before(act)
                for u in range(2, KD):
                    split_hi(act, at + u)

            @block.gpsimd
            def _(pool):
                split_lo(pool, at)
                split_lo(pool, at + 1)
                if pool_before:
                    pool_before(pool)
                for u in range(2, KD):
                    split_lo(pool, at + u)
            return added_x

        def transposes(pe, src, units, read, done):
            for u in range(units):
                if u >= 4:
                    pe.wait_ge(read, u - 3)
                for i in range(TT):
                    mm = pe.transpose(ps[:, u % 4, i * P:(i + 1) * P], src[:, i, u * P:(u + 1) * P], ident)
                mm.then_inc(done, 1)

        e_t, e_z, e_mod = sem("e_transposed"), sem("e_gated"), sem("e_mod")
        e_hi, e_lo = sem("e_hi"), sem("e_lo")
        with phase() as block:
            def dve5(dve):
                for u in range(KD + 2):
                    if u < KD:
                        dve.wait_ge(e_t, u + 1)
                        dve.tensor_tensor(zs[:, u, :], ps[:, u % 4, :], zs[:, u, :], ALU.mult).then_inc(e_z, 1)
                    if u >= 2:
                        k = u - 2
                        dve.wait_ge(e_hi, k + 1)
                        dve.tensor_tensor(h_lo[:, k, :], zs[:, k, :], h_hi[:, k, :].bitcast(F32),
                                          ALU.subtract).then_inc(e_lo, 1)
                dve.tensor_tensor(mod[:, 24:96], ps[:, 7, 24:96], S("adab")[:, 24:96], ALU.add).then_inc(e_mod, 1)
                dve.wait_ge(e_mod, 1)
                for i, (col, g) in enumerate(((32, "ng1"), (56, "n1g"), (80, "n2g"))):
                    dve.scalar_tensor_tensor(out=amp[:, 1 + i, :], in0=mod[:, col:col + 8], scalar=1.0, in1=S(g),
                                             op0=ALU.add, op1=ALU.mult)
            def act5(act):
                for u in range(KD):
                    act.wait_ge(e_z, u + 1)
                    act.activation(h_hi[:, u, :], zs[:, u, :], ACT.Copy).then_inc(e_hi, 1)

            out_projection("e", block, PIECE_AT["nsa_out"][0], Since(e_lo, 0), mod[:, 16:24], dve5,
                           lambda pe: transposes(pe, ot, KD, e_z, e_t), act5)

        n1 = norm_parts("n1", xT, ntmp, nsq, KD, 6, amp[:, 1, :], mod[:, 24:32], h_parts)
        qd, kd = area(0, 8, T), area(4096, 8, T)
        zd = area(8192, 8, T)
        vd = area(12288, TT, D)
        od = area(16384, TT, D)
        raw6 = area(16384, 4, T)
        rt61, rt62 = area(18432, 2, T), area(19456, 2, T)
        order6 = ["act"] * 32
        ev6 = {"act": sem("ev6_act")}
        left6 = evacuated(order6, ev6)
        rope_dil = rope_parts("r6", 16, lambda r: raw6[:, r % 4, :], rt61, rt62,
                              lambda r: (qd if r < 8 else kd)[:, r % 8, :], C("cos"), C("sin"), 4, left6)
        base6 = PIECE_AT["dq"][0]
        with phase() as block:
            @block.sync
            def _(sp):
                ask_pieces(sp, PIECE_AT["dz"][1] + R)

            @block.tensor
            def _(pe):
                n1[2](pe)
                for u in range(32):
                    if u >= 4:
                        left6(pe, u - 4)
                    if 16 <= u < 24:
                        token_unit(pe, base6 + u, u % 4, h_parts, tile_tokens if u < 19 else class_tokens)
                    else:
                        feature_unit(pe, base6 + u, u % 4, h_parts, n1[7] if u == 0 else None)
                    if 2 <= u < 18:
                        rope_dil[0](pe, u - 2)

            @block.scalar
            def _(act):
                split_hi(act, base6)
                split_hi(act, base6 + 1)
                n1[1](act)
                n1[3](act)
                n1[5](act)
                for u in range(32):
                    if u + 2 < 32:
                        split_hi(act, base6 + u + 2)
                    act.wait_ge(piece_used, base6 + u + 1)
                    b = ps[:, u % 4, :]
                    if u < 16:
                        if u >= 4:
                            rope_dil[3].wait(act, u - 3)
                        ins = act.activation(raw6[:, u % 4, :], b, ACT.Copy)
                    elif u < 24:
                        ins = act.activation(vd[:, :, (u - 16) * P:(u - 15) * P],
                                             b.rearrange("p (a b) -> p a b", b=P), ACT.Copy)
                    else:
                        ins = act.activation(zd[:, u - 24, :], b, ACT.Silu)
                    ins.then_inc(ev6["act"], 1)

            @block.gpsimd
            def _(pool):
                for u in range(32):
                    split_lo(pool, base6 + u)
                    if 3 <= u < 19:
                        rope_dil[1](pool, u - 3)

            @block.vector
            def _(dve):
                n1[0](dve)
                n1[4](dve)
                for r in range(16):
                    rope_dil[2](dve, r)

        kd_pad = place("kd_pad", HR_AT, [2, KD, T])
        dil_units = []
        for i in range(TT):
            for h in range(NH):
                u, keys = h // 2, kd_pad[:, h % 2]
                cols = slice(h * DH, (h + 1) * DH)
                if h < 6:
                    lo = max(i - 1, 0)
                    dil_units.append((qd[:, u, tile_tokens(i)], keys[:, u, lo * P:(i + 1) * P],
                                      C("band129")[:, (0 if i else P):2 * P],
                                      [vd[:, b, cols] for b in range(lo, i + 1)], BIG))
                else:
                    mask = C("causal")[:, T - P:T] if h < 11 else C("causal16")
                    dil_units.append((qd[:, u, class_tokens(i)], keys[:, u, class_tokens(i)], mask,
                                      [vd[:, i, cols]], BIG))
        dr = sb("dr", [P, 2, 8])

        def plain_finish(dst):
            def finish(dve, g, o, den, nmax, o_read):
                r = dr[:, g % 2, :]
                v = note("dve", dve.reciprocal(r, den))
                dve.wait_ge(dve_step, v)
                dve.tensor_tensor(dst(g), o, r.unsqueeze(2).to_broadcast([P, 8, DH]), ALU.mult).then_inc(o_read.sem, 1)
            return finish

        with phase() as block:
            dnmax, dden = attention("dil", block, dil_units, 20480, plain_finish(
                lambda g: od[:, g // 2, (g % 2) * 512:(g % 2 + 1) * 512].rearrange("p (h d) -> p h d", d=DH)),
                pads=[(kd_pad[:, :, u:u + 2, :], kd[:, u:u + 2, :]) for u in range(0, KD, 2)])

        lse = area(20480, TT, NH)
        lsub = area(20544, TT, NH)
        lg = area(20608, 3, TT)
        lmx = area(20620, 3, TT)
        lrow = area(20640, 3, T)
        lmax = area(22176, T)
        lsum = area(22688, T)
        f_ln, f_lse, f_sub, f_exp, f_sum, f_log, f_row, f_rows, f_e, f_eexp, f_alpha, f_t, f_az, f_z = (
            sem("f_" + n) for n in "ln lse sub exp sum log row rows e eexp alpha t az gated".split())
        f_mx, f_hi, f_lo = sem("f_mx"), sem("f_hi"), sem("f_lo")
        oz = area(0, KD, T)
        dview = dden.rearrange("p (a b) -> p a b", b=NH)
        with phase() as block:
            def act8(act):
                act.activation(lse, dview, ACT.Ln).then_inc(f_ln, 1)
                act.wait_ge(f_sub, 3)
                act.activation(lsub, lsub, ACT.Exp).then_inc(f_exp, 1)
                act.wait_ge(f_sum, 3)
                act.activation(lg, lg, ACT.Ln).then_inc(f_log, 1)
                act.wait_ge(f_rows, 1)
                for g in range(3):
                    act.activation(lrow[:, g, :], ps[:, 4 + g, :], ACT.Copy).then_inc(f_row, 1)
                act.wait_ge(f_e, 3)
                act.activation(lrow, lrow, ACT.Exp).then_inc(f_eexp, 1)
                for u in range(KD):
                    act.wait_ge(f_z, u + 1)
                    act.activation(h_hi[:, u, :], zd[:, u, :], ACT.Copy).then_inc(f_hi, 1)

            def dve8(dve):
                dve.wait_ge(f_ln, 1)
                dve.tensor_tensor(lse, lse, dnmax.rearrange("p (a b) -> p a b", b=NH), ALU.subtract).then_inc(f_lse, 1)
                dve.wait_ge(f_lse, 1)
                for g, (a, b) in enumerate(DIL_GROUPS):
                    dve.tensor_reduce(lmx[:, g, :], lse[:, :, a:b], AX.X, ALU.max).then_inc(f_mx, 1)
                dve.wait_ge(f_mx, 3)
                for g, (a, b) in enumerate(DIL_GROUPS):
                    dve.tensor_tensor(lsub[:, :, a:b], lse[:, :, a:b],
                                      lmx[:, g, :].unsqueeze(2).to_broadcast([P, TT, b - a]),
                                      ALU.subtract).then_inc(f_sub, 1)
                dve.wait_ge(f_exp, 1)
                for g, (a, b) in enumerate(DIL_GROUPS):
                    dve.tensor_reduce(lg[:, g, :], lsub[:, :, a:b], AX.X, ALU.add).then_inc(f_sum, 1)
                dve.wait_ge(f_log, 1)
                for g, (a, b) in enumerate(DIL_GROUPS):
                    dve.scalar_tensor_tensor(out=lg[:, g, :], in0=lg[:, g, :], scalar=-math.log(b - a),
                                             in1=lmx[:, g, :], op0=ALU.add, op1=ALU.add).then_inc(f_log, 1)
                dve.wait_ge(f_row, 3)
                v = note("dve", dve.tensor_tensor(lmax, lrow[:, 0, :], lrow[:, 1, :], ALU.max))
                dve.wait_ge(dve_step, v)
                v = note("dve", dve.tensor_tensor(lmax, lmax, lrow[:, 2, :], ALU.max))
                dve.wait_ge(dve_step, v)
                for g in range(3):
                    dve.tensor_tensor(lrow[:, g, :], lrow[:, g, :], lmax, ALU.subtract).then_inc(f_e, 1)
                dve.wait_ge(f_eexp, 1)
                v = note("dve", dve.tensor_tensor(lsum, lrow[:, 0, :], lrow[:, 1, :], ALU.add))
                dve.wait_ge(dve_step, v)
                v = note("dve", dve.tensor_tensor(lsum, lsum, lrow[:, 2, :], ALU.add))
                dve.wait_ge(dve_step, v)
                v = note("dve", dve.reciprocal(lsum, lsum))
                dve.wait_ge(dve_step, v)
                for g in range(3):
                    dve.scalar_tensor_tensor(out=lrow[:, g, :], in0=lrow[:, g, :], scalar=3.0, in1=lsum,
                                             op0=ALU.mult, op1=ALU.mult).then_inc(f_alpha, 1)
                dve.wait_ge(f_alpha, 3)
                for u in range(KD):
                    dve.wait_ge(f_t, u + 1)
                    parts = [(slice(0, P), 0 if u < 3 else 1 if u < 5 else 2)]
                    if u == 5:
                        parts = [(slice(0, DH), 1), (slice(DH, P), 2)]
                    for rows, g in parts:
                        src = ps[rows, u % 4, :]
                        dst, al = oz[rows, u, :], lrow[rows, g, :]
                        if g:
                            src = src.rearrange("p (r a) -> p a r", r=TT)
                            dst = dst.rearrange("p (a r) -> p a r", r=TT)
                            al = al.rearrange("p (a r) -> p a r", r=TT)
                        ins = dve.tensor_tensor(dst, src, al, ALU.mult)
                        if rows.stop < P:
                            v = note("dve", ins)
                            dve.wait_ge(dve_step, v)
                        else:
                            ins.then_inc(f_az, 1)
                for u in range(KD):
                    dve.wait_ge(f_hi, u + 1)
                    dve.tensor_tensor(h_lo[:, u, :], zd[:, u, :], h_hi[:, u, :].bitcast(F32),
                                      ALU.subtract).then_inc(f_lo, 1)

            def pool8(pool):
                for u in range(KD):
                    pool.wait_ge(f_az, u + 1)
                    pool.tensor_tensor(zd[:, u, :], oz[:, u, :], zd[:, u, :], ALU.mult).then_inc(f_z, 1)

            def pe8(pe):
                pe.wait_ge(f_log, 4)
                for g in range(3):
                    for i in range(TT):
                        cols = tile_tokens(i) if g == 0 else class_tokens(i)
                        mm = pe.matmul(ps[:, 4 + g, cols], lg[:, g, i:i + 1].to_broadcast([P, P]), ident,
                                       start=True, stop=True)
                mm.then_inc(f_rows, 1)
                transposes(pe, od, KD, f_az, f_t)
                pe.wait_ge(f_row, 3)
            out_projection("f", block, PIECE_AT["dil_out"][0], Since(f_lo, 0), mod[:, 40:48], dve8, pe8, act8, pool8)

        nf = norm_parts("nf", xT, xT, nsq, KD, 6, S("fg"), None)
        n2 = norm_parts("n2", xT, ntmp, nsq, KD, 7, amp[:, 2, :], mod[:, 48:56], h_parts)
        raw9, sq9, qn9 = area(0, 5, T), area(2560, 5, T), area(5120, 5, T)
        qr9 = area(7680, 5, T)
        v9 = area(10240, TT, P)
        ccs = area(10752, 4, T)
        hp = area(12800, 4, T + 2)
        conv = area(14856, 4, T)
        rt91, rt92 = area(16904, 2, T), area(17928, 2, T)
        sd9 = area(18952, 2, T)
        va9 = area(19976, 2, T)
        order9 = ["act"] * 10 + ["dve"] * 8
        ev9 = {"act": sem("ev9_act"), "dve": sem("ev9_dve")}
        left9 = evacuated(order9, ev9)
        q_sq, q_sum, q_var, q_root, q_norm = sem("q_sq"), sem("q_sum"), sem("q_var"), sem("q_root"), sem("q_norm")
        hp_zero, conv_in = sem("hp_zero"), sem("conv_in")
        rope_two = rope_parts("r9", 5, lambda r: qn9[:, r, :], rt91, rt92, lambda r: qr9[:, r, :],
                              rope2[:, 0, :], rope2[:, 1, :], 4, lambda eng, r: eng.wait_ge(q_norm, r + 1))
        base9 = PIECE_AT["q2"][0]
        with phase() as block:
            @block.sync
            def _(sp):
                ask_pieces(sp, PIECE_AT["cb"][1] + R)

            @block.tensor
            def _(pe):
                nf[2](pe)
                n2[2](pe)
                for u in range(18):
                    if u >= 4:
                        left9(pe, u - 4)
                    if u == 5:
                        token_unit(pe, base9 + u, u % 4, h_parts, tile_tokens)
                    else:
                        feature_unit(pe, base9 + u, u % 4, h_parts, n2[7] if u == 0 else None)
                    if 1 <= u < 6:
                        r = u - 1
                        pe.wait_ge(q_sq, r + 1)
                        if r >= 2:
                            pe.wait_ge(q_var, r - 1)
                        pe.matmul(ps[:, 6 + r % 2, :], C("bones"), sq9[:, r, :], start=True,
                                  stop=True).then_inc(q_sum, 1)
                    if 4 <= u < 9:
                        rope_two[0](pe, u - 4)

            @block.scalar
            def _(act):
                split_hi(act, base9)
                split_hi(act, base9 + 1)
                nf[1](act)
                nf[3](act)
                nf[6].wait(act, KD)
                n2[1](act)
                n2[3](act)
                n2[5](act)
                for u in range(16):
                    split_hi(act, base9 + u + 2)
                    if u >= 10:
                        continue
                    act.wait_ge(piece_used, base9 + u + 1)
                    b = ps[:, u % 4, :]
                    if u < 5:
                        act.activation(raw9[:, u, :], b, ACT.Copy).then_inc(ev9["act"], 1)
                        left9(act, u)
                        act.activation(sq9[:, u, :], raw9[:, u, :], ACT.Square).then_inc(q_sq, 1)
                        act.wait_ge(q_var, u + 1)
                        act.activation(sd9[:, u % 2, :], va9[:, u % 2, :], ACT.Sqrt).then_inc(q_root, 1)
                    elif u == 5:
                        act.activation(v9.rearrange("p a b -> p (a b)"), b, ACT.Copy).then_inc(ev9["act"], 1)
                    else:
                        act.activation(ccs[:, u - 6, :], b, ACT.Copy).then_inc(ev9["act"], 1)

            @block.gpsimd
            def _(pool):
                pool.memset(hp[:, :, 0:2], 0.0).then_inc(hp_zero, 1)
                for u in range(18):
                    split_lo(pool, base9 + u)
                    if 8 <= u < 13:
                        rope_two[1](pool, u - 8)

            @block.vector
            def _(dve):
                nf[0](dve)
                nf[4](dve)
                nf[6].wait(dve, KD)
                n2[0](dve)
                n2[4](dve)
                for r in range(5):
                    dve.wait_ge(q_sum, r + 1)
                    dve.tensor_scalar(va9[:, r % 2, :], ps[:, 6 + r % 2, :], 1.0 / DH, EPS,
                                      ALU.mult, ALU.add).then_inc(q_var, 1)
                    dve.wait_ge(q_root, r + 1)
                    inverse_root(dve, va9[:, r % 2, :], sd9[:, r % 2, :], rstd[:, :])
                    dve.scalar_tensor_tensor(out=qn9[:, r, :], in0=raw9[:, r, :],
                                             scalar=S("qg" if r < 4 else "kg"), in1=rstd[:, :],
                                             op0=ALU.mult, op1=ALU.mult).then_inc(q_norm, 1)
                    dve.wait_ge(q_norm, r + 1)
                for r in range(5):
                    rope_two[2](dve, r)
                dve.wait_ge(hp_zero, 1)
                for u in range(4):
                    dve.wait_ge(piece_used, base9 + 10 + u + 1)
                    left9(dve, 6 + u)
                    dve.tensor_tensor(hp[:, u, 2:T + 2], ps[:, (10 + u) % 4, :], ccs[:, u, :],
                                      ALU.mult).then_inc(ev9["dve"], 1)
                for u in range(4):
                    left9(dve, 10 + u)
                    w = S("convw")
                    v = note("dve", dve.tensor_scalar(conv[:, u, :], hp[:, u, 0:T], w[:, u:u + 1], None, ALU.mult))
                    for k in (1, 2):
                        dve.wait_ge(dve_step, v)
                        v = note("dve", dve.scalar_tensor_tensor(
                            out=conv[:, u, :], in0=hp[:, u, k:T + k], scalar=w[:, 4 * k + u:4 * k + u + 1],
                            in1=conv[:, u, :], op0=ALU.mult, op1=ALU.add))
                    dve.wait_ge(dve_step, v)
                    dve.wait_ge(piece_used, base9 + 14 + u + 1)
                    dve.tensor_tensor(conv[:, u, :], ps[:, (14 + u) % 4, :], conv[:, u, :],
                                      ALU.mult).then_inc(ev9["dve"], 1)

        neg_sink = sb("neg_sink", [P, NQ2])
        o10 = area(0, TT, 512)
        k_pad = place("k_pad", HR_AT, [2, 1, T])
        win_units = []
        for i in range(TT):
            for h in range(NQ2):
                g = h // 4
                lo = max(i - 1, 0)
                win_units.append((qr9[:, h % 4, tile_tokens(i)], k_pad[:, g, 0, lo * P:(i + 1) * P],
                                  C("band128")[:, (0 if i else P):2 * P],
                                  [v9[:, b, g * DH:(g + 1) * DH] for b in range(lo, i + 1)],
                                  neg_sink[:, h:h + 1]))

        def win_finish(dve, g, o, den, nmax, o_read):
            dve.tensor_copy(o10[:, g, :].rearrange("p (h d) -> p h d", d=DH), o).then_inc(o_read.sem, 1)

        with phase() as block:
            @block.vector
            def _(dve):
                dve.tensor_scalar(neg_sink[:, :], S("sinks"), -1.0, None, ALU.mult)
        with phase() as block:
            wnmax, wden = attention("win", block, win_units, 18440, win_finish, pads=[(k_pad, qr9[:, 4:5, :])])

        at11, m11 = area(2048, 4, T), area(4096, 8, T)
        sq11 = area(8192, 4, T)
        se = area(12288, TT, NQ2)
        rd = area(12320, TT, NQ2)
        g_e, g_x, g_d, g_o, g_t, g_a = (sem("g_" + n) for n in "e sinks d o t a".split())
        na = norm_parts("na", at11, m11[:, 0:4, :], sq11, 4, 4, S("aog"), None, (h_hi[:, 0:4, :], h_lo[:, 0:4, :]))
        nb_ = norm_parts("nb", conv, m11[:, 4:8, :], sq11, 4, 5, S("cog"), None, (h_hi[:, 4:8, :], h_lo[:, 4:8, :]))
        m_ready = sem("m_ready")
        with phase() as block:
            def act11(act):
                act.wait_ge(g_e, 1)
                act.activation(se, se, ACT.Exp).then_inc(g_x, 1)
                act.wait_ge(g_a, 4)
                na[1](act)
                na[3](act)
                na[5](act)
                nb_[1](act)
                nb_[3](act)
                nb_[5](act)

            def dve11(dve):
                wn = wnmax.rearrange("p (a b) -> p a b", b=NQ2)
                wd = wden.rearrange("p (a b) -> p a b", b=NQ2)
                dve.tensor_tensor(se, wn, S("sinks").unsqueeze(1).to_broadcast([P, TT, NQ2]), ALU.add).then_inc(g_e, 1)
                dve.wait_ge(g_x, 1)
                v = note("dve", dve.tensor_tensor(rd, se, wd, ALU.add))
                dve.wait_ge(dve_step, v)
                v = note("dve", dve.reciprocal(rd, rd))
                dve.wait_ge(dve_step, v)
                for i in range(TT):
                    o = o10[:, i, :].rearrange("p (h d) -> p h d", d=DH)
                    dve.tensor_tensor(o, o, rd[:, i, :].unsqueeze(2).to_broadcast([P, NQ2, DH]),
                                      ALU.mult).then_inc(g_o, 1)
                for u in range(4):
                    dve.wait_ge(g_t, u + 1)
                    dve.tensor_copy(at11[:, u, :], ps[:, u % 4, :]).then_inc(g_a, 1)
                dve.wait_ge(g_a, 4)
                na[0](dve)
                na[4](dve)
                na[6].wait(dve, 4)
                nb_[0](dve)
                nb_[4](dve)

            def pe11(pe):
                pe.wait_ge(g_o, 4)
                transposes(pe, o10, 4, g_a, g_t)
                na[2](pe)
                nb_[2](pe)
                na[7].wait(pe, 4)
                nb_[7].wait(pe, 4)
            out_projection("g", block, PIECE_AT["out2"][0], None, mod[:, 64:72], dve11, pe11, act11)

        n3 = norm_parts("n3", xT, ntmp, nsq, KD, 6, amp[:, 3, :], mod[:, 72:80], h_parts)
        qp = area(0, 16, T)
        scs = area(8192, TT * 16, PK)
        order12 = ["act", "dve"] * 16
        ev12 = {"act": sem("ev12_act"), "dve": sem("ev12_dve")}
        left12 = evacuated(order12, ev12)
        k_sum = sem("k_sum")
        base12, sub12 = PIECE_AT["wq"][0], PIECE_AT["subkeys"][0]
        scv = scs.rearrange("p (s q) k -> p s (q k)", q=4)
        with phase() as block:
            @block.sync
            def _(sp):
                ask_pieces(sp, N_PIECES)

            @block.tensor
            def _(pe):
                n3[2](pe)
                for u in range(16):
                    if u >= 4:
                        left12(pe, u - 4)
                    feature_unit(pe, base12 + u, u % 4, h_parts, n3[7] if u == 0 else None)
                for u in range(16, 32):
                    left12(pe, u - 4)
                    s, i, q = (u - 16) // 8, (u - 16) // 2 % 4, u % 2
                    if u == 16:
                        left12(pe, 15)
                        left12(pe, 14)
                    if (u - 16) % 8 == 0:
                        w = piece_ready(pe, sub12 + s)
                    for j in range(4):
                        mm = pe.matmul(ps[:, u % 4, j * P:(j + 1) * P], qp[:, s * 8 + q * 4 + j, tile_tokens(i)],
                                       w[:, (q * 4 + j) * P:(q * 4 + j + 1) * P], start=True, stop=True)
                    mm.then_inc(k_sum, 1)

            def out12(eng, who, u):
                if u < 16:
                    eng.wait_ge(piece_used, base12 + u + 1)
                    dst = qp[:, u, :]
                else:
                    eng.wait_ge(k_sum, u - 15)
                    s, i, q = (u - 16) // 8, (u - 16) // 2 % 4, u % 2
                    dst = scv[:, i * 4 + s * 2 + q, :]
                if who == "act":
                    eng.activation(dst, ps[:, u % 4, :], ACT.Copy).then_inc(ev12["act"], 1)
                else:
                    eng.tensor_copy(dst, ps[:, u % 4, :]).then_inc(ev12["dve"], 1)

            @block.scalar
            def _(act):
                split_hi(act, base12)
                split_hi(act, base12 + 1)
                n3[1](act)
                n3[3](act)
                n3[5](act)
                for u in range(32):
                    if u + 2 < 16:
                        split_hi(act, base12 + u + 2)
                    if u % 2 == 0:
                        out12(act, "act", u)

            @block.gpsimd
            def _(pool):
                for u in range(16):
                    split_lo(pool, base12 + u)

            @block.vector
            def _(dve):
                n3[0](dve)
                n3[4](dve)
                for u in range(1, 32, 2):
                    out12(dve, "dve", u)

        eu_raw = place("eu_raw", WR_AT, [2, PIECE])
        eu_split = place("eu_split", WR_AT + 2 * PIECE, [2, 2, PIECE], F32R)
        e_gel = place("e_gel", WR_AT + 6 * PIECE, [2, T])
        eu_landed = [sem(f"eu_landed{i}") for i in range(2)]
        eu_hi, eu_lo, ea_sum, e_gelus = sem("eu_hi"), sem("eu_lo"), sem("ea_sum"), sem("e_gelus")
        e_stored = [sem(f"e_stored{i}") for i in range(2)]
        u_pairs = u_in.rearrange("(r b) p n -> r b p n", b=2)
        gelu_pairs = gelu_dram.rearrange("(r b) p t -> r b p t", b=2)

        def early_load(sp, r, b):
            sp.wait_ge(eu_lo, r * 2 + (b + 1))
            sp.dma_start(eu_raw[:, b, :], u_pairs[r, b]).then_inc(eu_landed[b], 16)

        def early_store(sp, r, b):
            sp.wait_ge(e_gelus, r * 2 + (b + 1 + 2))
            sp.dma_start(gelu_pairs[r, b], e_gel[:, b, :]).then_inc(e_stored[b], 16)

        def early_loads(sp, r0, r1):
            for b in range(2):
                early_load(sp, r0, b)
            with sp.Fori(0, r1 - r0 - 1) as r:
                for b in range(2):
                    early_load(sp, r + (r0 + 1), b)
                    early_store(sp, r + r0, b)
            early_load(sp, r1, 0)
            early_store(sp, r1 - 1, 0)
            early_load(sp, r1, 1)

        def early_upper(act, r, b):
            act.wait_ge(eu_landed[b], r * 16 + 16)
            act.wait_ge(ea_sum, r * 2 + (b + 1))
            act.activation(eu_split[:, b, 0, :], eu_raw[:, b, :], ACT.Copy).then_inc(eu_hi, 1)

        def early_lower(pool, r, b):
            pool.wait_ge(eu_hi, r * 2 + (b + 1))
            pool.tensor_tensor(eu_split[:, b, 1, :], eu_raw[:, b, :], eu_split[:, b, 0, :].bitcast(F32),
                               ALU.subtract).then_inc(eu_lo, 1)

        def early_first(pe, r, b, units):
            for k in units:
                if k == 0:
                    pe.wait_ge(eu_lo, r * 2 + (b + 1 + 2))
                    pe.wait_ge(e_gelus, r * 2 + (b + 1))
                for u, h in HI_LO:
                    mm = pe.matmul(ps[:, 6 + b, :], eu_split[:, b, u, k * P:(k + 1) * P], h_parts[h][:, k, :],
                                   start=(k + u + h == 0), stop=(k == KD - 1 and u == 1))
            if units[-1] == KD - 1:
                mm.then_inc(ea_sum, 1)

        def early_gelu(act, r, b):
            act.wait_ge(ea_sum, r * 2 + (b + 1 + 2))
            act.wait_ge(e_stored[b], r * 16 + 16)
            act.activation(e_gel[:, b, :], ps[:, 6 + b, :], ACT.Gelu_apprx_tanh).then_inc(e_gelus, 1)

        rep = area(0, 16, PK)
        cand = area(2048, PH, PTOP * PTOP)
        rep2 = area(4096, PH, PTOP * PTOP)
        eq = rep2.rearrange("p h (k a) -> p h k a", a=PTOP)
        prod = area(16384, PH, PTOP * PTOP).rearrange("p h (k a) -> p h k a", a=PTOP)
        vals = area(18432, 16, PTOP)
        ids_u = area(18688, 16, PTOP).bitcast(U32)
        ids_f = area(18944, 16, PTOP)
        top = area(19200, PH, PTOP)
        pos_u = area(19328, PH, PTOP).bitcast(U32)
        posab = area(19456, 2, P)
        posab_u = area(19712, 2, P).bitcast(U32)
        sel = area(19968, 3, P)
        gsum = area(20352, PH)
        selT = area(20480, 3, T)
        t_cand, t_vals, t_top, t_gate, t_sel, t_tr, t_read = (
            sem("t_" + n) for n in "cand vals top gate sel tr read".split())
        ids3 = ids_f.rearrange("p (h two) k -> p h two k", two=2)
        val3 = vals.rearrange("p (h two) k -> p h two k", two=2)
        TOP_PAIRS, PAIRS, LATE, KEPT = TT * EARLY_TOP // 2, EARLY_TOP // 2, 1, 3
        with phase() as block:
            @block.sync
            def _(sp):
                for b in range(2):
                    sp.sem_inc(e_stored[b], 16)
                early_loads(sp, 0, TOP_PAIRS)

            @block.gpsimd
            def _(pool):
                pool.sem_inc(eu_lo, 2)
                with pool.Fori(0, TOP_PAIRS) as r:
                    for b in range(2):
                        early_lower(pool, r, b)
                early_lower(pool, TOP_PAIRS, 0)

            @block.scalar
            def _(act):
                act.sem_inc(e_gelus, 2)
                for b in range(2):
                    early_upper(act, 0, b)

                def turns(r0, r1):
                    with act.Fori(0, r1 - r0) as r:
                        for b in range(2):
                            early_gelu(act, r + r0, b)
                            early_upper(act, r + (r0 + 1), b)

                def selection(i):
                    act.wait_ge(t_tr, i + 1)
                    act.activation(selT[:, :, tile_tokens(i)],
                                   ps[:, i % 2, 0:3 * P].rearrange("p (a b) -> p a b", b=P),
                                   ACT.Copy).then_inc(t_read, 1)

                for i in range(TT):
                    r0 = i * PAIRS
                    turns(r0, r0 + LATE)
                    if i >= 1:
                        selection(i - 1)
                    turns(r0 + LATE, r0 + KEPT)
                    act.wait_ge(t_top, i + 1)
                    act.activation(top, top, ACT.Exp).then_inc(t_gate, 1)
                    turns(r0 + KEPT, r0 + PAIRS - int(i == TT - 1))
                early_gelu(act, TOP_PAIRS - 1, 0)
                early_upper(act, TOP_PAIRS, 0)
                selection(TT - 1)

            @block.tensor
            def _(pe):
                pe.sem_inc(ea_sum, 2)

                def turns(r0, r1):
                    with pe.Fori(0, r1 - r0) as r:
                        for b in range(2):
                            early_first(pe, r + r0, b, range(KD))

                def selection(i):
                    pe.wait_ge(t_sel, i + 1)
                    if i >= 2:
                        pe.wait_ge(t_read, i - 1)
                    for j in range(3):
                        mm = pe.transpose(ps[:, i % 2, j * P:(j + 1) * P], sel[:, j, :], ident)
                    mm.then_inc(t_tr, 1)

                for i in range(TT):
                    turns(i * PAIRS, i * PAIRS + LATE)
                    if i >= 1:
                        selection(i - 1)
                    turns(i * PAIRS + LATE, (i + 1) * PAIRS)
                selection(TT - 1)

            @block.vector
            def _(dve):
                def step(ins):
                    dve.wait_ge(dve_step, note("dve", ins))

                def top16(src, scratch, values, index, n):
                    for j in range(n):
                        v = note("dve", dve.max(values[:, j, 0:8], src[:, j, :]))
                    dve.wait_ge(dve_step, v)
                    for j in range(n):
                        note("dve", dve.max_index(index[:, j, 0:8], values[:, j, 0:8], src[:, j, :]))
                        v = note("dve", dve.match_replace(scratch[:, j, :], values[:, j, 0:8], src[:, j, :], -3e38))
                    dve.wait_ge(dve_step, v)
                    for j in range(n):
                        v = note("dve", dve.max(values[:, j, 8:16], scratch[:, j, :]))
                    dve.wait_ge(dve_step, v)
                    for j in range(n):
                        v = note("dve", dve.max_index(index[:, j, 8:16], values[:, j, 8:16], scratch[:, j, :]))
                    dve.wait_ge(dve_step, v)

                for i in range(TT):
                    top16(scs[:, i * 16:(i + 1) * 16, :], rep, vals, ids_u, 16)
                    dve.tensor_copy(ids_f, ids_u).then_inc(t_vals, 1)
                    dve.wait_ge(t_vals, i + 1)
                    dve.tensor_tensor(cand.rearrange("p h (a b) -> p h a b", b=PTOP),
                                      val3[:, :, 0, :].unsqueeze(3).to_broadcast([P, PH, PTOP, PTOP]),
                                      val3[:, :, 1, :].unsqueeze(2).to_broadcast([P, PH, PTOP, PTOP]),
                                      ALU.add).then_inc(t_cand, 1)
                    dve.wait_ge(t_cand, i + 1)
                    top16(cand, rep2, top, pos_u, PH)
                    step(dve.tensor_copy(gsum, top[:, :, 0]))
                    dve.tensor_tensor(top, top, gsum.unsqueeze(2).to_broadcast([P, PH, PTOP]),
                                      ALU.subtract).then_inc(t_top, 1)
                    flat = pos_u.rearrange("p h k -> p (h k)")
                    note("dve", dve.tensor_scalar(posab_u[:, 0, :], flat, 4, None, ALU.logical_shift_right))
                    step(dve.tensor_scalar(posab_u[:, 1, :], flat, 15, None, ALU.bitwise_and))
                    step(dve.tensor_copy(posab, posab_u))
                    if i >= 1:
                        dve.wait_ge(t_tr, i)
                    for j in range(2):
                        step(dve.tensor_tensor(
                            eq.rearrange("p h k a -> p (h k) a"),
                            posab[:, j, :].unsqueeze(2).to_broadcast([P, P, PTOP]),
                            C("iota16").unsqueeze(1).to_broadcast([P, P, PTOP]), ALU.is_equal))
                        step(dve.tensor_tensor(
                            prod, eq, ids3[:, :, j, :].unsqueeze(2).to_broadcast([P, PH, PTOP, PTOP]), ALU.mult))
                        step(dve.tensor_reduce(sel[:, j, :], prod.rearrange("p h k a -> p (h k) a"), AX.X, ALU.add))
                    dve.wait_ge(t_gate, i + 1)
                    step(dve.tensor_reduce(gsum, top, AX.X, ALU.add))
                    step(dve.reciprocal(gsum, gsum))
                    dve.tensor_tensor(sel[:, 2, :].rearrange("p (h k) -> p h k", k=PTOP), top,
                                      gsum.unsqueeze(2).to_broadcast([P, PH, PTOP]), ALU.mult).then_inc(t_sel, 1)
                    dve.wait_ge(t_sel, i + 1)

        QT, NQ = 4, 4
        stage = area(0, 2, NG * CHUNK * GI)
        hot_a = area(16384, NQ * QT, P)
        hot_b = area(18432, NQ * QT, P)
        a_ready, b_dve, b_pool = sem("a_ready"), sem("b_dve"), sem("b_pool")
        g_done, g_read, keys_here = sem("g_done"), sem("g_read"), sem("keys_here")
        keys_seen = sem("keys_seen")
        keys_q = area(22016, 2, QT)
        stored = [sem("stored0"), sem("stored1")]
        NCH = T // CHUNK
        STEP = NQ * QT
        POOL_QUADS = (0, 2)
        QC = CHUNK // STEP
        with phase() as block:
            @block.vector
            def _(dve):
                with dve.Fori(0, T // STEP) as q:
                    for quad in range(NQ):
                        dve.wait_ge(g_done, q * NQ + (quad + 1))
                        for s in range(QT):
                            slot, t = quad * QT + s, q * STEP + (quad * QT + s)
                            if quad not in POOL_QUADS:
                                dve.tensor_scalar(hot_b[:, slot, :], C("iota"), selT[:, 1, bass.ds(t, 1)], None,
                                                  ALU.is_equal).then_inc(b_dve, 1)
                            dve.tensor_scalar(hot_a[:, slot, :], C("iota"), selT[:, 0, bass.ds(t, 1)],
                                              selT[:, 2, bass.ds(t, 1)], ALU.is_equal, ALU.mult).then_inc(a_ready, 1)

            def gates_pool(pool, ch, more):
                for b in range(2):
                    for st in range(QC // 2):
                        q = ch * QC + (b * (QC // 2) + st)
                        for quad in POOL_QUADS:
                            pool.wait_ge(g_done, q * NQ + (quad + 1))
                            pool.tensor_copy(keys_q[:, quad // 2, :],
                                             selT[:, 1, bass.ds(q * STEP + quad * QT, QT)]).then_inc(keys_here, 1)
                            pool.wait_ge(keys_here, q * 2 + (quad // 2 + 1))
                            pool.sem_inc(keys_seen, 1)
                            for s in range(QT):
                                pool.tensor_scalar(hot_b[:, quad * QT + s, :], C("iota"),
                                                   keys_q[:, quad // 2, s:s + 1], None,
                                                   ALU.is_equal).then_inc(b_pool, 1)
                    if more or b == 0:
                        early_lower(pool, ch + (TOP_PAIRS + b), 1 - b)

            @block.gpsimd
            def _(pool):
                with pool.Fori(0, NCH - 1) as ch:
                    gates_pool(pool, ch, True)
                gates_pool(pool, NCH - 1, False)

            @block.tensor
            def _(pe):
                pe.sem_inc(g_done, NQ)
                with pe.Fori(0, NCH) as ch:
                    for n in range(QC * NQ):
                        q, quad = ch * QC + n // NQ, n % NQ
                        if quad in POOL_QUADS:
                            pe.wait_ge(b_pool, q * (2 * QT) + (quad // 2 + 1) * QT)
                        else:
                            pe.wait_ge(b_dve, q * (2 * QT) + (quad // 2 + 1) * QT)
                        pe.wait_ge(a_ready, q * STEP + (quad + 1) * QT)
                        pe.wait_ge(g_read, q * NQ + (quad + 1))
                        for s in range(QT):
                            mm = pe.matmul(ps[:, quad, s * P:(s + 1) * P], hot_b[:, quad * QT + s, :],
                                           hot_a[:, quad * QT + s, :], start=True, stop=True)
                        mm.then_inc(g_done, 1)
                        early_first(pe, ch + TOP_PAIRS, n // KD, [n % KD])

            def gates_act(act, pair, more):
                for half in range(2):
                    ch = pair * 2 + half
                    act.wait_ge(stored[half], pair * 16 + 16)
                    sv = stage[:, half, :].rearrange("p (g t i) -> p t g i", t=CHUNK, i=GI)
                    for n in range(QC * NQ):
                        act.wait_ge(g_done, ch * (QC * NQ) + (n + 1 + NQ))
                        act.activation(sv[:, n * QT:(n + 1) * QT, :, :],
                                       ps[:, n % NQ, :].rearrange("p (t g i) -> p t g i", t=QT, i=GI),
                                       ACT.Copy).then_inc(g_read, 1)
                        b = n // KD
                        if n % KD == 2:
                            early_gelu(act, ch + (TOP_PAIRS - 1 + b), 1 - b)
                        if n % KD == 1 and (more or half == 0 or b == 0):
                            early_upper(act, ch + (TOP_PAIRS + b), 1 - b)

            @block.scalar
            def _(act):
                act.sem_inc(g_read, NQ)
                with act.Fori(0, NCH // 2 - 1) as pair:
                    gates_act(act, pair, True)
                gates_act(act, NCH // 2 - 1, False)
                early_gelu(act, TOP_PAIRS + NCH - 1, 1)

            @block.sync
            def _(sp):
                for half in range(2):
                    sp.sem_inc(stored[half], 16)

                def gates_store(ch, part=0, parts=1):
                    sp.wait_ge(g_read, NQ + ch * QC * NQ + (part + 1) * QC * NQ // parts)
                    lo, hi = part * CHUNK * GI // parts, (part + 1) * CHUNK * GI // parts
                    sp.dma_start(gates_dram[:, :, ch * CHUNK * GI + lo:ch * CHUNK * GI + hi]
                                 .rearrange("g p n -> p g n"),
                                 stage[:, ch % 2, :].rearrange("p (g n) -> p g n", g=NG)[:, :, lo:hi]
                                 ).then_inc(stored[ch % 2], 16)

                for ch in range(NCH):
                    if ch < NCH - 1:
                        for b in range(2):
                            early_load(sp, TOP_PAIRS + ch + 1, b)
                    if ch >= 1:
                        gates_store(ch - 1)
                    early_store(sp, TOP_PAIRS + ch - 1, 1)
                    early_store(sp, TOP_PAIRS + ch, 0)
                for part in range(2):
                    gates_store(NCH - 1, part, 2)
                early_store(sp, TOP_PAIRS + NCH - 1, 1)
                for i in range(2):
                    sp.wait_ge(stored[i], 16 + 16 * (NCH // 2 + i))
                for b in range(2):
                    sp.wait_ge(e_stored[b], 16 + 16 * (TOP_PAIRS + NCH))

        M2 = 2
        acc = place("acc", 0, [KD, T])
        v2_raw = place("v2_raw", KD * T, [2, M2, PIECE])
        g2_buf = place("g2_buf", 8192, [2, GI * T])
        gel2 = place("gel2", 12288, [2, M2, T])
        wgt2 = place("wgt2", 14336, [2, M2, 2, T], F32R)
        v2_split = place("v2_split", WR_AT, [2, M2, 2, PIECE], F32R)
        gview2 = g2_buf.rearrange("p b (t i) -> p b i t", i=GI)
        v2_landed = [sem(f"v2_landed{i}") for i in range(2)]
        g2_landed = [sem(f"g2_landed{i}") for i in range(2)]
        gel2_landed = [sem(f"gel2_landed{i}") for i in range(2)]
        v2_hi, v2_lo, w2_hi, w2_done = sem("v2_hi"), sem("v2_lo"), sem("w2_hi"), sem("w2_done")
        gated2, y2_sum, y2_added, acc2_zero = sem("gated2"), sem("y2_sum"), sem("y2_added"), sem("acc2_zero")
        v_pairs = v_in.rearrange("(m i p) d -> m p i d", i=M2, p=P)
        gelu_in = gelu_dram.rearrange("(m i) p t -> m p i t", i=M2)
        NM = EARLY // M2
        with phase() as block:
            @block.sync
            def _(sp):
                with sp.Fori(0, NM // 4) as quad:
                    for x in range(4):
                        m, s = quad * 4 + x, x % 2
                        sp.wait_ge(v2_lo, m * M2 + M2)
                        sp.dma_start(v2_raw[:, s, :, :], v_pairs[m]).then_inc(v2_landed[s], 16)
                        sp.wait_ge(w2_done, m * M2 + M2)
                        sp.dma_start(gel2[:, s, :, :], gelu_in[m]).then_inc(gel2_landed[s], 16)
                        if s == 0:
                            sp.wait_ge(gated2, m * M2 + 4 * M2 - GI)
                            sp.dma_start(g2_buf[:, x // 2, :],
                                         gates_dram[quad * 2 + x // 2]).then_inc(g2_landed[x // 2], 16)

            @block.tensor
            def _(pe):
                pe.sem_inc(y2_sum, 2 * KD)
                with pe.Fori(0, NM // 2) as pair:
                    for s in range(2):
                        m = pair * 2 + s
                        pe.wait_ge(v2_lo, m * M2 + (M2 + 2 * M2))
                        pe.wait_ge(w2_done, m * M2 + (M2 + 2 * M2))
                        for j in range(KD):
                            pe.wait_ge(y2_added, m * KD + (j + 1))
                            for i in range(M2):
                                for a, b in HI_LO:
                                    mm = pe.matmul(ps[:, 2 + j % 4, :], v2_split[:, s, i, a, j * P:(j + 1) * P],
                                                   wgt2[:, s, i, b, :], start=(i + a + b == 0),
                                                   stop=(i == M2 - 1 and a == 1))
                            mm.then_inc(y2_sum, 1)

            @block.scalar
            def _(act):
                with act.Fori(0, NM // 2) as pair:
                    for s in range(2):
                        m = pair * 2 + s
                        act.wait_ge(y2_sum, m * KD + KD)
                        act.wait_ge(v2_landed[s], pair * 16 + 16)
                        for i in range(M2):
                            act.activation(v2_split[:, s, i, 0, :], v2_raw[:, s, i, :], ACT.Copy).then_inc(v2_hi, 1)
                        for i in range(M2):
                            act.wait_ge(gated2, m * M2 + (i + 1 + 4 * M2))
                            act.activation(wgt2[:, s, i, 0, :], gel2[:, s, i, :], ACT.Copy).then_inc(w2_hi, 1)

            @block.gpsimd
            def _(pool):
                pool.memset(acc[:, :, :], 0.0).then_inc(acc2_zero, 1)
                pool.sem_inc(v2_lo, 2 * M2)
                with pool.Fori(0, NM // 2) as pair:
                    for s in range(2):
                        for i in range(M2):
                            pool.wait_ge(v2_hi, pair * (2 * M2) + (s * M2 + i + 1))
                            pool.tensor_tensor(v2_split[:, s, i, 1, :], v2_raw[:, s, i, :],
                                               v2_split[:, s, i, 0, :].bitcast(F32),
                                               ALU.subtract).then_inc(v2_lo, 1)

            @block.vector
            def _(dve):
                G0 = 4 * M2

                def gated(quad, x):
                    s, g = x % 2, x // 2
                    if s == 0:
                        dve.wait_ge(g2_landed[g], quad * 16 + 16)
                    dve.wait_ge(gel2_landed[s], quad * 32 + (x // 2 + 1) * 16)
                    for i in range(M2):
                        dve.tensor_tensor(gel2[:, s, i, :], gel2[:, s, i, :], gview2[:, g, s * M2 + i, :],
                                          ALU.mult).then_inc(gated2, 1)

                def lower_weights(quad, x):
                    s, m = x % 2, quad * 4 + x
                    for i in range(M2):
                        dve.wait_ge(w2_hi, m * M2 + (i + 1))
                        dve.tensor_tensor(wgt2[:, s, i, 1, :], gel2[:, s, i, :],
                                          wgt2[:, s, i, 0, :].bitcast(F32), ALU.subtract).then_inc(w2_done, 1)

                def added(quad, x, units):
                    m = quad * 4 + x
                    for j in units:
                        dve.wait_ge(y2_sum, m * KD + (j + 1 + 2 * KD))
                        dve.wait_ge(y2_added, m * KD + (j + 2))
                        dve.tensor_tensor(acc[:, j, :], ps[:, 2 + j % 4, :], acc[:, j, :],
                                          ALU.add).then_inc(y2_added, 1)

                def turn(quad, x):
                    after = (quad, x + 1) if x < 3 else (quad + 1, 0)
                    gated(*after)
                    added(quad, x, range(0, KD // 2))
                    lower_weights(*after)
                    added(quad, x, range(KD // 2, KD))

                dve.sem_inc(gated2, G0)
                dve.sem_inc(w2_done, 2 * M2)
                dve.sem_inc(y2_added, 4)
                dve.wait_ge(acc2_zero, 1)
                gated(0, 0)
                lower_weights(0, 0)
                with dve.Fori(0, NM // 4 - 1) as quad:
                    for x in range(4):
                        turn(quad, x)
                for x in range(3):
                    turn(NM // 4 - 1, x)
                added(NM // 4 - 1, 3, range(KD))
        UB = 2
        WS = GI + 1
        at = 0
        at += KD * T
        u_raw = place("u_raw", at, [UB, PIECE]); at += UB * PIECE
        v_raw = place("v_raw", at, [GI, PIECE]); at += GI * PIECE
        gbuf = place("gbuf", at, [2, GI * T]); at += 2 * GI * T
        gel = place("gel", WR_AT + GI * 2 * PIECE, [2, T])
        u_split = place("u_split", at, [UB, 2, PIECE], F32R); at += UB * 2 * PIECE
        wgt = place("wgt", at, [WS, 2, T], F32R); at += WS * 2 * T
        assert at <= HR_AT
        v_split = place("v_split", WR_AT, [GI, 2, PIECE], F32R)
        G0, NG2 = EARLY // GI, NG - EARLY // GI
        ug = u_in.rearrange("(g i) p n -> g i p n", i=GI)
        vg = v_in.rearrange("(g i p) d -> g p i d", i=GI, p=P)
        gview = gbuf.rearrange("p b (t i) -> p b i t", i=GI)
        u_landed, U0 = eu_landed, 16 * EARLY // UB
        v_landed = sem("v_landed")
        g_landed = [sem(f"g_landed{i}") for i in range(2)]
        u_hi, u_lo, v_hi, v_lo = sem("u_hi"), sem("u_lo"), sem("v_hi"), sem("v_lo")
        a_sum, gelus = sem("a_sum"), sem("gelus")
        y_sum, y_added, x_final = sem("y_sum"), sem("y_added"), sem("x_final")
        gated, w_done = sem("gated"), sem("w_done")
        out_stored = sem("out_stored")
        A0, UL0, VL0, GE0, W0, Y0, B0 = UB, UB, GI, 2, 2 * GI, KD, 4

        with phase() as block:
            @block.sync
            def _(sp):
                with sp.Fori(0, NG2 // 2) as pair:
                    for b in range(2):
                        g = pair * 2 + b
                        for i in range(GI):
                            sp.wait_ge(u_lo, g * GI + (i + 1))
                            sp.dma_start(u_raw[:, i % UB, :], ug[g + G0, i]).then_inc(u_landed[i % UB], 16)
                            if i == 1:
                                sp.wait_ge(w_done, g * GI + GI)
                                sp.dma_start(gbuf[:, b, :], gates_dram[g + G0]).then_inc(g_landed[b], 16)
                                sp.wait_ge(v_lo, g * GI + GI)
                                sp.dma_start(v_raw[:, :, :], vg[g + G0]).then_inc(v_landed, 16)
                for i in range(2):
                    sp.wait_ge(x_final, (i + 1) * (KD // 2))
                    sp.dma_start(out[:, i * (KD // 2):(i + 1) * (KD // 2), :],
                                 xT[:, i * (KD // 2):(i + 1) * (KD // 2), :]).then_inc(out_stored, 16)
                sp.wait_ge(out_stored, 32)

            @block.tensor
            def _(pe):
                def first(i, g):
                    pe.wait_ge(u_lo, g * GI + (i + 1 + UL0))
                    pe.wait_ge(gelus, g * GI + (i + 1))
                    for k in range(KD):
                        for a, b in HI_LO:
                            mm = pe.matmul(ps[:, i % 2, :], u_split[:, i % UB, a, k * P:(k + 1) * P],
                                           h_parts[b][:, k, :], start=(k + a + b == 0),
                                           stop=(k == KD - 1 and a == 1))
                    mm.then_inc(a_sum, 1)

                def slot(i, g_parity):
                    return i if i else (0, GI)[g_parity]

                def second(g, parity):
                    pe.wait_ge(v_lo, g * GI + (GI + VL0))
                    pe.wait_ge(w_done, g * GI + (GI + W0))
                    for j in range(KD):
                        pe.wait_ge(y_added, g * KD + (j + 1))
                        for i in range(GI):
                            for a, b in HI_LO:
                                mm = pe.matmul(ps[:, 2 + j % 4, :], v_split[:, i, a, j * P:(j + 1) * P],
                                               wgt[:, slot(i, parity), b, :], start=(i + a + b == 0),
                                               stop=(i == GI - 1 and a == 1))
                        mm.then_inc(y_sum, 1)

                pe.sem_inc(a_sum, A0)
                pe.sem_inc(y_sum, Y0)
                first(0, 0)
                for i in range(1, GI):
                    first(i, 0)
                with pe.Fori(0, NG2 // 2 - 1) as pair:
                    for b in range(2):
                        g = pair * 2 + b
                        first(0, g + 1)
                        second(g, b)
                        for i in range(1, GI):
                            first(i, g + 1)
                first(0, NG2 - 1)
                second(NG2 - 2, 0)
                for i in range(1, GI):
                    first(i, NG2 - 1)
                second(NG2 - 1, 1)

            @block.scalar
            def _(act):
                def u_upper(i, g):
                    buf = i % UB
                    act.wait_ge(u_landed[buf], g * (16 * GI // UB) + (16 * (i // UB + 1) + U0))
                    act.wait_ge(a_sum, g * GI + (i + 1))
                    act.activation(u_split[:, buf, 0, :], u_raw[:, buf, :], ACT.Copy).then_inc(u_hi, 1)

                def v_upper(i, g):
                    if i == 0:
                        act.wait_ge(v_landed, g * 16 + 16)
                        act.wait_ge(y_sum, g * KD + KD)
                    act.activation(v_split[:, i, 0, :], v_raw[:, i, :], ACT.Copy).then_inc(v_hi, 1)

                def gelu(i, g):
                    act.wait_ge(a_sum, g * GI + (i + 1 + A0))
                    act.wait_ge(w_done, g * GI + (i + 1 + W0 - 2))
                    act.activation(gel[:, i % 2, :], ps[:, i % 2, :], ACT.Gelu_apprx_tanh).then_inc(gelus, 1)

                act.sem_inc(gelus, GE0)
                u_upper(0, 0)
                u_upper(1, 0)
                with act.Fori(0, NG2 - 1) as g:
                    gelu(0, g)
                    u_upper(2, g)
                    v_upper(0, g)
                    v_upper(1, g)
                    gelu(1, g)
                    u_upper(3, g)
                    v_upper(2, g)
                    v_upper(3, g)
                    gelu(2, g)
                    u_upper(0, g + 1)
                    gelu(3, g)
                    u_upper(1, g + 1)
                g = NG2 - 1
                gelu(0, g)
                u_upper(2, g)
                v_upper(0, g)
                v_upper(1, g)
                gelu(1, g)
                u_upper(3, g)
                v_upper(2, g)
                v_upper(3, g)
                gelu(2, g)
                gelu(3, g)

            @block.gpsimd
            def _(pool):
                def u_lower(i, g):
                    buf = i % UB
                    pool.wait_ge(u_hi, g * GI + (i + 1))
                    pool.tensor_tensor(u_split[:, buf, 1, :], u_raw[:, buf, :], u_split[:, buf, 0, :].bitcast(F32),
                                       ALU.subtract).then_inc(u_lo, 1)

                def v_lower(i, g):
                    pool.wait_ge(v_hi, g * GI + (i + 1))
                    pool.tensor_tensor(v_split[:, i, 1, :], v_raw[:, i, :], v_split[:, i, 0, :].bitcast(F32),
                                       ALU.subtract).then_inc(v_lo, 1)

                pool.sem_inc(u_lo, UL0)
                pool.sem_inc(v_lo, VL0)
                u_lower(0, 0)
                u_lower(1, 0)
                with pool.Fori(0, NG2 - 1) as g:
                    u_lower(2, g)
                    v_lower(0, g)
                    v_lower(1, g)
                    u_lower(3, g)
                    v_lower(2, g)
                    v_lower(3, g)
                    u_lower(0, g + 1)
                    u_lower(1, g + 1)
                g = NG2 - 1
                u_lower(2, g)
                v_lower(0, g)
                v_lower(1, g)
                u_lower(3, g)
                v_lower(2, g)
                v_lower(3, g)

            @block.vector
            def _(dve):
                def weights(i, g, parity):
                    if i == 0:
                        dve.wait_ge(g_landed[parity], g * 8 + (16 - 8 * parity))
                    s = i if i else (0, GI)[parity]
                    dve.wait_ge(gelus, g * GI + (i + 1 + GE0))
                    dve.tensor_tensor(gel[:, i % 2, :], gel[:, i % 2, :], gview[:, parity, i, :],
                                      ALU.mult).then_inc(gated, 1)
                    dve.wait_ge(gated, g * (2 * GI) + (2 * i + 1))
                    if i == 1:
                        dve.wait_ge(y_sum, g * KD + KD)
                    dve.tensor_copy(wgt[:, s, 0, :], gel[:, i % 2, :]).then_inc(gated, 1)
                    dve.wait_ge(gated, g * (2 * GI) + (2 * i + 2))
                    dve.tensor_tensor(wgt[:, s, 1, :], gel[:, i % 2, :], wgt[:, s, 0, :].bitcast(F32),
                                      ALU.subtract).then_inc(w_done, 1)

                def adds(g):
                    for j in range(KD):
                        dve.wait_ge(y_sum, g * KD + (j + 1 + Y0))
                        dve.wait_ge(y_added, g * KD + (j + 2))
                        dve.tensor_tensor(acc[:, j, :], ps[:, 2 + j % 4, :], acc[:, j, :],
                                          ALU.add).then_inc(y_added, 1)

                dve.sem_inc(w_done, W0)
                dve.sem_inc(y_added, B0)
                for i in range(GI):
                    weights(i, 0, 0)
                with dve.Fori(0, NG2 // 2 - 1) as pair:
                    for b in range(2):
                        g = pair * 2 + b
                        weights(0, g + 1, 1 - b)
                        adds(g)
                        for i in range(1, GI):
                            weights(i, g + 1, 1 - b)
                weights(0, NG2 - 1, 1)
                adds(NG2 - 2)
                for i in range(1, GI):
                    weights(i, NG2 - 1, 1)
                adds(NG2 - 1)
                for j in range(KD):
                    dve.wait_ge(y_added, B0 + (NG2 - 1) * KD + j + 1)
                    dve.scalar_tensor_tensor(out=xT[:, j, :], in0=acc[:, j, :], scalar=mod[:, 88 + j:89 + j],
                                             in1=xT[:, j, :], op0=ALU.mult, op1=ALU.add).then_inc(x_final, 1)


def pieces_of(w):
    n = w.shape[1] // P
    return w.reshape(KD, P, n, P).transpose(2, 1, 0, 3).reshape(n, P, PIECE)


def row_pieces(w):
    return w.reshape(KD, P, -1, PIECE).transpose(2, 0, 1, 3).reshape(-1, P, PIECE)


def columns(v):
    return v.reshape(-1, P).T


def constants():
    c = np.zeros((P, CONST_W), np.float32)

    def put(name, a):
        lo, hi = CONST_AT[name]
        c[:, lo:hi] = a.reshape(P, hi - lo)

    p = np.arange(P)
    put("ident", np.eye(P))
    put("ones", np.ones((P, P)))
    put("bones", (p[:, None] // DH == p[None, :] // DH).astype(np.float32))
    rot = np.zeros((P, P))
    for m in range(P):
        if m % DH < HALF:
            rot[m + HALF, m] = -1.0
        else:
            rot[m - HALF, m] = 1.0
    put("rot", rot)
    inv = np.float32(10000.0) ** (-np.arange(HALF, dtype=np.float32) / np.float32(HALF))
    inv = inv.astype(np.float32)[p % HALF]
    angle = (np.arange(T, dtype=np.float32)[None, :] * inv[:, None]).astype(np.float64)
    put("cos", np.cos(angle))
    put("sin", np.sin(angle))
    put("invf", inv)
    u = np.arange(T)
    put("causal", np.where(u[None, :] - (T - P) <= p[:, None], 0.0, -BIG))
    d = p[:, None] - p[None, :]
    put("causal16", np.where((d >= 0) & (d % 4 == 0), 0.0, -BIG))
    dist = p[:, None] + P - np.arange(2 * P)[None, :]
    put("band129", np.where((dist >= 0) & (dist <= 128), 0.0, -BIG))
    put("band128", np.where((dist >= 0) & (dist < 128), 0.0, -BIG))
    t = np.arange(TT)[None, :, None] * P + p[:, None, None]
    n = np.arange(CMP_PAD)[None, None, :]
    put("mcmp", np.where((n * SPAN + 2 * SPAN - 1 <= t) & (n < N_CMP), 0.0, -BIG))
    put("valid", (t[:, :, 0] >= 2 * SPAN - 1).astype(np.float32))
    put("iota", np.tile(p, (P, 1)))
    put("iota16", np.tile(np.arange(PTOP), (P, 1)))
    return c


def small_arrays(x):
    s = np.zeros((P, SMALL_W), np.float32)

    def put(name, a):
        lo, hi = SMALL_AT[name]
        s[:, lo:hi] = a.reshape(P, hi - lo)

    put("c", columns(x["c"][0]))
    put("c2", columns(x["c_2"][0]))
    put("ng0", columns(x["norm_g"][0]))
    put("ng1", columns(x["norm_g"][1]))
    put("fg", columns(x["final_g"]))
    put("n1g", columns(x["norm1_g_2"][0]))
    put("n2g", columns(x["norm2_g_2"][0]))
    put("adab", columns(np.concatenate([x["ada_b"][0], x["ada_b"][1], x["ada_b_2"][0]])))
    put("qg", np.tile(x["q_norm_g_2"][0], 2))
    put("kg", np.tile(x["k_norm_g_2"][0], 2))
    put("aog", columns(x["attn_out_g_2"][0]))
    put("cog", columns(x["conv_out_g_2"][0]))
    put("convw", x["conv_w_2"][0].reshape(3, 4, P).transpose(2, 0, 1))
    put("sinks", np.tile(x["sinks_2"][0], (P, 1)))
    put("pek", x["nsa_pe_k"][0].reshape(16, P).T)
    put("pev", x["nsa_pe_v"][0].reshape(16, P).T)
    put("w2k", x["nsa_ck_w2"][0].reshape(2, P, DH).transpose(1, 0, 2))
    put("w2v", x["nsa_cv_w2"][0].reshape(2, P, DH).transpose(1, 0, 2))
    return s


def weight_stream(x):
    w = np.zeros((N_PIECES, P, PIECE), np.float32)

    def put(name, a):
        lo, hi = PIECE_AT[name]
        w[lo:hi] = a

    def pairs(m, heads):
        return m.reshape(D, 2, heads // 2, DH).transpose(0, 2, 1, 3).reshape(D, heads * DH)

    n = x["nsa_w_in"][0]
    kc, vc, ks, vs_, kw, vw_ = (n[:, D + i * P:D + (i + 1) * P] for i in range(6))
    put("ada0", row_pieces(x["ada_w"][0]))
    put("cmp_in", pieces_of(np.concatenate([kc, vc], 1)))
    put("ksw", pieces_of(np.concatenate([ks, kw], 1)))
    put("q", pieces_of(pairs(n[:, :D], NH)))
    put("cmp_w1", np.concatenate([x[k][0].reshape(4, 4, P, CMP_H).transpose(0, 2, 1, 3).reshape(4, P, PIECE)
                                  for k in ("nsa_ck_w1", "nsa_cv_w1")]))
    gates = np.zeros((D, P), np.float32)
    gates[:, :3 * NH] = n[:, 2 * D + 6 * P:]
    put("vsw", pieces_of(np.concatenate([vs_, vw_, gates], 1)))
    put("z", pieces_of(n[:, D + 6 * P:2 * D + 6 * P]))
    put("ada12", row_pieces(np.concatenate([x["ada_w"][1], x["ada_w_2"][0]], 1)))
    put("nsa_out", pieces_of(x["nsa_w_out"][0]))
    d = x["dil_w_in"][0]
    for i, name in enumerate(("dq", "dk", "dv", "dz")):
        put(name, pieces_of(d[:, i * D:(i + 1) * D]))
    put("dil_out", pieces_of(x["dil_w_out"][0]))
    m = x["w_in_2"][0]
    put("q2", pieces_of(pairs(m[:, :512], NQ2)))
    put("k2", pieces_of(m[:, 512:640]))
    put("v2", pieces_of(m[:, 640:768]))
    for i, name in enumerate(("cb", "cc", "cu")):
        put(name, pieces_of(m[:, 768 + 512 * i:1280 + 512 * i]))
    put("out2", pieces_of(x["w_out_2"][0]))
    put("wq", pieces_of(x["peer_wq_2"][0]))
    put("subkeys", x["peer_subkeys_2"][0].reshape(2, 8, P, P).transpose(0, 3, 1, 2).reshape(2, P, PIECE))
    return w


def kernel(**inputs):
    import concourse.bacc as _bacc
    from concourse.bass_utils import run_bass_kernel_spmd as _run

    x = {k: np.asarray(v) for k, v in inputs.items()}
    nc = _bacc.Bacc("TRN2", target_bir_lowering=False, num_devices=1)
    arrays = {
        "w_stream": weight_stream(x),
        "consts": constants(),
        "small": small_arrays(x),
        "x_in": np.ascontiguousarray(x["x"][0].reshape(T, KD, P).transpose(2, 1, 0)),
        "positions": np.ascontiguousarray(x["positions_2"][0]),
        "u_table": np.ascontiguousarray(x["peer_u_2"][0].reshape(PK, PK, KD, P).transpose(0, 3, 2, 1)
                                        .reshape(PK, P, PIECE)),
        "v_table": np.ascontiguousarray(x["peer_v_2"][0]),
    }
    aps = [nc.dram_tensor(name, a.shape, mybir.dt.from_np(a.dtype), kind="ExternalInput").ap()
           for name, a in arrays.items()]
    out = nc.dram_tensor("out_t", (P, KD, T), F32, kind="ExternalOutput").ap()
    gates = nc.dram_tensor("gates_scratch", (NG, P, GI * T), F32).ap()
    gelus = nc.dram_tensor("gelu_scratch", (EARLY, P, T), F32).ap()
    build(nc, *aps, out, gates, gelus)
    r = _run(nc, [arrays], core_ids=[0])
    return np.ascontiguousarray(r.results[0]["out_t"].transpose(2, 1, 0)).reshape(1, T, D)
```
